# Optimizing a Trainium2 kernel written in Bass

```python
import jax, jax.numpy as jnp
from jax import lax
import numpy as np

D_MODEL = 1024
BATCH = 1
SEQ = 1024
DEPTH = 1

GRID_W = 64
CTX_LEN = 256
LN_EPS = 1e-5
DEEPNORM_ALPHA = (2.0 * DEPTH) ** 0.25
DEEPNORM_BETA = (8.0 * DEPTH) ** -0.25

SSD_EXPAND = 2
D_INNER = SSD_EXPAND * D_MODEL
SSD_HEAD_DIM = 64
SSD_HEADS = D_INNER // SSD_HEAD_DIM
SSD_GROUPS = 4
SSD_STATE = 128
SSD_CHUNK = 128
CONV_W = 5
CONV_CH = D_INNER + 2 * SSD_GROUPS * SSD_STATE

ATTN_HEAD_DIM = 64
ATTN_Q_HEADS = 16
ATTN_KV_HEADS = 4
GQA_GROUP = ATTN_Q_HEADS // ATTN_KV_HEADS
ATTN_WIDTH = ATTN_Q_HEADS * ATTN_HEAD_DIM
KV_WIDTH = ATTN_KV_HEADS * ATTN_HEAD_DIM
WINDOW = 128
ATTN_BLOCK = 128
ATTN_SCALE = ATTN_HEAD_DIM ** -0.5
ROPE_BASE = 10000.0
ROPE_AXIS_DIM = ATTN_HEAD_DIM // 2

N_IN = D_INNER + CONV_CH + 2 * SSD_HEADS + ATTN_WIDTH + 2 * KV_WIDTH + 2 * D_MODEL

N_EXPERTS = 16
EXPERT_FF = 1024
CAPACITY_FACTOR = 2

kernel_name = "hybrid_ssd_swa_ecmoe_dit_block"

def layer_norm(x):
    xf = x.astype(jnp.float32)
    mu = jnp.mean(xf, -1, keepdims=True)
    var = jnp.mean(jnp.square(xf - mu), -1, keepdims=True)
    return ((xf - mu) * lax.rsqrt(var + LN_EPS)).astype(x.dtype)

def layer_norm_affine(x, g, b):
    xf = x.astype(jnp.float32)
    mu = jnp.mean(xf, -1, keepdims=True)
    var = jnp.mean(jnp.square(xf - mu), -1, keepdims=True)
    y = (xf - mu) * lax.rsqrt(var + LN_EPS) * g.astype(jnp.float32) + b.astype(jnp.float32)
    return y.astype(x.dtype)

def rms_norm(xf, g):
    return xf * lax.rsqrt(jnp.mean(jnp.square(xf), -1, keepdims=True) + LN_EPS) * g.astype(jnp.float32)

def modulate(h, shift, scale):
    return h * (1.0 + scale) + shift

def axial_rope(rows, dtype):
    row = jnp.repeat(jnp.arange(rows, dtype=jnp.float32), GRID_W)
    col = jnp.tile(jnp.arange(GRID_W, dtype=jnp.float32), rows)
    inv_freq = ROPE_BASE ** (-jnp.arange(0, ROPE_AXIS_DIM, 2, dtype=jnp.float32) / ROPE_AXIS_DIM)
    ang_r = row[:, None] * inv_freq[None, :]
    ang_c = col[:, None] * inv_freq[None, :]
    ang = jnp.concatenate([ang_r, ang_r, ang_c, ang_c], -1)
    return (jnp.cos(ang).astype(dtype)[None, :, None, :],
            jnp.sin(ang).astype(dtype)[None, :, None, :])

def apply_rope(x, cos, sin):
    x1, x2, x3, x4 = jnp.split(x, 4, axis=-1)
    rot = jnp.concatenate([-x2, x1, -x4, x3], -1)
    return x * cos + rot * sin

def split_projection(p):
    sizes = (D_INNER, CONV_CH, 2 * SSD_HEADS, ATTN_WIDTH, KV_WIDTH, KV_WIDTH, 2 * D_MODEL)
    points = []
    acc = 0
    for s in sizes[:-1]:
        acc += s
        points.append(acc)
    return jnp.split(p, points, axis=-1)

def depthwise_conv_centred(x, w, b):
    y = lax.conv_general_dilated(
        x, w[:, None, :], window_strides=(1,),
        padding=[(CONV_W // 2, CONV_W // 2)],
        dimension_numbers=("NWC", "WIO", "NWC"),
        feature_group_count=x.shape[-1])
    return y + b

def ssd_chunked(xdt, da, bm, cm, init_state):
    b, L, H, P = xdt.shape
    G, N = bm.shape[2], bm.shape[3]
    R = H // G
    Q = SSD_CHUNK
    nc = L // Q
    xdt = xdt.astype(jnp.float32).reshape(b, nc, Q, G, R, P)
    da = da.astype(jnp.float32).reshape(b, nc, Q, G, R)
    bm = bm.astype(jnp.float32).reshape(b, nc, Q, G, N)
    cm = cm.astype(jnp.float32).reshape(b, nc, Q, G, N)
    a_cum = jnp.cumsum(da, axis=2)
    seg = a_cum[:, :, :, None] - a_cum[:, :, None, :]
    lower = jnp.tril(jnp.ones((Q, Q), dtype=bool))[:, :, None, None]
    decay = jnp.exp(jnp.where(lower, seg, -jnp.inf))
    lmat = jnp.einsum("bcign,bcjgn->bcijg", cm, bm)[..., None] * decay
    y_diag = jnp.einsum("bcijgr,bcjgrp->bcigrp", lmat, xdt)
    decay_end = jnp.exp(a_cum[:, :, -1:] - a_cum)
    chunk_states = jnp.einsum("bcjgn,bcjgr,bcjgrp->bcgrpn", bm, decay_end, xdt)
    chunk_decay = jnp.exp(a_cum[:, :, -1])

    def step(s, inp):
        dec, st = inp
        return s * dec[..., None, None] + st, s

    init = init_state.astype(jnp.float32).reshape(b, G, R, P, N)
    final, s_prev = lax.scan(step, init, (jnp.moveaxis(chunk_decay, 1, 0),
                                          jnp.moveaxis(chunk_states, 1, 0)))
    s_prev = jnp.moveaxis(s_prev, 0, 1)
    y_off = jnp.einsum("bcign,bcigr,bcgrpn->bcigrp", cm, jnp.exp(a_cum), s_prev)
    y = (y_diag + y_off).reshape(b, L, H, P)
    return y, final.reshape(b, H, P, N)

def ssd_core(xbc, dt_raw, a_log, dt_bias, state_f, state_b):
    b, L, _ = xbc.shape
    xs, bm, cm = jnp.split(xbc, [D_INNER, D_INNER + SSD_GROUPS * SSD_STATE], axis=-1)
    xs = xs.reshape(b, L, SSD_HEADS, SSD_HEAD_DIM)
    bm = bm.reshape(b, L, SSD_GROUPS, SSD_STATE)
    cm = cm.reshape(b, L, SSD_GROUPS, SSD_STATE)
    dt = jax.nn.softplus(dt_raw.reshape(b, L, 2, SSD_HEADS).astype(jnp.float32)
                         + dt_bias.astype(jnp.float32))
    da = dt * (-jnp.exp(a_log.astype(jnp.float32)))
    xdt = xs.astype(jnp.float32)[:, :, None] * dt[..., None]
    y_f, fin_f = ssd_chunked(xdt[:, :, 0], da[:, :, 0], bm, cm, state_f)
    y_b, fin_b = ssd_chunked(jnp.flip(xdt[:, :, 1], 1), jnp.flip(da[:, :, 1], 1),
                             jnp.flip(bm, 1), jnp.flip(cm, 1), state_b)
    return y_f + jnp.flip(y_b, 1), xs, fin_f, fin_b

def ssd_output(y, xs, z, d_skip, norm_w):
    b, L = z.shape[:2]
    y = y + d_skip.astype(jnp.float32)[:, None] * xs.astype(jnp.float32)
    y = y.reshape(b, L, D_INNER) * jax.nn.silu(z.astype(jnp.float32))
    return rms_norm(y, norm_w).astype(z.dtype)

def windowed_attention(q, k, v, k_ctx, v_ctx, sink):
    b, L = q.shape[:2]
    nblk = L // ATTN_BLOCK
    span = ATTN_BLOCK + 2 * WINDOW
    kp = jnp.pad(k, ((0, 0), (WINDOW, WINDOW), (0, 0), (0, 0)))
    vp = jnp.pad(v, ((0, 0), (WINDOW, WINDOW), (0, 0), (0, 0)))
    qg = q.reshape(b, L, ATTN_KV_HEADS, GQA_GROUP, ATTN_HEAD_DIM) * ATTN_SCALE
    q_off = jnp.arange(ATTN_BLOCK)
    k_off = jnp.arange(span)
    rel = (k_off[None, :] - WINDOW) - q_off[:, None]
    s_sink = jnp.broadcast_to(
        sink.astype(jnp.float32).reshape(ATTN_KV_HEADS, GQA_GROUP, 1, 1),
        (b, ATTN_KV_HEADS, GQA_GROUP, ATTN_BLOCK, 1))

    def block(i):
        start = i * ATTN_BLOCK
        qb = lax.dynamic_slice_in_dim(qg, start, ATTN_BLOCK, axis=1)
        kb = lax.dynamic_slice_in_dim(kp, start, span, axis=1)
        vb = lax.dynamic_slice_in_dim(vp, start, span, axis=1)
        key_pos = start - WINDOW + k_off
        valid = (jnp.abs(rel) <= WINDOW) & ((key_pos >= 0) & (key_pos < L))[None, :]
        s_loc = jnp.einsum("bqkrd,bskd->bkrqs", qb, kb).astype(jnp.float32)
        s_loc = jnp.where(valid, s_loc, -jnp.inf)
        s_ctx = jnp.einsum("bqkrd,bskd->bkrqs", qb, k_ctx).astype(jnp.float32)
        p = jax.nn.softmax(jnp.concatenate([s_loc, s_ctx, s_sink], -1), axis=-1).astype(v.dtype)
        o = (jnp.einsum("bkrqs,bskd->bqkrd", p[..., :span], vb)
             + jnp.einsum("bkrqs,bskd->bqkrd", p[..., span:-1], v_ctx))
        return o.reshape(b, ATTN_BLOCK, ATTN_WIDTH)

    out = lax.map(block, jnp.arange(nblk))
    return jnp.moveaxis(out, 0, 1).reshape(b, L, ATTN_WIDTH)

def context_attention(q, k, v, sink):
    b, S = q.shape[:2]
    qg = q.reshape(b, S, ATTN_KV_HEADS, GQA_GROUP, ATTN_HEAD_DIM) * ATTN_SCALE
    s = jnp.einsum("bqkrd,bskd->bkrqs", qg, k).astype(jnp.float32)
    s_sink = jnp.broadcast_to(
        sink.astype(jnp.float32).reshape(ATTN_KV_HEADS, GQA_GROUP, 1, 1),
        (b, ATTN_KV_HEADS, GQA_GROUP, S, 1))
    p = jax.nn.softmax(jnp.concatenate([s, s_sink], -1), axis=-1)[..., :-1].astype(v.dtype)
    o = jnp.einsum("bkrqs,bskd->bqkrd", p, v)
    return o.reshape(b, S, ATTN_WIDTH)

def merge_branches(y_ssd, y_attn, gates, w_ssd_br, w_attn_br, w_o, b_o):
    g_ssd, g_attn = jnp.split(jax.nn.sigmoid(gates), 2, axis=-1)
    m = g_ssd * (y_ssd @ w_ssd_br) + g_attn * (y_attn @ w_attn_br)
    return m @ w_o + b_o

def token_mixer(h, hc, cos, sin, w_in, conv_w, conv_b, a_log, dt_bias, d_skip, ssd_norm_w,
                attn_sink, w_ssd_br, w_attn_br, w_o, b_o, with_ctx_out):
    b, L, _ = h.shape
    S = hc.shape[1]
    zc, xbcc, dtc, qc, kc, vc, gc = split_projection(hc @ w_in)
    xbcc = jax.nn.silu(depthwise_conv_centred(xbcc, conv_w, conv_b))
    zero = jnp.zeros((b, SSD_HEADS, SSD_HEAD_DIM, SSD_STATE), jnp.float32)
    yc_core, xsc, fin_f, fin_b = ssd_core(xbcc, dtc, a_log, dt_bias, zero, zero)
    kc = kc.reshape(b, S, ATTN_KV_HEADS, ATTN_HEAD_DIM)
    vc = vc.reshape(b, S, ATTN_KV_HEADS, ATTN_HEAD_DIM)
    z, xbc, dtr, q, k, v, g = split_projection(h @ w_in)
    xbc = jax.nn.silu(depthwise_conv_centred(xbc, conv_w, conv_b))
    y_core, xs, _, _ = ssd_core(xbc, dtr, a_log, dt_bias, fin_f, fin_b)
    y_ssd = ssd_output(y_core, xs, z, d_skip, ssd_norm_w)
    q = apply_rope(q.reshape(b, L, ATTN_Q_HEADS, ATTN_HEAD_DIM), cos, sin)
    k = apply_rope(k.reshape(b, L, ATTN_KV_HEADS, ATTN_HEAD_DIM), cos, sin)
    v = v.reshape(b, L, ATTN_KV_HEADS, ATTN_HEAD_DIM)
    y_attn = windowed_attention(q, k, v, kc, vc, attn_sink)
    y = merge_branches(y_ssd, y_attn, g, w_ssd_br, w_attn_br, w_o, b_o)
    yc = None
    if with_ctx_out:
        yc_ssd = ssd_output(yc_core, xsc, zc, d_skip, ssd_norm_w)
        yc_attn = context_attention(qc.reshape(b, S, ATTN_Q_HEADS, ATTN_HEAD_DIM), kc, vc, attn_sink)
        yc = merge_branches(yc_ssd, yc_attn, gc, w_ssd_br, w_attn_br, w_o, b_o)
    return y, yc

def expert_choice_ffn(h, w_router, w_gate_up, w_down):
    b, L, D = h.shape
    cap = CAPACITY_FACTOR * L // N_EXPERTS
    aff = jax.nn.softmax((h @ w_router).astype(jnp.float32), axis=-1)
    gate_vals, idx = lax.top_k(jnp.swapaxes(aff, 1, 2), cap)
    xs = jax.vmap(lambda hb, ib: hb[ib])(h, idx)
    gu = jnp.einsum("becd,edf->becf", xs, w_gate_up)
    g, u = jnp.split(gu, 2, axis=-1)
    ye = jnp.einsum("becf,efd->becd", jax.nn.silu(g) * u, w_down)
    ye = ye * gate_vals[..., None].astype(h.dtype)
    return jax.vmap(lambda ib, yb: jnp.zeros((L, D), h.dtype).at[ib.reshape(-1)].add(yb.reshape(-1, D)))(idx, ye)

def setup_inputs(seed: int = 0) -> dict:
    key = jax.random.key(seed)
    ks = jax.random.split(key, 26)
    f32 = jnp.float32

    def nrm(k, shape, scale):
        return jax.random.normal(k, shape, f32) * scale

    dt0 = jnp.exp(jax.random.uniform(ks[9], (DEPTH, 2, SSD_HEADS), f32,
                                     minval=np.log(1e-3), maxval=np.log(1e-1)))
    return {
        "x": nrm(ks[0], (BATCH, SEQ, D_MODEL), 1.0),
        "c": nrm(ks[1], (BATCH, D_MODEL), 1.0),
        "ctx": nrm(ks[2], (BATCH, CTX_LEN, D_MODEL), 1.0),
        "c_ctx": nrm(ks[3], (D_MODEL,), 1.0),
        "w_ada": nrm(ks[4], (DEPTH, D_MODEL, 6 * D_MODEL), 0.5 * D_MODEL ** -0.5),
        "b_ada": nrm(ks[5], (DEPTH, 6 * D_MODEL), 0.02),
        "w_in": nrm(ks[6], (DEPTH, D_MODEL, N_IN), D_MODEL ** -0.5),
        "conv_w": nrm(ks[7], (DEPTH, CONV_W, CONV_CH), CONV_W ** -0.5),
        "conv_b": nrm(ks[8], (DEPTH, CONV_CH), 0.02),
        "a_log": jnp.log(jax.random.uniform(ks[10], (DEPTH, 2, SSD_HEADS), f32, minval=1.0, maxval=16.0)),
        "dt_bias": dt0 + jnp.log(-jnp.expm1(-dt0)),
        "d_skip": 1.0 + nrm(ks[11], (DEPTH, SSD_HEADS), 0.1),
        "ssd_norm_w": 1.0 + nrm(ks[12], (DEPTH, D_INNER), 0.02),
        "attn_sink": nrm(ks[13], (DEPTH, ATTN_Q_HEADS), 0.5),
        "w_ssd_br": nrm(ks[14], (DEPTH, D_INNER, D_MODEL), DEEPNORM_BETA * D_INNER ** -0.5),
        "w_attn_br": nrm(ks[15], (DEPTH, ATTN_WIDTH, D_MODEL), DEEPNORM_BETA * ATTN_WIDTH ** -0.5),
        "w_o": nrm(ks[16], (DEPTH, D_MODEL, D_MODEL), DEEPNORM_BETA * D_MODEL ** -0.5),
        "b_o": nrm(ks[17], (DEPTH, D_MODEL), 0.02),
        "ln1_g": 1.0 + nrm(ks[18], (DEPTH, D_MODEL), 0.02),
        "ln1_b": nrm(ks[19], (DEPTH, D_MODEL), 0.02),
        "w_router": nrm(ks[20], (DEPTH, D_MODEL, N_EXPERTS), D_MODEL ** -0.5),
        "w_gate_up": nrm(ks[21], (DEPTH, N_EXPERTS, D_MODEL, 2 * EXPERT_FF), D_MODEL ** -0.5),
        "w_down": nrm(ks[22], (DEPTH, N_EXPERTS, EXPERT_FF, D_MODEL), DEEPNORM_BETA * EXPERT_FF ** -0.5),
        "ln2_g": 1.0 + nrm(ks[23], (DEPTH, D_MODEL), 0.02),
        "ln2_b": nrm(ks[24], (DEPTH, D_MODEL), 0.02),
    }

def reference(x, c, ctx, c_ctx, w_ada, b_ada, w_in, conv_w, conv_b, a_log, dt_bias, d_skip,
              ssd_norm_w, attn_sink, w_ssd_br, w_attn_br, w_o, b_o, ln1_g, ln1_b,
              w_router, w_gate_up, w_down, ln2_g, ln2_b):
    L = x.shape[1]
    rows = L // GRID_W
    cos, sin = axial_rope(rows, x.dtype)
    xc = ctx
    for l in range(DEPTH):
        last = l == DEPTH - 1
        mod = jax.nn.silu(c) @ w_ada[l] + b_ada[l]
        mod_c = jax.nn.silu(c_ctx) @ w_ada[l] + b_ada[l]
        sh1, sc1, g1, sh2, sc2, g2 = [m[:, None, :] for m in jnp.split(mod, 6, axis=-1)]
        csh1, csc1, cg1, csh2, csc2, cg2 = [m[None, None, :] for m in jnp.split(mod_c, 6, axis=-1)]
        h = modulate(layer_norm(x), sh1, sc1)
        hc = modulate(layer_norm(xc), csh1, csc1)
        y, yc = token_mixer(h, hc, cos, sin, w_in[l], conv_w[l], conv_b[l], a_log[l], dt_bias[l],
                            d_skip[l], ssd_norm_w[l], attn_sink[l], w_ssd_br[l], w_attn_br[l],
                            w_o[l], b_o[l], not last)
        x = layer_norm_affine(DEEPNORM_ALPHA * x + g1 * y, ln1_g[l], ln1_b[l])
        h = modulate(layer_norm(x), sh2, sc2)
        x = layer_norm_affine(DEEPNORM_ALPHA * x + g2 * expert_choice_ffn(h, w_router[l], w_gate_up[l], w_down[l]),
                              ln2_g[l], ln2_b[l])
        if not last:
            xc = layer_norm_affine(DEEPNORM_ALPHA * xc + cg1 * yc, ln1_g[l], ln1_b[l])
            hc = modulate(layer_norm(xc), csh2, csc2)
            xc = layer_norm_affine(DEEPNORM_ALPHA * xc + cg2 * expert_choice_ffn(hc, w_router[l], w_gate_up[l], w_down[l]),
                                   ln2_g[l], ln2_b[l])
    return x


_drawn_inputs = setup_inputs


def setup_inputs(seed=0):
    import zlib

    import numpy as np

    out = dict(_drawn_inputs(seed))
    spreads = {}
    factors = {'ctx': 8.0,
     'c_ctx': 7.171,
     'b_ada': 8.0,
     'conv_b': 8.0,
     'a_log': 2.875,
     'dt_bias': 3.77,
     'd_skip': 8.0,
     'ssd_norm_w': 64.0,
     'attn_sink': 28.624,
     'w_attn_br': 4.516,
     'b_o': 8.0,
     'ln1_g': 8.37,
     'ln1_b': 8.164,
     'ln2_g': 8.357,
     'ln2_b': 8.274,
     'w_router': 4.088,
     'w_gate_up': 3.796,
     'w_down': 3.792}
    for name, (base, spread) in spreads.items():
        noise = np.random.default_rng([zlib.crc32(name.encode()), seed]).standard_normal(out[name].shape)
        drawn = base * np.exp(spread * noise) if base else spread * noise
        out[name] = __import__('jax').numpy.asarray(drawn.astype(out[name].dtype))
    for name, factor in factors.items():
        out[name] = (out[name] * factor).astype(out[name].dtype)
    return out
```

```python
from contextlib import ExitStack

import numpy as np
import concourse.bass as bass
from concourse import mybir

ALU = mybir.AluOpType
ACT = mybir.ActivationFunctionType
AX_X = mybir.AxisListType.X
F32 = mybir.dt.float32
F32R = mybir.dt.float32r
U32 = mybir.dt.uint32
ds = bass.ds

P = 128
D = 1024
KT = D // P
SEQ = 1024
CTX = 256
TOK = CTX + SEQ
NCHUNK = TOK // P
CCHUNK = CTX // P
LCHUNK = SEQ // P
D_INNER = 2048
GROUPS = 4
STATE = 128
CONV_W = 5
CONV_CH = D_INNER + 2 * GROUPS * STATE
HEADS = 32
HPG = HEADS // GROUPS
PDIM = 64
QH = 16
KVH = 4
HD = 64
GRID_W = 64
WINDOW = 128
FF = 1024
EXPERTS = 16
CAP = 2 * SEQ // EXPERTS
EPS = 1e-5
ALPHA = 2.0 ** 0.25
SCALE = HD ** -0.5
NEG = -1e30

Z0 = 0
XBC0 = Z0 + D_INNER
DT0 = XBC0 + CONV_CH
Q0 = DT0 + 2 * HEADS
K0 = Q0 + QH * HD
V0 = K0 + KVH * HD
G0 = V0 + KVH * HD

BLANK = WINDOW
KV_LAT0 = CTX + BLANK
KV_TOK = KV_LAT0 + SEQ + BLANK


def shape_constants():
    i = np.arange(P)
    upper = (i[:, None] <= i[None, :]).astype(np.float32)
    inv = 10000.0 ** (-np.arange(0, HD // 2, 2, dtype=np.float32) / (HD // 2))
    t = np.arange(SEQ)
    row = (t // GRID_W).astype(np.float32)[:, None] * inv[None, :]
    col = (t % GRID_W).astype(np.float32)[:, None] * inv[None, :]
    ang = np.concatenate([row, row, col, col], -1).astype(np.float32).T
    ang = np.concatenate([ang, ang], 0)
    rotate = np.zeros((P, P), np.float32)
    for m in range(P):
        quarter = (m % HD) // (HD // 4)
        rotate[m + 16 if quarter % 2 == 0 else m - 16, m] = -1.0 if quarter % 2 == 0 else 1.0
    q, k = i[:, None], np.arange(3 * P)[None, :]
    near = np.abs(k - P - q) <= WINDOW
    masks = np.zeros((LCHUNK, P, CTX + 3 * P), np.float32)
    for b in range(LCHUNK):
        pos = b * P - WINDOW + k
        masks[b, :, CTX:] = np.where(near & (pos >= 0) & (pos < SEQ), 0.0, NEG)
    edges = np.stack([masks[:, :, CTX:CTX + P].transpose(0, 2, 1), masks[:, :, CTX + 2 * P:].transpose(0, 2, 1)], 2)
    return {
        "lanes": np.ascontiguousarray(np.tile(-np.eye(4, dtype=np.float32)[:, :, None], (2, 4, P))).reshape(8, 16 * P),
        "edges": np.ascontiguousarray(edges).reshape(LCHUNK, P, 2 * P),
        "squares": np.concatenate([np.eye(P, dtype=np.float32), upper, upper.T, np.ones((P, P), np.float32), rotate], 1),
        "cosine": np.cos(ang).astype(np.float32),
        "sine": np.sin(ang).astype(np.float32),
        "masks": masks,
    }


class Stage:

    def __init__(self, nc, inputs, out, ctx):
        self.nc, self.x, self.out, self.ctx = nc, inputs, out, ctx
        self.sems = []

    def sem(self, name):
        self.sems.append(self.nc.alloc_semaphore(name=name))
        return self.sems[-1]

    def recycle(self):
        self.nc.clear_and_free_semaphores(self.sems)
        self.nc.all_engine_barrier()
        self.sems = []

    def scratch(self, name, shape):
        return self.nc.dram_tensor(name, shape, F32).ap()


def own(stack, nc, name, shape, dtype=F32):
    return stack.enter_context(nc.sbuf_tensor(name, shape, dtype))


def bank(stack, nc, name, shape, dtype=F32):
    return stack.enter_context(nc.psum_tensor(name, shape, dtype))


def adaln_stage(s, mod):
    nc = s.nc
    NB = 6 * D // 512
    with ExitStack() as st:
        cond = own(st, nc, "cond", [P, 2, KT])
        act_c = own(st, nc, "act_c", [P, 2, KT])
        w = own(st, nc, "w_ada_t", [P, 2, KT, 512])
        bias = own(st, nc, "b_ada_t", [2, 6 * D])
        row = own(st, nc, "mod_row", [2, 2, 512])
        acc = bank(st, nc, "mod_acc", [P, 2, 512])
        cond_in, bias_in, silu_done = s.sem("cond_in"), s.sem("bias_in"), s.sem("cond_silu")
        w_in = [s.sem(f"ada_w_in{b}") for b in range(2)]
        w_free, acc_free = s.sem("ada_w_free"), s.sem("mod_acc_free")
        stored = [s.sem(f"mod_stored{b}") for b in range(2)]
        wv = s.x["w_ada"][0].rearrange("(p k) n -> p k n", k=KT)
        with nc.Block() as block:

            @block.sync
            def _(sp):
                sp.dma_start(cond[:, 0, :], s.x["c"][0].rearrange("(p k) -> p k", k=KT)).then_inc(cond_in, 16)
                sp.dma_start(cond[:, 1, :], s.x["c_ctx"].rearrange("(p k) -> p k", k=KT)).then_inc(cond_in, 16)
                for r in range(2):
                    sp.dma_start(bias[r:r + 1, :], s.x["b_ada"]).then_inc(bias_in, 16)
                with sp.Fori(0, NB // 2) as i:
                    for b in range(2):
                        sp.wait_ge(w_free, 2 * i + b + 1)
                        sp.dma_start(w[:, b], wv[:, :, ds(1024 * i + 512 * b, 512)]).then_inc(w_in[b], 16)

            @block.scalar
            def _(act):
                act.wait_ge(cond_in, 32)
                nc.scalar.activation(act_c[:], cond[:], ACT.Silu).then_inc(silu_done, 1)

            @block.tensor
            def _(pe):
                pe.sem_inc(w_free, 2)
                pe.wait_ge(silu_done, 1)
                with pe.Fori(0, NB // 2) as i:
                    for b in range(2):
                        pe.wait_ge(w_in[b], 16 * i + 16)
                        pe.wait_ge(acc_free, 2 * i + b + 1)
                        for k in range(KT):
                            mm = nc.tensor.matmul(acc[0:2, b, :], act_c[:, :, k], w[:, b, k, :],
                                                  start=(k == 0), stop=(k == KT - 1))
                        mm.then_inc(w_free, 1)

            @block.vector
            def _(dve):
                dve.sem_inc(acc_free, 2)
                dve.wait_ge(bias_in, 32)
                with dve.Fori(0, NB // 2) as i:
                    for b in range(2):
                        dve.wait_ge(w_free, 2 * i + b + 3)
                        dve.wait_ge(stored[b], 16 * i)
                        nc.vector.tensor_tensor(row[:, b, :], acc[0:2, b, :],
                                                bias[:, ds(1024 * i + 512 * b, 512)], ALU.add).then_inc(acc_free, 1)

            @block.gpsimd
            def _(pool):
                with pool.Fori(0, NB // 2) as i:
                    for b in range(2):
                        pool.wait_ge(acc_free, 2 * i + b + 3)
                        pool.dma_start(mod[:, ds(1024 * i + 512 * b, 512)], row[:, b, :]).then_inc(stored[b], 16)
                for b in range(2):
                    pool.wait_ge(stored[b], 16 * (NB // 2))


def norm_stage(s, mod, hi, lo):
    nc = s.nc
    with ExitStack() as st:
        ident = own(st, nc, "ident1", [P, P])
        colm = own(st, nc, "mod_cols", [P, 4, KT])
        x = own(st, nc, "x_in", [P, 2, D])
        xn = own(st, nc, "x_norm", [P, 2, D])
        stats = own(st, nc, "ln_stats", [P, 2, 6])
        mv = own(st, nc, "ln_mv", [P, 2])
        rstd = own(st, nc, "ln_rstd", [P, 2])
        carrier = s.sem("ln_carrier")
        h = own(st, nc, "h_full", [P, 2, KT, P])
        tp = bank(st, nc, "ln_tp", [P, 2, KT, P])
        ident_in, cols_in = s.sem("ident1_in"), s.sem("mod_cols_in")
        x_in = [s.sem(f"x_in{b}") for b in range(2)]
        x_free, xn_ready, turned = s.sem("x_free"), s.sem("xn_ready"), s.sem("x_turned")
        var_ready, root_ready, chain = s.sem("ln_var"), s.sem("ln_root"), s.sem("ln_chain")
        h_ready, hi_ready, lo_ready = s.sem("h_ready"), s.sem("h_hi_ready"), s.sem("h_lo_ready")
        STEPS = 8

        with nc.Block() as block:

            @block.sync
            def _(sp):
                sp.dma_start(ident[:], s.squares[:, 0:P]).then_inc(ident_in, 16)
                for j, (r, part) in enumerate([(1, 0), (1, 1), (0, 0), (0, 1)]):
                    for k in range(KT):
                        sp.dma_start(colm[:, j, k:k + 1],
                                     mod[r:r + 1, part * D + k * P:part * D + k * P + P].rearrange("o p -> p o")
                                     ).then_inc(cols_in, 16)

                def load(src, t, b, n):
                    sp.wait_ge(x_free, n + 1)
                    sp.dma_start(x[:, b], src).then_inc(x_in[b], 16)

                for t in range(CCHUNK):
                    load(s.x["ctx"][0, t * P:t * P + P, :], t, t % 2, t)
                with sp.Fori(0, LCHUNK // 2) as i:
                    for b in range(2):
                        load(s.x["x"][0, ds((2 * i + b) * P, P), :], None, b, 2 * i + b + CCHUNK)

            @block.vector
            def _(dve):
                dve.sem_inc(x_free, 2)
                dve.wait_ge(cols_in, 16 * 4 * KT)
                dve.tensor_scalar(colm[:, 1, :], colm[:, 1, :], 1.0, None, ALU.add).then_inc(chain, 1)
                dve.tensor_scalar(colm[:, 3, :], colm[:, 3, :], 1.0, None, ALU.add).then_inc(chain, 1)

                def tile(n, b, turn, m):
                    at = 2 + STEPS * n

                    def then(ins, k):
                        ins.then_inc(chain, 1)
                        dve.wait_ge(chain, at + k)

                    dve.wait_ge(x_in[b], 16 * turn + 16)
                    nc.vector.bn_stats(stats[:, 0, :], x[:, b, 0:512]).then_inc(chain, 1)
                    then(nc.vector.bn_stats(stats[:, 1, :], x[:, b, 512:1024]), 2)
                    dve.sem_inc(carrier, 1)
                    then(nc.vector.bn_aggr(mv[:], stats[:]), 3)
                    then(nc.vector.tensor_scalar(rstd[:, 0:1], mv[:, 1:2], EPS, None, ALU.add), 4)
                    then(nc.vector.reciprocal(rstd[:, 1:2], rstd[:, 0:1]), 5)
                    nc.vector.tensor_scalar(rstd[:, 0:1], rstd[:, 1:2], 1.0, None, ALU.mult).then_inc(var_ready, 1)
                    dve.wait_ge(root_ready, n + 1)
                    dve.wait_ge(turned, n) if not isinstance(n, int) or n > 0 else None
                    nc.vector.tensor_scalar(xn[:, b], x[:, b], mv[:, 0:1], rstd[:, 1:2],
                                            ALU.subtract, ALU.mult).then_inc(x_free, 1)
                    dve.wait_ge(turned, n + 1)
                    then(nc.vector.tensor_tensor(h[:, b], tp[:, b], colm[:, m + 1, :].unsqueeze(2).to_broadcast([P, KT, P]),
                                                 ALU.mult), 6)
                    then(nc.vector.tensor_tensor(h[:, b], h[:, b], colm[:, m, :].unsqueeze(2).to_broadcast([P, KT, P]),
                                                 ALU.add), 7)
                    dve.wait_ge(hi_ready, n + 1)
                    cut = slice(n * P, n * P + P) if isinstance(n, int) else ds(n * P, P)
                    then(nc.vector.tensor_tensor(lo[:, :, cut], h[:, b], hi[:, :, cut].bitcast(F32), ALU.subtract), 8)

                for t in range(CCHUNK):
                    tile(t, t % 2, t // 2, 0)
                with dve.Fori(0, LCHUNK // 2) as i:
                    for b in range(2):
                        tile(2 * i + b + CCHUNK, b, i + 1, 2)

            @block.scalar
            def _(act):
                def tile(n, b):
                    act.wait_ge(var_ready, n + 1)
                    nc.scalar.activation(rstd[:, 1:2], rstd[:, 0:1], ACT.Sqrt).then_inc(root_ready, 1)
                    act.wait_ge(chain, 2 + STEPS * n + 7)
                    cut = slice(n * P, n * P + P) if isinstance(n, int) else ds(n * P, P)
                    nc.scalar.copy(hi[:, :, cut], h[:, b]).then_inc(hi_ready, 1)

                for t in range(CCHUNK):
                    tile(t, t % 2)
                with act.Fori(0, LCHUNK // 2) as i:
                    for b in range(2):
                        tile(2 * i + b + CCHUNK, b)

            @block.tensor
            def _(pe):
                pe.wait_ge(ident_in, 16)

                def tile(n, b):
                    pe.wait_ge(x_free, n + 3)
                    for k in range(KT):
                        mm = nc.tensor.transpose(tp[:, b, k, :], xn[:, b, k * P:k * P + P], ident[:])
                    mm.then_inc(turned, 1)

                for t in range(CCHUNK):
                    tile(t, t % 2)
                with pe.Fori(0, LCHUNK // 2) as i:
                    for b in range(2):
                        tile(2 * i + b + CCHUNK, b)


def project_f_stage(s, hi, lo, xbcF, xbcT, qkF, gF):
    nc = s.nc
    NX, NQK, NG = CONV_CH // P, (QH + KVH) * HD // P, 2 * D // P
    SEGS = [(0, CTX), (CTX, 512), (CTX + 512, 512)]
    PAD = 2 + CTX + 4 + SEQ + 2
    W_OUT = PAD - 4
    with ExitStack() as st:
        squares = own(st, nc, "squares", [P, 5, P])
        cos, sin = own(st, nc, "cos", [P, SEQ]), own(st, nc, "sin", [P, SEQ])
        taps = own(st, nc, "conv_taps", [P, NX, CONV_W + 1])
        w = own(st, nc, "w_raw", [P, 2, KT, P])
        whi = own(st, nc, "w_hi", [P, 2, KT, P], F32R)
        wlo = own(st, nc, "w_lo", [P, 2, KT, P], F32R)
        padded = own(st, nc, "conv_in", [P, 2, PAD])
        conv = own(st, nc, "conv_acc", [P, 2, W_OUT])
        wide = own(st, nc, "f_out", [P, 2, TOK])
        zeros = own(st, nc, "f_zeros", [P, BLANK])
        turned = own(st, nc, "t_out", [P, 2, TOK])
        tap = own(st, nc, "conv_tap_cols", [P, 2, CONV_W + 1])
        lat = bank(st, nc, "f_lat", [P, 2, SEQ])
        cxt = bank(st, nc, "f_ctx", [P, 2, 2 * CTX])
        tp = bank(st, nc, "f_tp", [P, SEQ])
        ident, rotate = squares[:, 0, :], squares[:, 4, :]

        tables_in = s.sem("f_tables_in")
        w_in = [s.sem(f"f_w_in{b}") for b in range(2)]
        hi_made, w_free = s.sem("f_hi_made"), s.sem("f_w_free")
        used, acc_free = s.sem("f_w_used"), s.sem("f_acc_free")
        conv_step, wide_made = s.sem("f_conv_step"), s.sem("f_wide_made")
        tp_full, tp_free = s.sem("f_tp_full"), s.sem("f_tp_free")
        ctx_turned = s.sem("f_ctx_turned")
        rot_step = s.sem("f_rot_step")
        wide_out = [s.sem(f"f_wide_out{b}") for b in range(2)]
        turned_out = [s.sem(f"f_turned_out{b}") for b in range(2)]
        zeros_made, blanks_out = s.sem("f_zeros_made"), s.sem("f_blanks_out")
        CS = CONV_W + 1
        wv = s.x["w_in"][0].rearrange("(k p) n -> p k n", p=P)
        NF = NX + NQK + NG

        def pairs(eng, kind, step):
            f0, n = {"xbc": (0, NX), "qk": (NX, NQK), "gate": (NX + NQK, NG - 2)}[kind]
            with eng.Fori(0, n // 2) as i:
                for b in range(2):
                    step(2 * i + (f0 + b), b, kind, i + f0 // 2, 2 * i + b)

        with nc.Block() as block:

            @block.sync
            def _(sp):
                sp.dma_start(squares[:], s.squares.rearrange("p (a q) -> p a q", q=P)).then_inc(tables_in, 16)
                sp.dma_start(cos[:], s.cosine).then_inc(tables_in, 16)
                sp.dma_start(sin[:], s.sine).then_inc(tables_in, 16)
                sp.dma_start(taps[:], s.x["taps"]).then_inc(tables_in, 16)
                for col, f0, n in ((XBC0, 0, NX), (Q0, NX, NQK), (G0, NX + NQK, NG)):
                    with sp.Fori(0, n // 2) as i:
                        for b in range(2):
                            sp.wait_ge(w_free, 2 * i + (f0 + b + 1))
                            sp.dma_start(w[:, b], wv[:, :, ds(2 * P * i + (col + P * b), P)]).then_inc(w_in[b], 16)

            @block.tensor
            def _(pe):
                pe.sem_inc(used, 2)
                pe.wait_ge(tables_in, 64)

                def product(f, b, ctx, after_turn=False):
                    pe.wait_ge(w_free, f + 3)
                    pe.wait_ge(acc_free, f + 1)
                    if after_turn:
                        pe.wait_ge(ctx_turned, f + 1)
                    outs = [(cxt[:, b, 0:CTX], 0, CTX)] if ctx else []
                    outs += [(lat[:, b, 0:512], CTX, 512), (lat[:, b, 512:1024], CTX + 512, 512)]
                    for k in range(KT):
                        for n_pass, (weights, part) in enumerate(((whi, hi), (whi, lo), (wlo, hi))):
                            for o, a, n in outs:
                                mm = nc.tensor.matmul(o, weights[:, b, k, :], part[:, k, a:a + n],
                                                      start=(k == 0 and n_pass == 0),
                                                      stop=(k == KT - 1 and n_pass == 2))
                    mm.then_inc(used, 1)

                def turn(f, b):
                    pe.wait_ge(wide_made, f + 3)
                    pe.wait_ge(tp_free, f + 1)
                    for c in range(NCHUNK):
                        at = cxt[:, b, CTX + c * P:CTX + c * P + P] if c < CCHUNK else tp[:, (c - CCHUNK) * P:(c - CCHUNK) * P + P]
                        mm = nc.tensor.transpose(at, wide[:, b, c * P:c * P + P], ident)
                    mm.then_inc(tp_full, 1)

                def rotated(f, b):
                    pe.wait_ge(acc_free, f + 3)
                    pe.wait_ge(tp_free, f + 1)
                    for n in range(2):
                        mm = nc.tensor.matmul(tp[:, n * 512:n * 512 + 512], rotate,
                                              wide[:, b, CTX + n * 512:CTX + n * 512 + 512], start=True, stop=True)
                    mm.then_inc(tp_full, 1)

                product(0, 0, True, True)
                product(1, 1, True, True)
                turn(0, 0)
                with pe.Fori(1, NX // 2) as i:
                    product(2 * i, 0, True, True)
                    turn(2 * i - 1, 1)
                    product(2 * i + 1, 1, True, True)
                    turn(2 * i, 0)
                product(NX, 0, True, True)
                turn(NX - 1, 1)
                product(NX + 1, 1, True, True)
                rotated(NX, 0)
                with pe.Fori(1, NQK // 2) as i:
                    product(2 * i + NX, 0, True)
                    rotated(2 * i + (NX - 1), 1)
                    product(2 * i + (NX + 1), 1, True)
                    rotated(2 * i + NX, 0)
                product(NX + NQK, 0, False)
                rotated(NX + NQK - 1, 1)
                product(NX + NQK + 1, 1, False)
                with pe.Fori(1, NG // 2) as i:
                    for b in range(2):
                        product(2 * i + (NX + NQK + b), b, False)

            @block.scalar
            def _(act):
                act.sem_inc(acc_free, 2)
                act.sem_inc(wide_made, 2)
                act.sem_inc(tp_free, 1)
                act.sem_inc(ctx_turned, 2)

                def split_hi(f, b, turn):
                    act.wait_ge(w_in[b], 16 * turn + 16)
                    act.wait_ge(used, f + 1)
                    nc.scalar.copy(whi[:, b], w[:, b]).then_inc(hi_made, 1)

                def turned_copy(f, b, turn):
                    act.wait_ge(tp_full, f + 1)
                    act.wait_ge(turned_out[b], 16 * turn)
                    nc.scalar.copy(turned[:, b, 0:CTX], cxt[:, b, CTX:2 * CTX]).then_inc(ctx_turned, 1)
                    nc.scalar.copy(turned[:, b, CTX:TOK], tp[:]).then_inc(tp_free, 1)

                def evacuate(f, b, kind, turn, within):
                    act.wait_ge(used, f + 3)
                    if kind == "xbc":
                        act.wait_ge(conv_step, CS * f + CS)
                        nc.scalar.copy(padded[:, b, 2:2 + CTX], cxt[:, b, 0:CTX])
                        nc.scalar.copy(padded[:, b, 6 + CTX:6 + CTX + SEQ], lat[:, b, :]).then_inc(acc_free, 1)
                        if not (isinstance(f, int) and f == 0):
                            turned_copy(f - 1, 1 - b, turn - (1 - b))
                            act.wait_ge(wide_out[b], 16 * turn)
                        act.wait_ge(conv_step, CS * f + 3 * CS)
                        nc.scalar.activation(wide[:, b, 0:CTX], conv[:, b, 0:CTX], ACT.Silu, bias=tap[:, b, CONV_W:CS])
                        nc.scalar.activation(wide[:, b, CTX:TOK], conv[:, b, 4 + CTX:W_OUT], ACT.Silu,
                                             bias=tap[:, b, CONV_W:CS]).then_inc(wide_made, 1)
                    elif kind == "qk":
                        act.wait_ge(wide_out[b], 32 * turn - 16 * (NX // 2))
                        nc.scalar.copy(wide[:, b, 0:CTX], cxt[:, b, 0:CTX])
                        nc.scalar.copy(wide[:, b, CTX:TOK], lat[:, b, :]).then_inc(acc_free, 1)
                    else:
                        act.wait_ge(wide_out[b], 16 * turn + 16 * (NQK // 2))
                        nc.scalar.activation(wide[:, b, CTX:TOK], lat[:, b, :], ACT.Sigmoid).then_inc(acc_free, 1)

                def step(f, b, kind, turn, within):
                    split_hi(f + 1, 1 - b, turn + b)
                    evacuate(f, b, kind, turn, within)

                split_hi(0, 0, 0)
                step(0, 0, "xbc", 0, 0)
                step(1, 1, "xbc", 0, 1)
                with act.Fori(1, NX // 2) as i:
                    step(2 * i, 0, "xbc", i, 2 * i)
                    step(2 * i + 1, 1, "xbc", i, 2 * i + 1)
                split_hi(NX + 1, 1, NX // 2)
                turned_copy(NX - 1, 1, NX // 2 - 1)
                evacuate(NX, 0, "qk", NX // 2, 0)
                step(NX + 1, 1, "qk", NX // 2, 1)
                with act.Fori(1, NQK // 2) as i:
                    for b in range(2):
                        step(2 * i + (NX + b), b, "qk", i + NX // 2, 2 * i + b)
                pairs(act, "gate", step)
                step(NF - 2, 0, "gate", NF // 2 - 1, NG - 2)
                evacuate(NF - 1, 1, "gate", NF // 2 - 1, NG - 1)

            @block.vector
            def _(dve):
                dve.sem_inc(w_free, 2)
                dve.wait_ge(tables_in, 64)
                dve.memset(padded[:], 0.0).then_inc(conv_step, 2 * CS)

                def split_lo(f, b):
                    dve.wait_ge(hi_made, f + 1)
                    nc.vector.tensor_tensor(wlo[:, b], w[:, b], whi[:, b].bitcast(F32), ALU.subtract).then_inc(w_free, 1)

                def convolve(f, b, kind, turn, within):
                    split_lo(f + 1, 1 - b)
                    dve.wait_ge(wide_made, f + 1)
                    cut = slice(f, f + 1) if isinstance(f, int) else ds(f, 1)
                    nc.vector.tensor_copy(tap[:, b, :], taps[:, cut, :].rearrange("p o c -> p (o c)")).then_inc(conv_step, 1)
                    dve.wait_ge(acc_free, f + 3)
                    dve.wait_ge(conv_step, CS * f + 2 * CS + 1)
                    nc.vector.tensor_scalar(conv[:, b], padded[:, b, 0:W_OUT], tap[:, b, 0:1], None,
                                            ALU.mult).then_inc(conv_step, 1)
                    for c in range(1, CONV_W):
                        dve.wait_ge(conv_step, CS * f + 2 * CS + 1 + c)
                        nc.vector.scalar_tensor_tensor(conv[:, b], padded[:, b, c:c + W_OUT], tap[:, b, c:c + 1],
                                                       conv[:, b], ALU.mult, ALU.add).then_inc(conv_step, 1)

                def rotate_in(f, b, within):
                    dve.wait_ge(tp_full, f + 1)
                    nc.vector.tensor_tensor(conv[:, b, 0:SEQ], tp[:, 0:SEQ], sin[:], ALU.mult).then_inc(tp_free, 1)
                    nc.vector.tensor_tensor(wide[:, b, CTX:TOK], wide[:, b, CTX:TOK], cos[:], ALU.mult).then_inc(rot_step, 1)
                    dve.wait_ge(tp_free, f + 2)
                    dve.wait_ge(rot_step, 2 * within + 1)
                    nc.vector.tensor_tensor(wide[:, b, CTX:TOK], wide[:, b, CTX:TOK], conv[:, b, 0:SEQ],
                                            ALU.add).then_inc(rot_step, 1)

                split_lo(0, 0)
                pairs(dve, "xbc", convolve)
                dve.wait_ge(wide_made, NX + 2)
                split_lo(NX + 1, 1)
                split_lo(NX + 2, 0)
                rotate_in(NX, 0, 0)
                with dve.Fori(1, NQK // 2) as i:
                    split_lo(2 * i + (NX + 1), 1)
                    rotate_in(2 * i + (NX - 1), 1, 2 * i - 1)
                    split_lo(2 * i + (NX + 2), 0)
                    rotate_in(2 * i + NX, 0, 2 * i)
                split_lo(NX + NQK + 1, 1)
                rotate_in(NX + NQK - 1, 1, NQK - 1)
                with dve.Fori(1, NG // 2) as i:
                    split_lo(2 * i + (NX + NQK), 0)
                    split_lo(2 * i + (NX + NQK + 1), 1)

            @block.gpsimd
            def _(pool):
                pool.memset(zeros[:], 0.0).then_inc(zeros_made, 1)
                pool.wait_ge(zeros_made, 1)
                for a in (CTX, KV_LAT0 + SEQ):
                    pool.dma_start(qkF[:, a:a + BLANK].rearrange("(f p) t -> p f t", p=P),
                                   zeros[:].unsqueeze(1).to_broadcast([P, NQK, BLANK])).then_inc(blanks_out, 16)

                def store(f, b, kind, turn, within):
                    row = within * P
                    rows = slice(row, row + P) if isinstance(row, int) else ds(row, P)
                    if kind == "xbc":
                        pool.wait_ge(wide_made, f + 3)
                        pool.dma_start(xbcF[rows, :], wide[:, b]).then_inc(wide_out[b], 16)
                        pool.wait_ge(tp_free, f + 2)
                        pool.dma_start(xbcT[:, rows].rearrange("(c p) n -> p c n", p=P),
                                       turned[:, b].rearrange("p (c n) -> p c n", n=P)).then_inc(turned_out[b], 16)
                    elif kind == "qk":
                        pool.wait_ge(rot_step, 2 * within + 2)
                        pool.dma_start(qkF[rows, 0:CTX], wide[:, b, 0:CTX]).then_inc(wide_out[b], 16)
                        pool.dma_start(qkF[rows, KV_LAT0:KV_LAT0 + SEQ], wide[:, b, CTX:TOK]).then_inc(wide_out[b], 16)
                    else:
                        pool.wait_ge(acc_free, f + 3)
                        pool.dma_start(gF[rows, :], wide[:, b, CTX:TOK]).then_inc(wide_out[b], 16)

                for kind in ("xbc", "qk", "gate"):
                    pairs(pool, kind, store)
                for b in range(2):
                    store(NF - 2 + b, b, "gate", NF // 2 - 1, NG - 2 + b)
                pool.wait_ge(blanks_out, 32)
                for b in range(2):
                    pool.wait_ge(wide_out[b], 16 * (NF + NQK) // 2)
                    pool.wait_ge(turned_out[b], 16 * NX // 2)


def project_t_stage(s, hi, lo, zT, vT, dtT):
    nc = s.nc
    NZ, VW, DW = D_INNER // 512, KVH * HD, 2 * HEADS
    STAGED = 4
    with ExitStack() as st:
        w = own(st, nc, "wt_raw", [P, 2, KT, 512])
        whi = own(st, nc, "wt_hi", [P, 2, KT, 512], F32R)
        wlo = own(st, nc, "wt_lo", [P, 2, KT, 512], F32R)
        rows = own(st, nc, "t_rows", [P, STAGED, 512])
        zeros = own(st, nc, "t_zeros", [P, VW])
        acc = bank(st, nc, "t_acc", [P, 8, 512])
        w_in = [s.sem(f"t_w_in{b}") for b in range(2)]
        hi_made, w_free = s.sem("t_hi_made"), s.sem("t_w_free")
        acc_full, acc_free = s.sem("t_acc_full"), s.sem("t_acc_free")
        rows_out = [s.sem(f"t_rows_out{j}") for j in range(STAGED)]
        zeros_made, zeros_out = s.sem("t_zeros_made"), s.sem("t_zeros_out")
        wv = s.x["w_in"][0].rearrange("(k p) n -> p k n", p=P)

        with nc.Block() as block:

            @block.sync
            def _(sp):
                with sp.Fori(0, NZ // 2) as i:
                    for b in range(2):
                        sp.wait_ge(w_free, 2 * i + (b + 1))
                        sp.dma_start(w[:, b], wv[:, :, ds(1024 * i + (Z0 + 512 * b), 512)]).then_inc(w_in[b], 16)
                sp.wait_ge(w_free, NZ + 1)
                sp.dma_start(w[:, 0, :, 0:VW], wv[:, :, V0:V0 + VW]).then_inc(w_in[0], 16)
                sp.dma_start(w[:, 0, :, VW:VW + DW], wv[:, :, DT0:DT0 + DW]).then_inc(w_in[0], 16)

            @block.tensor
            def _(pe):
                def product(u, b, tiles, t0, width):
                    pe.wait_ge(w_free, u + 3)
                    for t in range(tiles):
                        a = (t0 + t) * P
                        pe.wait_ge(acc_free, u * LCHUNK + (t + 1))
                        for k in range(KT):
                            for n_pass, (part, weights) in enumerate(((hi, whi), (hi, wlo), (lo, whi))):
                                mm = nc.tensor.matmul(acc[:, t % 8, 0:width], part[:, k, a:a + P],
                                                      weights[:, b, k, 0:width],
                                                      start=(k == 0 and n_pass == 0), stop=(k == KT - 1 and n_pass == 2))
                        mm.then_inc(acc_full, 1)

                with pe.Fori(0, NZ // 2) as i:
                    for b in range(2):
                        product(2 * i + b, b, LCHUNK, CCHUNK, 512)
                product(NZ, 0, NCHUNK, 0, VW + DW)

            @block.scalar
            def _(act):
                act.sem_inc(acc_free, 8)

                def split_hi(u, b, need, width):
                    act.wait_ge(w_in[b], need)
                    if not isinstance(u, int) or u > 1:
                        act.wait_ge(acc_full, LCHUNK * u - LCHUNK)
                    nc.scalar.copy(whi[:, b, :, 0:width], w[:, b, :, 0:width]).then_inc(hi_made, 1)

                def tile(n, j, turn, func, width, t):
                    act.wait_ge(acc_full, n + 1)
                    act.wait_ge(rows_out[j], 16 * turn)
                    nc.scalar.activation(rows[:, j, 0:width], acc[:, t % 8, 0:width], func).then_inc(acc_free, 1)

                def silu_tiles(u):
                    for t in range(LCHUNK):
                        tile(u * LCHUNK + t, t % STAGED, 2 * u + t // STAGED, ACT.Silu, 512, t)

                split_hi(0, 0, 16, 512)
                split_hi(1, 1, 16, 512)
                silu_tiles(0)
                with act.Fori(1, NZ // 2) as i:
                    split_hi(2 * i, 0, 16 * i + 16, 512)
                    silu_tiles(2 * i - 1)
                    split_hi(2 * i + 1, 1, 16 * i + 16, 512)
                    silu_tiles(2 * i)
                split_hi(NZ, 0, 16 * (NZ // 2) + 32, VW + DW)
                silu_tiles(NZ - 1)
                for t in range(NCHUNK):
                    turns = 2 * NZ + t // STAGED
                    extra = t // STAGED
                    tile(NZ * LCHUNK + t, t % STAGED, turns + extra, ACT.Copy, VW + DW, t)

            @block.vector
            def _(dve):
                dve.sem_inc(w_free, 2)

                def split_lo(u, b, width):
                    dve.wait_ge(hi_made, u + 1)
                    nc.vector.tensor_tensor(wlo[:, b, :, 0:width], w[:, b, :, 0:width],
                                            whi[:, b, :, 0:width].bitcast(F32), ALU.subtract).then_inc(w_free, 1)

                with dve.Fori(0, NZ // 2) as i:
                    for b in range(2):
                        split_lo(2 * i + b, b, 512)
                split_lo(NZ, 0, VW + DW)

            @block.gpsimd
            def _(pool):
                pool.memset(zeros[:], 0.0).then_inc(zeros_made, 1)
                pool.wait_ge(zeros_made, 1)
                for a in (CTX, KV_LAT0 + SEQ):
                    pool.dma_start(vT[a:a + BLANK, :], zeros[:]).then_inc(zeros_out, 16)

                def store(u, col):
                    for t in range(LCHUNK):
                        pool.wait_ge(acc_free, u * LCHUNK + (8 + t + 1))
                        pool.dma_start(zT[t * P:t * P + P, ds(col, 512)], rows[:, t % STAGED, :]).then_inc(rows_out[t % STAGED], 16)

                with pool.Fori(0, NZ) as i:
                    store(i, 512 * i)
                for t in range(NCHUNK):
                    j = t % STAGED
                    pool.wait_ge(acc_free, NZ * LCHUNK + 8 + t + 1)
                    a = t * P if t < CCHUNK else KV_LAT0 + (t - CCHUNK) * P
                    pool.dma_start(vT[a:a + P, :], rows[:, j, 0:VW]).then_inc(rows_out[j], 16)
                    pool.dma_start(dtT[t * P:t * P + P, :], rows[:, j, VW:VW + DW]).then_inc(rows_out[j], 16)
                pool.wait_ge(zeros_out, 32)
                for j in range(STAGED):
                    last = sum(2 for t in range(NCHUNK) if t % STAGED == j)
                    pool.wait_ge(rows_out[j], 16 * (2 * NZ + last))


def decay_stage(s, dtT, tabs, cumrow):
    nc = s.nc
    W = 2 * HEADS
    CUM, ECUM, DT, WX, DEC = range(5)
    SERIES = [1.0 / (2 * n + 1) for n in range(8, 0, -1)]
    with ExitStack() as st:
        sq = own(st, nc, "d_squares", [P, 4, P])
        raw = own(st, nc, "d_raw", [P, NCHUNK, W])
        bias, alog = own(st, nc, "d_bias", [P, W]), own(st, nc, "d_alog", [P, W])
        mag, e, r, q, t = (own(st, nc, f"d_{n}", [P, NCHUNK, W]) for n in ("mag", "e", "r", "q", "t"))
        a = own(st, nc, "d_a", [P, W])
        da, end = own(st, nc, "d_da", [P, NCHUNK, W]), own(st, nc, "d_end", [P, NCHUNK, W])
        tab = own(st, nc, "d_tab", [P, NCHUNK, 5, W])
        rows_hi, rows_lo = own(st, nc, "d_rows_hi", [W, LCHUNK, P], F32R), own(st, nc, "d_rows_lo", [W, LCHUNK, P], F32R)
        cum_ps = bank(st, nc, "d_cum_ps", [P, 2, 512])
        end_ps = bank(st, nc, "d_end_ps", [P, 2, 512])
        row_ps = bank(st, nc, "d_row_ps", [P, LCHUNK, P])
        loaded, step, act_done = s.sem("d_loaded"), s.sem("d_step"), s.sem("d_act_done")
        sums_done, rows_done, copied, stored = s.sem("d_sums_done"), s.sem("d_rows_done"), s.sem("d_copied"), s.sem("d_stored")

        def wide(ap):
            return ap.unsqueeze(1).to_broadcast([P, NCHUNK, W])

        with nc.Block() as block:

            @block.sync
            def _(sp):
                sp.dma_start(raw[:], dtT.rearrange("(c p) n -> p c n", p=P)).then_inc(loaded, 16)
                sp.dma_start(bias[:], s.x["dt_bias"].rearrange("a d h -> a (d h)").to_broadcast([P, W])).then_inc(loaded, 16)
                sp.dma_start(alog[:], s.x["a_log"].rearrange("a d h -> a (d h)").to_broadcast([P, W])).then_inc(loaded, 16)
                sp.dma_start(sq[:], s.squares.rearrange("p (a q) -> p a q", q=P)[:, 0:4, :]).then_inc(loaded, 16)
                sp.wait_ge(copied, 2)
                sp.dma_start(tabs.rearrange("c p n -> p c n"), tab[:].rearrange("p c k n -> p c (k n)")).then_inc(stored, 16)
                sp.wait_ge(copied, 4)
                for part, rows in enumerate((rows_hi, rows_lo)):
                    sp.dma_start(cumrow[:, part].rearrange("c n i -> n c i"), rows[:].bitcast(F32)).then_inc(stored, 16)
                sp.wait_ge(stored, 48)

            @block.vector
            def _(dve):
                done = 0

                def then(ins):
                    nonlocal done
                    done += 1
                    ins.then_inc(step, 1)
                    dve.wait_ge(step, done)

                V = nc.vector
                dve.wait_ge(loaded, 64)
                then(V.tensor_tensor(raw[:], raw[:], wide(bias[:]), ALU.add))
                then(V.tensor_scalar(mag[:], raw[:], -1.0, None, ALU.mult))
                then(V.tensor_tensor(mag[:], mag[:], raw[:], ALU.max))
                dve.wait_ge(act_done, 1)
                then(V.tensor_scalar(t[:], e[:], 2.0, None, ALU.add))
                then(V.reciprocal(q[:], t[:]))
                then(V.tensor_tensor(r[:], e[:], q[:], ALU.mult))
                then(V.tensor_tensor(q[:], r[:], r[:], ALU.mult))
                then(V.tensor_scalar(t[:], q[:], SERIES[0], None, ALU.mult))
                for c in SERIES[1:]:
                    then(V.scalar_tensor_tensor(t[:], t[:], c, q[:], ALU.add, ALU.mult))
                then(V.scalar_tensor_tensor(t[:], t[:], 1.0, r[:], ALU.add, ALU.mult))
                then(V.tensor_scalar(raw[:], raw[:], 0.0, None, ALU.max))
                then(V.scalar_tensor_tensor(tab[:, :, DT, :], t[:], 2.0, raw[:], ALU.mult, ALU.add))
                dve.wait_ge(act_done, 2)
                then(V.tensor_scalar(a[:], a[:], -1.0, None, ALU.mult))
                V.tensor_tensor(da[:], tab[:, :, DT, :], wide(a[:]), ALU.mult).then_inc(copied, 1)
                dve.wait_ge(sums_done, 1)
                for d in range(2):
                    h = slice(HEADS * d, HEADS * d + HEADS)
                    then(V.tensor_copy(tab[:, :, CUM, h], cum_ps[:, d, 0:NCHUNK * HEADS].rearrange("p (c h) -> p c h", h=HEADS)))
                    then(V.tensor_copy(end[:, :, h], end_ps[:, d, 0:NCHUNK * HEADS].rearrange("p (c h) -> p c h", h=HEADS)))
                then(V.tensor_tensor(r[:], end[:], tab[:, :, CUM, :], ALU.subtract))
                V.nop().then_inc(rows_done, 1)
                dve.wait_ge(act_done, 5)
                V.tensor_tensor(tab[:, :, WX, :], q[:], tab[:, :, DT, :], ALU.mult).then_inc(copied, 1)
                dve.wait_ge(rows_done, 2)
                V.tensor_copy(rows_hi[:], row_ps[0:W]).then_inc(copied, 1)
                dve.wait_ge(copied, 3)
                V.tensor_tensor(rows_lo[:], row_ps[0:W], rows_hi[:].bitcast(F32), ALU.subtract).then_inc(copied, 1)

            @block.scalar
            def _(act):
                act.wait_ge(step, 3)
                nc.scalar.activation(e[:], mag[:], ACT.Exp, scale=-1.0).then_inc(act_done, 1)
                nc.scalar.activation(a[:], alog[:], ACT.Exp).then_inc(act_done, 1)
                act.wait_ge(rows_done, 1)
                nc.scalar.activation(q[:], r[:], ACT.Exp).then_inc(act_done, 1)
                nc.scalar.activation(tab[:, :, ECUM, :], tab[:, :, CUM, :], ACT.Exp).then_inc(act_done, 1)
                nc.scalar.activation(tab[:, :, DEC, :], end[:], ACT.Exp).then_inc(act_done, 1)

            @block.tensor
            def _(pe):
                pe.wait_ge(copied, 1)
                for d, triangle in ((0, 1), (1, 2)):
                    rhs = da[:, :, HEADS * d:HEADS * d + HEADS]
                    out = [o[:, d, 0:NCHUNK * HEADS].rearrange("p (c h) -> p c h", h=HEADS) for o in (cum_ps, end_ps)]
                    nc.tensor.matmul(out[0], sq[:, triangle, :], rhs, start=True, stop=True)
                    mm = nc.tensor.matmul(out[1], sq[:, 3, :], rhs, start=True, stop=True)
                mm.then_inc(sums_done, 1)
                pe.wait_ge(rows_done, 1)
                for c in range(LCHUNK):
                    mm = nc.tensor.transpose(row_ps[0:W, c, :], tab[:, CCHUNK + c, CUM, :], sq[:, 0, :])
                mm.then_inc(rows_done, 1)


def states_stage(s, xbcT, tabs, before):
    nc = s.nc
    ECOLS = 2 * HEADS
    with ExitStack() as st:
        x = own(st, nc, "s_x", [P, 2, 2, D_INNER])
        bt = own(st, nc, "s_bt", [P, 2, 2, GROUPS * STATE])
        tab = own(st, nc, "s_tab", [P, 2, 2, 5, ECOLS])
        xw = own(st, nc, "s_xw", [P, 2, 2, D_INNER])
        state = own(st, nc, "s_state", [P, 2, 2, D_INNER])
        add = bank(st, nc, "s_add", [P, 2, D_INNER])
        loaded = [[s.sem(f"s_loaded{d}{b}") for b in range(2)] for d in range(2)]
        kept = [[s.sem(f"s_kept{d}{b}") for b in range(2)] for d in range(2)]
        x_free, xw_made, added, decayed = s.sem("s_x_free"), s.sem("s_xw_made"), s.sem("s_added"), s.sem("s_decayed")
        made = s.sem("s_state_made")

        def heads(ap):
            return ap.rearrange("p (h q) -> p h q", q=PDIM)

        def column(ap):
            return ap.unsqueeze(2).to_broadcast([P, HEADS, PDIM])

        def steps(eng, step):
            for n in range(CCHUNK):
                step(n, n, 0, n * P, (CCHUNK - 1 - n) * P)
            with eng.Fori(1, 1 + LCHUNK // 2) as i:
                for b in range(2):
                    step(2 * i + b, b, i, (2 * i + b) * P, (NCHUNK + CCHUNK - 1 - b) * P - 2 * P * i)

        def rows(r):
            return slice(r, r + P) if isinstance(r, int) else ds(r, P)

        with nc.Block() as block:

            @block.sync
            def _(sp):
                def load(n, b, turn, *rs):
                    sp.wait_ge(x_free, 2 * n + 2)
                    for d, r in enumerate(rs):
                        sem = loaded[d][b]
                        sp.dma_start(x[:, d, b], xbcT[rows(r), 0:D_INNER]).then_inc(sem, 16)
                        sp.dma_start(bt[:, d, b], xbcT[rows(r), D_INNER:D_INNER + GROUPS * STATE]).then_inc(sem, 16)
                        sp.dma_start(tab[:, d, b], tabs.rearrange("c p n -> (c p) n")[rows(r), :].rearrange("p (k n) -> p k n", k=5)).then_inc(sem, 16)

                steps(sp, load)

            @block.gpsimd
            def _(pool):
                pool.sem_inc(xw_made, 4)

                def weigh(n, b, turn, *rs):
                    for d in range(2):
                        pool.wait_ge(loaded[d][b], 48 * turn + 48)
                        pool.wait_ge(added, 2 * n + (d + 1))
                        nc.gpsimd.tensor_tensor(heads(xw[:, d, b]), heads(x[:, d, b]),
                                                column(tab[:, d, b, 3, HEADS * d:HEADS * d + HEADS]), ALU.mult).then_inc(xw_made, 1)

                steps(pool, weigh)

            @block.tensor
            def _(pe):
                pe.sem_inc(added, 4)

                def product(n, b, turn, *rs):
                    for d in range(2):
                        pe.wait_ge(xw_made, 2 * n + (d + 5))
                        pe.wait_ge(made, 2 * n + (d + 1))
                        for g in range(GROUPS):
                            mm = nc.tensor.matmul(add[:, d, 512 * g:512 * g + 512], bt[:, d, b, STATE * g:STATE * g + STATE],
                                                  xw[:, d, b, 512 * g:512 * g + 512], start=True, stop=True)
                        mm.then_inc(added, 1)

                steps(pe, product)

            @block.vector
            def _(dve):
                dve.sem_inc(x_free, 4)
                dve.memset(state[:, :, 0, :], 0.0).then_inc(made, 2)

                def update(n, b, turn, *rs):
                    for d in range(2):
                        dve.wait_ge(made, 2 * n + (d + 1))
                        dve.wait_ge(loaded[d][b], 48 * turn + 48)
                        if not isinstance(turn, int):
                            dve.wait_ge(kept[d][1 - b], 16 * (turn - 1) if b == 0 else 16 * turn)
                        nc.vector.tensor_tensor(heads(state[:, d, 1 - b]), heads(state[:, d, b]),
                                                column(tab[:, d, b, 4, HEADS * d:HEADS * d + HEADS]), ALU.mult).then_inc(decayed, 1)
                        dve.wait_ge(decayed, 2 * n + (d + 1))
                        dve.wait_ge(added, 2 * n + (d + 5))
                        dve.nop().then_inc(x_free, 1)
                        nc.vector.tensor_tensor(state[:, d, 1 - b], state[:, d, 1 - b], add[:, d], ALU.add).then_inc(made, 1)

                steps(dve, update)

            @block.scalar
            def _(act):
                def keep(n, b, turn, *rs):
                    if isinstance(turn, int):
                        return
                    for d, r in enumerate(rs):
                        act.wait_ge(made, 2 * n + (d + 1))
                        act.dma_start(before[d].rearrange("c n q -> (c n) q")[rows(r - CTX), :], state[:, d, b]).then_inc(kept[d][b], 16)

                steps(act, keep)
                for d in range(2):
                    for b in range(2):
                        act.wait_ge(kept[d][b], 16 * LCHUNK // 2)


def scan_output_stage(s, xbcT, xbcF, zT, tabs, cumrow, before, yT):
    nc = s.nc
    V = nc.vector
    LANES = 4
    NARG = 2 + 2 * LANES
    ONES, HI, LO = slice(0, 2), slice(2, 2 + LANES), slice(2 + LANES, NARG)
    BANKS = 2 * HPG // LANES
    G = GROUPS
    with ExitStack() as st:
        sq = own(st, nc, "y_squares", [P, 3, P])
        ident = own(st, nc, "y_ident", [P, P], F32R)
        neg, negs = own(st, nc, "y_neg", [P, 2, P]), own(st, nc, "y_negs", [P, 2, LANES, P], F32R)
        dskip = own(st, nc, "y_dskip", [P, HEADS])
        x, z = own(st, nc, "y_x", [P, 2, D_INNER]), own(st, nc, "y_z", [P, 2, D_INNER])
        bc = own(st, nc, "y_bc", [P, 2, 2, GROUPS, P])
        before_t = own(st, nc, "y_before", [P, 2, 2, D_INNER])
        tab = own(st, nc, "y_tab", [P, 2, 5, 2, HEADS])
        own_cum = own(st, nc, "y_own_cum", [NARG, 2, 2, HEADS // LANES, P], F32R)
        all_cum = own(st, nc, "y_all_cum", [NARG, 2, 2, HPG, P], F32R)
        decay = own(st, nc, "y_decay", [P, 2, 2, HPG, P])
        xs = own(st, nc, "y_xs", [P, 2, 3, 512])
        part, pre = own(st, nc, "y_part", [P, 2, 512]), own(st, nc, "y_pre", [P, 2, 512])
        y = own(st, nc, "y_y", [P, D_INNER])
        g_ps = bank(st, nc, "y_g_ps", [P, 2, GROUPS, P])
        arg_ps = bank(st, nc, "y_arg_ps", [P, 2, LANES, P])
        off_ps, diag_ps = bank(st, nc, "y_off_ps", [P, 2, 512]), bank(st, nc, "y_diag_ps", [P, 2, 512])
        const_in, ready = s.sem("y_const_in"), s.sem("y_ready")
        tiles_in, cum_in = [s.sem(f"y_tiles_in{b}") for b in range(2)], [s.sem(f"y_cum_in{b}") for b in range(2)]
        args_made, exps_made, g_made, l_made = (s.sem(f"y_{n}") for n in ("args_made", "exps_made", "g_made", "l_made"))
        xs_made, off_made, off_read, diag_made, diag_read = (s.sem(f"y_{n}") for n in ("xs_made", "off_made", "off_read", "diag_made", "diag_read"))
        part_step, y_step, y_made, y_out, carrier, dve_carrier = (s.sem(f"y_{n}") for n in ("part_step", "y_step", "y_made", "y_out", "carrier", "dve_carrier"))
        TI = 9 * 16
        bf = xbcF.rearrange("(a g n) t -> n a g t", g=GROUPS, n=P)

        def cut(start, size):
            return slice(start, start + size) if isinstance(start, int) else ds(start, size)

        def chunks(eng, step):
            with eng.Fori(0, LCHUNK // 2 - 1) as i:
                for b in range(2):
                    step(2 * i + b, b, i, True)
            for b in range(2):
                step(LCHUNK - 2 + b, b, LCHUNK // 2 - 1, b == 0)

        def heads(ap):
            return ap.rearrange("p (h q) -> p h q", q=PDIM)

        def with_next(ahead, now):
            def step(n, b, i, more):
                for g in range(G):
                    if g < G - 1:
                        ahead(n, b, i, g + 1)
                    elif more:
                        ahead(n + 1, 1 - b, i + b, 0)
                    now(n, b, i, g)
            return step

        with nc.Block() as block:

            @block.sync
            def _(sp):
                def load_cum(n, g):
                    sp.wait_ge(args_made, BANKS * G * n + (BANKS * (g - 1) + BANKS + 1))
                    sp.sem_inc(carrier, 1)
                    src = cumrow.rearrange("c e (d h) i -> c e d h i", d=2)[cut(n, 1), :, :, HPG * g:HPG * g + HPG, :]
                    for d in range(2):
                        sp.dma_start(all_cum[ONES, g % 2, d].bitcast(F32), src[0:1, :, d].rearrange("c e h i -> (c e) h i")).then_inc(cum_in[g % 2], 16)

                def load_tiles(n, b):
                    sp.wait_ge(y_made, G * n + 1)
                    sp.sem_inc(carrier, 1)
                    for a in range(2):
                        sp.dma_start(bc[:, b, a], bf[:, D_INNER // 512 + a, :, cut(n * P + CTX, P)]).then_inc(tiles_in[b], 16)
                    sp.dma_start(tab[:, b], tabs.rearrange("c p n -> (c p) n")[cut(n * P + CTX, P), :].rearrange("p (k d h) -> p k d h", k=5, d=2)).then_inc(tiles_in[b], 16)
                    for part_, lanes in enumerate((HI, LO)):
                        src = cumrow[cut(n, 1), part_].rearrange("c (q r) i -> (c r) q i", r=LANES)
                        sp.dma_start(own_cum[lanes, b].rearrange("r d q i -> r (d q) i").bitcast(F32), src).then_inc(tiles_in[b], 16)
                    sp.dma_start(x[:, b], xbcT[cut(n * P + CTX, P), 0:D_INNER]).then_inc(tiles_in[b], 16)
                    for d in range(2):
                        sp.dma_start(before_t[:, b, d], before[d].rearrange("c n q -> (c n) q")[cut(n * P, P), :]).then_inc(tiles_in[b], 16)
                    sp.dma_start(z[:, b], zT[cut(n * P, P), :]).then_inc(tiles_in[b], 16)

                def step(n, b, i, more):
                    for g in range(G):
                        load_cum(n, g)
                    if more:
                        load_tiles(n + 1, 1 - b)

                sp.dma_start(sq[:], s.squares.rearrange("p (a q) -> p a q", q=P)[:, 0:3, :]).then_inc(const_in, 16)
                sp.dma_start(dskip[:], s.x["d_skip"].to_broadcast([P, HEADS])).then_inc(const_in, 16)
                sp.dma_start(all_cum[2:NARG].rearrange("r b d h i -> r b (d h i)")[:, 0].bitcast(F32), s.lanes).then_inc(const_in, 16)
                sp.dma_start(all_cum[2:NARG].rearrange("r b d h i -> r b (d h i)")[:, 1].bitcast(F32), s.lanes).then_inc(const_in, 16)
                load_tiles(0, 0)
                chunks(sp, step)

            @block.tensor
            def _(pe):
                pe.sem_inc(args_made, BANKS + 1)

                def exponents(n, b, i, g):
                    if g == 0:
                        pe.wait_ge(tiles_in[b], TI * i + TI)
                        for k in range(G):
                            mm = nc.tensor.matmul(g_ps[:, b, k, :], bc[:, b, 0, k, :], bc[:, b, 1, k, :], start=True, stop=True)
                        mm.then_inc(g_made, 1)
                    pe.wait_ge(cum_in[g % 2], 64 * n + (32 * (g // 2) + 32))
                    for k in range(BANKS):
                        d, half = k // 2, k % 2
                        pe.wait_ge(exps_made, BANKS * G * n + (BANKS * g + k + 1))
                        nc.tensor.matmul(arg_ps[:, k % 2], ident[:], negs[:, d], start=True, stop=False)
                        nc.tensor.matmul(arg_ps[:, k % 2], own_cum[:, b, d, 2 * g + half, :],
                                         all_cum[:, g % 2, d, LANES * half:LANES * half + LANES, :], start=False, stop=True).then_inc(args_made, 1)

                def sums(n, b, i, g):
                    pe.wait_ge(off_read, G * n + (g + 1))
                    for d in range(2):
                        mm = nc.tensor.matmul(off_ps[:, d], bc[:, b, 1, g, :], before_t[:, b, d, 512 * g:512 * g + 512], start=True, stop=True)
                    mm.then_inc(off_made, 1)
                    pe.wait_ge(xs_made, 3 * G * n + (3 * g + 3))
                    pe.wait_ge(diag_read, G * n + (g + 1))
                    pe.wait_ge(l_made, 2 * G * n + (2 * g + 2))
                    for h in range(HPG):
                        cols = slice(PDIM * h, PDIM * h + PDIM)
                        nc.tensor.matmul(diag_ps[:, g % 2, cols], decay[:, g % 2, 0, h, :], xs[:, g % 2, 0, cols], start=True, stop=False)
                        mm = nc.tensor.matmul(diag_ps[:, g % 2, cols], decay[:, g % 2, 1, h, :], xs[:, g % 2, 1, cols], start=False, stop=True)
                    mm.then_inc(diag_made, 1)

                pe.wait_ge(const_in, 64)
                pe.wait_ge(ready, 3)
                exponents(0, 0, 0, 0)
                chunks(pe, with_next(exponents, sums))

            @block.scalar
            def _(act):
                act.sem_inc(exps_made, 2)

                def step(n, b, i, more):
                    for g in range(G):
                        act.wait_ge(diag_made, G * n + (g + 1))
                        for k in range(BANKS):
                            d, half = k // 2, k % 2
                            act.wait_ge(args_made, BANKS * G * n + (BANKS * g + k + BANKS + 2))
                            nc.scalar.activation(decay[:, g % 2, d, LANES * half:LANES * half + LANES], arg_ps[:, k % 2], ACT.Exp).then_inc(exps_made, 1)

                chunks(act, step)

            @block.vector
            def _(dve):
                dve.sem_inc(off_read, 1)
                dve.sem_inc(diag_read, 2)
                dve.sem_inc(diag_made, 2)
                V.memset(own_cum[ONES].bitcast(F32), 1.0).then_inc(ready, 1)
                dve.wait_ge(const_in, 64)
                V.tensor_copy(ident[:], sq[:, 0, :])
                V.tensor_scalar(neg[:], sq[:, 1:3, :], -NEG, NEG, ALU.mult, ALU.add).then_inc(ready, 1)
                dve.wait_ge(ready, 2)
                V.tensor_copy(negs[:], neg[:].unsqueeze(2).to_broadcast([P, 2, LANES, P])).then_inc(ready, 1)

                def step(n, b, i, more):
                    dve.wait_ge(tiles_in[b], TI * i + TI)
                    dve.wait_ge(g_made, n + 1)
                    for g in range(G):
                        at = 3 * G * n + 3 * g
                        for d in range(2):
                            dve.wait_ge(exps_made, BANKS * G * n + (BANKS * g + 2 * d + 4))
                            V.tensor_tensor(decay[:, g % 2, d], decay[:, g % 2, d], g_ps[:, b, g, :].unsqueeze(1).to_broadcast([P, HPG, P]),
                                            ALU.mult).then_inc(l_made, 1)
                        dve.wait_ge(off_made, G * n + (g + 1))
                        dve.wait_ge(part_step, at + 1)
                        for d in range(2):
                            ins = V.tensor_tensor(heads(part[:, d]), heads(off_ps[:, d]),
                                                  tab[:, b, 1, d, HPG * g:HPG * g + HPG].unsqueeze(2).to_broadcast([P, HPG, PDIM]), ALU.mult)
                            ins.then_inc(part_step, 1)
                        dve.wait_ge(part_step, at + 3)
                        V.tensor_tensor(part[:, 0], part[:, 0], part[:, 1], ALU.add).then_inc(off_read, 1)
                        dve.wait_ge(off_read, G * n + (g + 2))
                        dve.wait_ge(diag_made, G * n + (g + 3))
                        dve.wait_ge(y_made, G * n + (g + 3))
                        V.tensor_tensor(pre[:, g % 2], part[:, 0], diag_ps[:, g % 2], ALU.add).then_inc(diag_read, 1)
                        dve.wait_ge(diag_read, G * n + (g + 3))
                        dve.sem_inc(part_step, 1)

                dve.sem_inc(part_step, 1)
                chunks(dve, step)

            @block.gpsimd
            def _(pool):
                pool.sem_inc(y_made, G)
                pool.wait_ge(const_in, 64)

                def scale(n, b, i, g):
                    if g == 0:
                        pool.wait_ge(tiles_in[b], TI * i + TI)
                    pool.wait_ge(diag_made, G * n + (g + 1))
                    pool.wait_ge(y_made, G * n + (g + 3))
                    hs = slice(HPG * g, HPG * g + HPG)
                    for j in range(3):
                        col = tab[:, b, 2, j, hs] if j < 2 else dskip[:, hs]
                        nc.gpsimd.tensor_tensor(heads(xs[:, g % 2, j]), heads(x[:, b, 512 * g:512 * g + 512]),
                                                col.unsqueeze(2).to_broadcast([P, HPG, PDIM]), ALU.mult).then_inc(xs_made, 1)

                def finish(n, b, i, g):
                    cols = slice(512 * g, 512 * g + 512)
                    pool.wait_ge(diag_read, G * n + (g + 3))
                    pool.wait_ge(xs_made, 3 * G * n + (3 * g + 3))
                    nc.gpsimd.tensor_tensor(xs[:, g % 2, 2], pre[:, g % 2], xs[:, g % 2, 2], ALU.add).then_inc(y_step, 1)
                    pool.wait_ge(y_step, G * n + (g + 1))
                    nc.gpsimd.tensor_tensor(y[:, cols], xs[:, g % 2, 2], z[:, b, cols], ALU.mult).then_inc(y_made, 1)
                    if g == G - 1:
                        pool.wait_ge(y_made, G * n + 2 * G)
                        pool.sem_inc(dve_carrier, 1)
                        pool.dma_start(yT[cut(n * P, P), :], y[:]).then_inc(y_out, 16)
                        pool.wait_ge(y_out, 16 * n + 16)

                scale(0, 0, 0, 0)
                chunks(pool, with_next(scale, finish))


def attention_stage(s, qkF, vT, aF):
    nc = s.nc
    V = nc.vector
    KEYS = CTX + 3 * P
    NKT = KEYS // P
    PER_KV = QH // KVH
    TOP_HI, TOP_LO = HD, HD + 32
    K2 = TOP_LO + 1
    ORDER = (0, 2, 1, 4, 3)
    EDGES = (2, 4)
    HEAD_CUTS = ((0, 4), (4, 10), (10, 16))
    with ExitStack() as st:
        ident = own(st, nc, "a_ident", [P, P])
        sink, negsink = own(st, nc, "a_sink", [P, QH]), own(st, nc, "a_negsink", [P, QH])
        q_raw, k_raw = own(st, nc, "a_q_raw", [P, QH, P]), own(st, nc, "a_k_raw", [P, KVH, 3 * P])
        kc_raw = own(st, nc, "a_kc_raw", [P, KVH, CTX])
        q1, q2 = own(st, nc, "a_q1", [P, 2, QH, P], F32R), own(st, nc, "a_q2", [P, 2, QH, P], F32R)
        k1, k2 = own(st, nc, "a_k1", [P, 2, KVH, KEYS], F32R), own(st, nc, "a_k2", [P, 2, KVH, KEYS], F32R)
        vctx, vwin = own(st, nc, "a_vctx", [P, CCHUNK, KVH, 2 * HD]), own(st, nc, "a_vwin", [P, 2, 3, KVH, 2 * HD])
        mask, edge = own(st, nc, "a_mask", [P, 2, KEYS]), own(st, nc, "a_edge", [P, 2, 2, P])
        masked = own(st, nc, "a_masked", [P, 2, KEYS])
        top, negtop = own(st, nc, "a_top", [P, QH]), own(st, nc, "a_negtop", [P, QH])
        sink_col, sunk = own(st, nc, "a_sink_col", [QH, 1]), own(st, nc, "a_sunk", [QH, P])
        sunk_row, sum_cols = own(st, nc, "a_sunk_row", [1, 2, QH, P]), own(st, nc, "a_sum_cols", [1, 2 * HD])
        thi, tlo = own(st, nc, "a_thi", [QH, P], F32R), own(st, nc, "a_tlo", [QH, P], F32R)
        prob = own(st, nc, "a_prob", [P, 2, NKT, PER_KV, P])
        cols, inverse = own(st, nc, "a_cols", [P, 2, QH, P]), own(st, nc, "a_inverse", [HD, QH, P])
        sums, inv_sums = own(st, nc, "a_sums", [P, QH]), own(st, nc, "a_inv_sums", [P, QH])
        a_ps = bank(st, nc, "a_a_ps", [P, 2, 1024])
        b_ps = bank(st, nc, "a_b_ps", [P, 2, PER_KV, P])
        c_ps = bank(st, nc, "a_c_ps", [P, PER_KV, P])
        tp = bank(st, nc, "a_tp", [P, 512])
        const_in, raw_in, top_in = s.sem("a_const_in"), s.sem("a_raw_in"), s.sem("a_top_in")
        block_in = [s.sem(f"a_block_in{b}") for b in range(2)]
        fixed, k_hi, q_hi, k_lo, q_lo, q2_made = (s.sem(f"a_{n}") for n in ("fixed", "k_hi", "q_hi", "k_lo", "q_lo", "q2_made"))
        scored, maxed, negated, sunk_made = (s.sem(f"a_{n}") for n in ("scored", "maxed", "negated", "sunk_made"))
        top_turned, top_hi, top_lo = s.sem("a_top_turned"), s.sem("a_top_hi"), s.sem("a_top_lo")
        b_made, b_masked, exps_made = s.sem("a_b_made"), s.sem("a_b_masked"), s.sem("a_exps_made")
        summed, cols_made, carrier = s.sem("a_summed"), s.sem("a_cols_made"), s.sem("a_carrier")
        sums_in, inverted, inv_out, inv_in = s.sem("a_sums_in"), s.sem("a_inverted"), s.sem("a_inv_out"), s.sem("a_inv_in")
        divided, cols_out, stored = s.sem("a_divided"), s.sem("a_cols_out"), s.sem("a_stored")
        inv_rows = s.scratch("inv_rows", [P, QH])
        kc_in, blanked, pool_carrier, sp_carrier = s.sem("a_kc_in"), s.sem("a_blanked"), s.sem("a_pool_carrier"), s.sem("a_sp_carrier")
        RAW_LOADS, BLOCK_LOADS = 4, 5
        G = KVH

        def cut(start, size):
            return slice(start, start + size) if isinstance(start, int) else ds(start, size)

        def blocks(eng, step):
            with eng.Fori(0, LCHUNK // 2 - 1) as i:
                for b in range(2):
                    step(2 * i + b, b, i, True, True)
            step(LCHUNK - 2, 0, LCHUNK // 2 - 1, False, True)
            step(LCHUNK - 1, 1, LCHUNK // 2 - 1, False, False)

        with nc.Block() as block:

            @block.sync
            def _(sp):
                kF = qkF[QH * HD:, :].rearrange("(g d) t -> d g t", d=HD)
                qF = qkF[0:QH * HD, :].rearrange("(h d) t -> d h t", d=HD)

                def load_raw(m):
                    for half in range(2):
                        part = slice(HD * half, HD * half + HD)
                        sp.dma_start(k_raw[part], kF[:, :, cut(m * P + CTX, 3 * P)]).then_inc(raw_in, 16)
                        sp.dma_start(q_raw[part], qF[:, :, cut(m * P + KV_LAT0, P)]).then_inc(raw_in, 16)

                def load_block(m, b):
                    for c in range(3):
                        sp.dma_start(vwin[:, b, c, :, 0:HD],
                                     vT[cut(m * P + (CTX + c * P), P), :].rearrange("p (g d) -> p g d", d=HD)).then_inc(block_in[b], 16)
                    sp.dma_start(mask[:, b], s.masks.rearrange("c p n -> (c p) n")[cut(m * P, P), :]).then_inc(block_in[b], 16)
                    sp.dma_start(edge[:, b], s.edges.rearrange("c p (e q) -> (c p) e q", e=2)[cut(m * P, P)]).then_inc(block_in[b], 16)

                def load_top(m, b):
                    sp.wait_ge(top_hi, m + 1)
                    sp.sem_inc(sp_carrier, 1)
                    sp.wait_ge(top_lo, m + 1)
                    sp.sem_inc(sp_carrier, 1)
                    sp.dma_start(q2[TOP_HI:TOP_HI + 1, b].bitcast(F32), thi[:].bitcast(F32)).then_inc(top_in, 16)
                    sp.dma_start(q2[TOP_LO:TOP_LO + 1, b].bitcast(F32), tlo[:].bitcast(F32)).then_inc(top_in, 16)
                    sp.wait_ge(sunk_made, m + 1)
                    sp.sem_inc(sp_carrier, 1)
                    sp.dma_start(sunk_row[0:1, b], sunk[:]).then_inc(top_in, 16)

                def step(n, b, i, split, ahead):
                    if split:
                        sp.wait_ge(k_lo, n + 3)
                        sp.sem_inc(sp_carrier, 1)
                        sp.wait_ge(q_lo, n + 2)
                        sp.sem_inc(sp_carrier, 1)
                        load_raw(n + 2)
                    if ahead:
                        load_top(n + 1, 1 - b)
                    if split:
                        sp.wait_ge(summed, G * n + (G + 2))
                        sp.sem_inc(sp_carrier, 1)
                        load_block(n + 2, b)

                for half in range(2):
                    sp.dma_start(kc_raw[HD * half:HD * half + HD], kF[:, :, 0:CTX]).then_inc(kc_in, 16)
                load_raw(0)
                sp.dma_start(ident[:], s.squares[:, 0:P]).then_inc(const_in, 16)
                sp.dma_start(sink[:], s.x["attn_sink"].to_broadcast([P, QH])).then_inc(const_in, 16)
                sp.dma_start(sink_col[:], s.x["attn_sink"].rearrange("o h -> h o")).then_inc(const_in, 16)
                sp.wait_ge(fixed, 1)
                for c in range(CCHUNK):
                    sp.dma_start(vctx[:, c, :, 0:HD], vT[c * P:c * P + P, :].rearrange("p (g d) -> p g d", d=HD)).then_inc(const_in, 16)
                load_block(0, 0)
                load_block(1, 1)
                sp.wait_ge(k_lo, 2)
                sp.wait_ge(q_lo, 1)
                load_raw(1)
                load_top(0, 0)
                blocks(sp, step)

            CONSTS = 16 * (3 + CCHUNK)

            @block.tensor
            def _(pe):
                pe.sem_inc(summed, 2)

                def a(m, b, heads):
                    for h in heads:
                        pe.wait_ge(maxed, QH * m + (h + 1))
                        g = h // PER_KV
                        for lo, hi in ((0, 512), (512, KEYS)):
                            nc.tensor.matmul(a_ps[:, h % 2, lo:hi], q1[:, b, h], k1[:, b, g, lo:hi], start=True, stop=False)
                            mm = nc.tensor.matmul(a_ps[:, h % 2, lo:hi], q2[0:HD, b, h], k2[0:HD, b, g, lo:hi], start=False, stop=True)
                        mm.then_inc(scored, 1)

                def turn_top(m):
                    pe.wait_ge(negated, m + 2)
                    nc.tensor.transpose(tp[0:QH, 0:P], negtop[:], ident[:]).then_inc(top_turned, 1)

                def b_scores(n, b, g):
                    for k, t in enumerate(ORDER):
                        pe.wait_ge(exps_made, NKT * G * n + (NKT * g + k + 1))
                        out = b_ps[:, (g + k) % 2]
                        nc.tensor.matmul(out, k1[:, b, g, t * P:t * P + P], q1[:, b, PER_KV * g:PER_KV * g + PER_KV], start=True, stop=False)
                        nc.tensor.matmul(out, k2[0:K2, b, g, t * P:t * P + P], q2[0:K2, b, PER_KV * g:PER_KV * g + PER_KV],
                                         start=False, stop=True).then_inc(b_made, 1)

                def c(n, b, g):
                    pe.wait_ge(exps_made, NKT * G * n + (NKT * g + NKT + 2))
                    pe.wait_ge(cols_made, G * n + (g + 1))
                    for t in range(NKT):
                        values = vctx[:, t, g] if t < CCHUNK else vwin[:, b, t - CCHUNK, g]
                        nc.tensor.matmul(c_ps[:], values, prob[:, g % 2, t], start=(t == 0), stop=False)
                    nc.tensor.matmul(c_ps[:], sum_cols[:], sunk_row[:, b, PER_KV * g:PER_KV * g + PER_KV],
                                     start=False, stop=True).then_inc(summed, 1)

                def step(n, b, i, split, ahead):
                    c(n, b, 0)
                    if ahead:
                        pe.wait_ge(block_in[1 - b], 16 * BLOCK_LOADS * i + 16 * BLOCK_LOADS * (1 + b))
                        pe.wait_ge(k_lo, n + 3)
                        pe.wait_ge(q_lo, n + 2)
                        pe.wait_ge(q2_made, n + 2)
                        a(n + 1, 1 - b, range(*HEAD_CUTS[0]))
                    for g in range(1, G):
                        b_scores(n, b, g)
                        if ahead and g < 3:
                            a(n + 1, 1 - b, range(*HEAD_CUTS[g]))
                        elif ahead:
                            turn_top(n + 1)
                        c(n, b, g)
                    if ahead:
                        pe.wait_ge(top_in, 48 * n + 96)
                        b_scores(n + 1, 1 - b, 0)

                pe.wait_ge(const_in, CONSTS)
                for b in range(2):
                    pe.wait_ge(block_in[b], 16 * BLOCK_LOADS)
                pe.wait_ge(k_lo, 2)
                pe.wait_ge(q_lo, 1)
                pe.wait_ge(q2_made, 1)
                a(0, 0, range(QH))
                turn_top(0)
                pe.wait_ge(top_in, 48)
                b_scores(0, 0, 0)
                blocks(pe, step)

            @block.scalar
            def _(act):
                act.sem_inc(exps_made, 2)
                act.sem_inc(cols_made, 1)

                def split_hi(m, b):
                    act.wait_ge(raw_in, 16 * RAW_LOADS * m + 16 * RAW_LOADS)
                    nc.scalar.copy(k1[:, b, :, CTX:KEYS], k_raw[:]).then_inc(k_hi, 1)
                    nc.scalar.copy(q1[:, b], q_raw[:]).then_inc(q_hi, 1)

                def top_parts(m, b):
                    act.wait_ge(top_turned, m + 1)
                    if not isinstance(m, int) or m > 0:
                        act.wait_ge(top_in, 48 * m)
                    nc.scalar.activation(sunk[:], tp[0:QH, 0:P], ACT.Exp, scale=SCALE, bias=sink_col[:]).then_inc(sunk_made, 1)
                    nc.scalar.copy(thi[:], tp[0:QH, 0:P]).then_inc(top_hi, 1)

                def exponentials(n, b, g):
                    act.wait_ge(summed, G * n + (g + 1))
                    for k, t in enumerate(ORDER):
                        act.wait_ge(b_made, NKT * G * n + (NKT * g + k + 1))
                        if t in EDGES:
                            act.wait_ge(b_masked, 2 * G * n + (2 * g + EDGES.index(t) + 1))
                        nc.scalar.activation(prob[:, g % 2, t], b_ps[:, (g + k) % 2], ACT.Exp, scale=SCALE).then_inc(exps_made, 1)

                def keep(n, b, g):
                    act.wait_ge(summed, G * n + (g + 3))
                    if g == 0:
                        act.wait_ge(stored, n + 1)
                    nc.scalar.copy(cols[:, b, PER_KV * g:PER_KV * g + PER_KV], c_ps[:]).then_inc(cols_made, 1)

                def step(n, b, i, split, ahead):
                    keep(n, b, 0)
                    for g in range(1, G):
                        exponentials(n, b, g)
                        if ahead and g == 3:
                            top_parts(n + 1, 1 - b)
                        if split and g == 3:
                            split_hi(n + 2, b)
                        keep(n, b, g)
                    if ahead:
                        exponentials(n + 1, 1 - b, 0)

                act.wait_ge(kc_in, 32)
                for b in range(2):
                    nc.scalar.copy(k1[:, b, :, 0:CTX], kc_raw[:])
                split_hi(0, 0)
                split_hi(1, 1)
                top_parts(0, 0)
                exponentials(0, 0, 0)
                blocks(act, step)

            @block.vector
            def _(dve):
                dve.sem_inc(maxed, 2)
                V.memset(sum_cols[:, 0:HD], 0.0)
                V.memset(sum_cols[:, HD:2 * HD], 1.0)
                V.memset(vctx[:], 1.0)
                V.memset(vwin[:], 1.0).then_inc(fixed, 1)

                def split_lo(m, b):
                    dve.wait_ge(q_hi, m + 1)
                    half = slice(HD, P)
                    V.tensor_tensor(q1[half, b], q_raw[half], q1[half, b].bitcast(F32), ALU.subtract).then_inc(q_lo, 1)

                def maxima(m, b, heads):
                    for h in heads:
                        dve.wait_ge(scored, QH * m + (h + 1))
                        dve.wait_ge(maxed, QH * m + (h + 1))
                        dve.sem_inc(carrier, 1)
                        V.tensor_tensor_reduce(masked[:, h % 2], a_ps[:, h % 2, 0:KEYS], mask[:, b], 1.0, NEG,
                                               ALU.add, ALU.max, top[:, h:h + 1]).then_inc(maxed, 1)

                def negate(m):
                    dve.wait_ge(maxed, QH * m + (QH + 2))
                    V.scalar_tensor_tensor(negtop[:], top[:], -1.0, negsink[:], ALU.mult, ALU.min).then_inc(negated, 1)

                def top_parts(m):
                    dve.wait_ge(top_hi, m + 1)
                    V.tensor_tensor(tlo[:], tp[0:QH, 0:P], thi[:].bitcast(F32), ALU.subtract).then_inc(top_lo, 1)

                def mask_edges(n, b, g):
                    for e, t in enumerate(EDGES):
                        k = ORDER.index(t)
                        dve.wait_ge(b_made, NKT * G * n + (NKT * g + k + 1))
                        out = b_ps[:, (g + k) % 2]
                        V.tensor_tensor(out, out, edge[:, b, e].unsqueeze(1).to_broadcast([P, PER_KV, P]), ALU.add).then_inc(b_masked, 1)

                def invert(n):
                    dve.wait_ge(sums_in, 16 * n + 16)
                    dve.sem_inc(carrier, 1)
                    V.reciprocal(inv_sums[:], sums[:]).then_inc(inverted, 1)

                def step(n, b, i, split, ahead):
                    if ahead:
                        dve.wait_ge(block_in[1 - b], 16 * BLOCK_LOADS * i + 16 * BLOCK_LOADS * (1 + b))
                        maxima(n + 1, 1 - b, range(*HEAD_CUTS[0]))
                    for g in range(1, G):
                        mask_edges(n, b, g)
                        if ahead and g < 3:
                            maxima(n + 1, 1 - b, range(*HEAD_CUTS[g]))
                        if ahead and g == 2:
                            negate(n + 1)
                        if ahead and g == 3:
                            top_parts(n + 1)
                    if ahead:
                        mask_edges(n + 1, 1 - b, 0)
                    if split:
                        split_lo(n + 2, b)
                    invert(n)

                dve.wait_ge(const_in, CONSTS)
                V.tensor_scalar(negsink[:], sink[:], -1.0 / SCALE, None, ALU.mult).then_inc(negated, 1)
                split_lo(0, 0)
                dve.wait_ge(negated, 1)
                for b in range(2):
                    dve.wait_ge(block_in[b], 16 * BLOCK_LOADS)
                maxima(0, 0, range(QH))
                negate(0)
                split_lo(1, 1)
                top_parts(0)
                mask_edges(0, 0, 0)
                blocks(dve, step)

            @block.gpsimd
            def _(pool):
                for b in range(2):
                    nc.gpsimd.memset(q2[HD:P, b].bitcast(F32), 0.0)
                    nc.gpsimd.memset(k2[HD:P, b].bitcast(F32), 0.0).then_inc(blanked, 1)
                pool.wait_ge(blanked, 2)
                pool.wait_ge(kc_in, 32)

                def split_lo(m, b):
                    pool.wait_ge(k_hi, m + 1)
                    nc.gpsimd.tensor_tensor(k2[0:HD, b, :, CTX:KEYS], k_raw[0:HD], k1[0:HD, b, :, CTX:KEYS].bitcast(F32), ALU.subtract).then_inc(k_lo, 1)
                    pool.wait_ge(q_hi, m + 1)
                    pool.sem_inc(pool_carrier, 1)
                    nc.gpsimd.tensor_copy(q2[0:HD, b], q1[0:HD, b].bitcast(F32)).then_inc(q2_made, 1)

                def step(n, b, i, split, ahead):
                    if split:
                        split_lo(n + 2, b)
                    divide(n, b)

                def divide(n, b):
                    pool.wait_ge(cols_made, G * n + (G + 1))
                    pool.sem_inc(pool_carrier, 1)
                    pool.dma_start(sums[:], cols[HD:HD + 1, b]).then_inc(sums_in, 16)
                    pool.wait_ge(inverted, n + 1)
                    pool.sem_inc(pool_carrier, 1)
                    pool.dma_start(inv_rows, inv_sums[:]).then_inc(inv_out, 16)
                    pool.wait_ge(inv_out, 16 * n + 16)
                    pool.sem_inc(pool_carrier, 1)
                    pool.dma_start(inverse[:], inv_rows.rearrange("p h -> (p h)").rearrange("(o h q) -> o h q", o=1, q=P).to_broadcast([HD, QH, P])).then_inc(inv_in, 16)
                    pool.wait_ge(inv_in, 16 * n + 16)
                    pool.sem_inc(pool_carrier, 1)
                    nc.gpsimd.tensor_tensor(cols[0:HD, b], cols[0:HD, b], inverse[:], ALU.mult).then_inc(divided, 1)
                    pool.wait_ge(divided, n + 1)
                    pool.sem_inc(pool_carrier, 1)
                    pool.dma_start(aF[:, cut(n * P, P)].rearrange("(h d) t -> d h t", d=HD), cols[0:HD, b]).then_inc(cols_out, 16)
                    pool.wait_ge(cols_out, 16 * n + 16)
                    pool.sem_inc(stored, 1)

                pool.sem_inc(stored, 2)
                for b in range(2):
                    for row in (TOP_HI, TOP_LO):
                        nc.gpsimd.memset(k2[row:row + 1, b].bitcast(F32), 1.0)
                    pool.wait_ge(k_hi, 1)
                    ins = nc.gpsimd.tensor_tensor(k2[0:HD, b, :, 0:CTX], kc_raw[0:HD], k1[0:HD, b, :, 0:CTX].bitcast(F32), ALU.subtract)
                    if b == 1:
                        ins.then_inc(k_lo, 1)
                for m in range(2):
                    split_lo(m, m)
                blocks(pool, step)


def branch_stage(s, yT, aF, gF, mF):
    nc = s.nc
    V = nc.vector
    HALF = SEQ // 2
    TILES = HALF // P
    KY, KA = D_INNER // P, QH * HD // P
    KW = KY + KA
    with ExitStack() as st:
        ident = own(st, nc, "b_ident", [P, P])
        normw = own(st, nc, "b_normw", [P, KY])
        y = own(st, nc, "b_y", [P, D_INNER])
        full = own(st, nc, "b_full", [P, KY, P])
        a = own(st, nc, "b_a", [P, 2, KA, P])
        ssq, mean, root = (own(st, nc, f"b_{n}", [P, 1]) for n in ("ssq", "mean", "root"))
        hi, lo = own(st, nc, "b_hi", [P, KW, HALF], F32R), own(st, nc, "b_lo", [P, KW, HALF], F32R)
        w = own(st, nc, "b_w", [P, KW, P])
        whi, wlo = own(st, nc, "b_whi", [P, 2, KW, P], F32R), own(st, nc, "b_wlo", [P, 2, KW, P], F32R)
        gates = own(st, nc, "b_gates", [P, 2, 2, HALF])
        m = own(st, nc, "b_m", [P, 2, HALF])
        part = own(st, nc, "b_part", [P, HALF])
        tp = bank(st, nc, "b_tp", [P, KY, P])
        acc = bank(st, nc, "b_acc", [P, 2, 2, 512])
        carrier = s.sem("b_carrier")
        const_in, y_in, w_in = s.sem("b_const_in"), s.sem("b_y_in"), s.sem("b_w_in")
        a_in = [s.sem(f"b_a_in{j}") for j in range(2)]
        gates_in = [s.sem(f"b_gates_in{j}") for j in range(2)]
        m_out = [s.sem(f"b_m_out{j}") for j in range(2)]
        y_free, squared, rooted, step, scaled, turned, full_made = (s.sem(f"b_{n}") for n in (
            "y_free", "squared", "rooted", "step", "scaled", "turned", "full_made"))
        y_split, a_hi, a_split = s.sem("b_y_hi"), s.sem("b_a_hi"), s.sem("b_a_split")
        y_lo, w_hi, w_split, used, m_made, m_step = (s.sem(f"b_{n}") for n in ("y_lo", "w_hi", "w_split", "used", "m_made", "m_step"))
        FT = D // P
        ssd_v = s.x["w_ssd_br"][0].rearrange("(k p) n -> p k n", p=P)
        attn_v = s.x["w_attn_br"][0].rearrange("(k p) n -> p k n", p=P)

        with nc.Block() as block:

            @block.sync
            def _(sp):
                sp.dma_start(ident[:], s.squares[:, 0:P]).then_inc(const_in, 16)
                sp.dma_start(normw[:], s.x["normw"]).then_inc(const_in, 16)
                for half in range(2):
                    with sp.Fori(0, TILES // 2) as i:
                        for b in range(2):
                            n = 2 * i + (half * TILES + b)
                            sp.wait_ge(y_free, n + 1)
                            sp.sem_inc(carrier, 1)
                            sp.dma_start(y[:], yT[ds(n * P, P), :]).then_inc(y_in, 16)
                            sp.wait_ge(a_split, n + 1)
                            sp.sem_inc(carrier, 1)
                            sp.dma_start(a[:, b], aF[:, ds(n * P, P)].rearrange("(k p) t -> p k t", p=P)).then_inc(a_in[b], 16)
                    with sp.Fori(0, FT // 2) as i:
                        for b in range(2):
                            f = 2 * i + (half * FT + b)
                            sp.wait_ge(w_split, f + 1)
                            sp.sem_inc(carrier, 1)
                            col = 2 * P * i + P * b
                            sp.dma_start(w[:, 0:KY], ssd_v[:, :, ds(col, P)]).then_inc(w_in, 16)
                            sp.dma_start(w[:, KY:KW], attn_v[:, :, ds(col, P)]).then_inc(w_in, 16)
                            sp.wait_ge(m_made, f + 1)
                            sp.sem_inc(carrier, 1)
                            for j in range(2):
                                sp.dma_start(gates[:, b, j], gF[ds(col + j * D, P), half * HALF:half * HALF + HALF]).then_inc(gates_in[b], 16)

            @block.scalar
            def _(act):
                for half in range(2):
                    with act.Fori(0, TILES // 2) as i:
                        for b in range(2):
                            n = 2 * i + (half * TILES + b)
                            cols = ds(2 * P * i + P * b, P)
                            act.wait_ge(y_in, 16 * n + 16)
                            act.wait_ge(y_lo, n)
                            nc.scalar.activation(full[:].rearrange("p k n -> p (k n)"), y[:], ACT.Square, accum_out=ssq[:]).then_inc(squared, 1)
                            act.wait_ge(step, 2 * n + 2)
                            nc.scalar.activation(root[:], ssq[:], ACT.Sqrt).then_inc(rooted, 1)
                            act.wait_ge(a_in[b], 16 * (half * TILES // 2) + 16 * i + 16)
                            nc.scalar.copy(hi[:, KY:KW, cols], a[:, b]).then_inc(a_hi, 1)
                            act.wait_ge(full_made, n + 1)
                            nc.scalar.copy(hi[:, 0:KY, cols], full[:]).then_inc(y_split, 1)
                    with act.Fori(0, FT // 2) as i:
                        for b in range(2):
                            f = 2 * i + (half * FT + b)
                            act.wait_ge(w_in, 32 * f + 32)
                            act.wait_ge(used, f + 1)
                            nc.scalar.copy(whi[:, b], w[:]).then_inc(w_hi, 1)

            @block.vector
            def _(dve):
                dve.sem_inc(y_free, 1)
                dve.sem_inc(a_split, 2)
                dve.sem_inc(w_split, 1)
                dve.sem_inc(m_made, 2)
                dve.wait_ge(const_in, 32)
                for half in range(2):
                    if half:
                        dve.wait_ge(used, FT + 2)
                    with dve.Fori(0, TILES // 2) as i:
                        for b in range(2):
                            n = 2 * i + (half * TILES + b)
                            cols = ds(2 * P * i + P * b, P)
                            dve.wait_ge(squared, n + 1)
                            V.tensor_scalar(mean[:], ssq[:], 1.0 / D_INNER, EPS, ALU.mult, ALU.add).then_inc(step, 1)
                            dve.wait_ge(step, 2 * n + 1)
                            V.reciprocal(ssq[:], mean[:]).then_inc(step, 1)
                            dve.wait_ge(rooted, n + 1)
                            V.tensor_scalar(y[:], y[:], root[:], None, ALU.mult).then_inc(scaled, 1)
                            dve.wait_ge(a_hi, n + 1)
                            V.tensor_tensor(lo[:, KY:KW, cols], a[:, b], hi[:, KY:KW, cols].bitcast(F32), ALU.subtract).then_inc(a_split, 1)
                            dve.wait_ge(turned, n + 1)
                            V.sem_inc(y_free, 1)
                            V.tensor_tensor(full[:], tp[:], normw[:].unsqueeze(2).to_broadcast([P, KY, P]), ALU.mult).then_inc(full_made, 1)
                            dve.wait_ge(y_split, n + 1)
                            V.tensor_tensor(lo[:, 0:KY, cols], full[:], hi[:, 0:KY, cols].bitcast(F32), ALU.subtract).then_inc(y_lo, 1)

                    def split_lo(f, b):
                        dve.wait_ge(w_hi, f + 1)
                        V.tensor_tensor(wlo[:, b], w[:], whi[:, b].bitcast(F32), ALU.subtract).then_inc(w_split, 1)

                    def merge(f, b, turn):
                        dve.wait_ge(used, f + 3)
                        dve.wait_ge(gates_in[b], 32 * turn + 32)
                        dve.wait_ge(m_out[b], 16 * turn)
                        dve.wait_ge(m_made, f + 2)
                        V.tensor_tensor(m[:, b], acc[:, b, 0], gates[:, b, 0], ALU.mult).then_inc(m_step, 1)
                        V.tensor_tensor(part[:], acc[:, b, 1], gates[:, b, 1], ALU.mult).then_inc(m_step, 1)
                        dve.wait_ge(m_step, 2 * f + 2)
                        V.tensor_tensor(m[:, b], m[:, b], part[:], ALU.add).then_inc(m_made, 1)

                    f0, t0 = half * FT, half * FT // 2
                    split_lo(f0, 0)
                    with dve.Fori(0, FT // 2 - 1) as i:
                        split_lo(2 * i + (f0 + 1), 1)
                        merge(2 * i + f0, 0, i + t0)
                        split_lo(2 * i + (f0 + 2), 0)
                        merge(2 * i + (f0 + 1), 1, i + t0)
                    split_lo(f0 + FT - 1, 1)
                    merge(f0 + FT - 2, 0, t0 + FT // 2 - 1)
                    merge(f0 + FT - 1, 1, t0 + FT // 2 - 1)

            @block.tensor
            def _(pe):
                pe.sem_inc(used, 2)
                pe.wait_ge(const_in, 32)
                for half in range(2):
                    with pe.Fori(0, TILES) as i:
                        n = i + half * TILES
                        pe.wait_ge(scaled, n + 1)
                        pe.wait_ge(full_made, n)
                        for k in range(KY):
                            mm = nc.tensor.transpose(tp[:, k, :], y[:, k * P:k * P + P], ident[:])
                        mm.then_inc(turned, 1)
                    pe.wait_ge(y_lo, TILES * (half + 1))
                    pe.wait_ge(a_split, TILES * (half + 1) + 2)
                    with pe.Fori(0, FT // 2) as i:
                        for b in range(2):
                            f = 2 * i + (half * FT + b)
                            pe.wait_ge(w_split, f + 2)
                            pe.wait_ge(m_made, f + 1)
                            for j, ks in ((0, range(KY)), (1, range(KY, KW))):
                                for k in ks:
                                    for n_pass, (weights, xpart) in enumerate(((whi, hi), (whi, lo), (wlo, hi))):
                                        mm = nc.tensor.matmul(acc[:, b, j], weights[:, b, k, :], xpart[:, k, :],
                                                              start=(k == ks[0] and n_pass == 0), stop=(k == ks[-1] and n_pass == 2))
                            mm.then_inc(used, 1)

            @block.gpsimd
            def _(pool):
                for half in range(2):
                    with pool.Fori(0, FT // 2) as i:
                        for b in range(2):
                            pool.wait_ge(m_made, 2 * i + (half * FT + b + 3))
                            pool.dma_start(mF[ds(2 * P * i + P * b, P), half * HALF:half * HALF + HALF], m[:, b]).then_inc(m_out[b], 16)
                for b in range(2):
                    pool.wait_ge(m_out[b], 16 * FT)


def residual_stage(s, mod, mF, x1T, h2T, affT):
    nc = s.nc
    V = nc.vector
    B_O, G1, LN_G, LN_B, SC2, SH2 = range(6)
    with ExitStack() as st:
        ident = own(st, nc, "r_ident", [P, P])
        rowv = own(st, nc, "r_rows", [P, 6, D])
        wr = own(st, nc, "r_router", [P, KT, EXPERTS])
        w = own(st, nc, "r_w", [P, KT, 512])
        whi, wlo = own(st, nc, "r_whi", [P, KT, D], F32R), own(st, nc, "r_wlo", [P, KT, D], F32R)
        m = own(st, nc, "r_m", [P, 2, KT, P])
        mhi, mlo = own(st, nc, "r_mhi", [P, 2, KT, P], F32R), own(st, nc, "r_mlo", [P, 2, KT, P], F32R)
        x = own(st, nc, "r_x", [P, 2, D])
        y, x1 = own(st, nc, "r_y", [P, D]), own(st, nc, "r_x1", [P, 2, D])
        h2 = own(st, nc, "r_h2", [P, 2, D])
        h2F = own(st, nc, "r_h2F", [P, KT, P])
        stats, mv, root = own(st, nc, "r_stats", [P, 2, 6]), own(st, nc, "r_mv", [P, 2]), own(st, nc, "r_root", [P, 2])
        carrier, pool_carrier = s.sem("r_carrier"), s.sem("r_pool_carrier")
        small = own(st, nc, "r_small", [P, 4])
        prob = own(st, nc, "r_prob", [P, EXPERTS])
        aff = own(st, nc, "r_aff", [P, EXPERTS])
        affF = own(st, nc, "r_affF", [EXPERTS, SEQ])
        acc = bank(st, nc, "r_acc", [P, 2, D])
        tp = bank(st, nc, "r_tp", [P, KT, P])
        lg = bank(st, nc, "r_logits", [P, 512])
        at = bank(st, nc, "r_affT", [P, 512])
        const_in, w_in, w_hi, w_split = s.sem("r_const_in"), s.sem("r_w_in"), s.sem("r_w_hi"), s.sem("r_w_split")
        m_in = [s.sem(f"r_m_in{b}") for b in range(2)]
        x_in = [s.sem(f"r_x_in{b}") for b in range(2)]
        x1_out = [s.sem(f"r_x1_out{b}") for b in range(2)]
        h2_out = [s.sem(f"r_h2_out{b}") for b in range(2)]
        m_hi, m_split, multiplied, x_free, step = (s.sem(f"r_{n}") for n in ("m_hi", "m_split", "multiplied", "x_free", "step"))
        squared, rooted, affine, gain, h2_made = (s.sem(f"r_{n}") for n in ("squared", "rooted", "affine", "gain", "h2_made"))
        turned, cols_made, routed, exp_made, aff_made, aff_turned, aff_kept, aff_out = (s.sem(f"r_{n}") for n in (
            "turned", "cols_made", "routed", "exp_made", "aff_made", "aff_turned", "aff_kept", "aff_out"))
        VS = 13

        def tiles(eng, step_):
            with eng.Fori(0, LCHUNK // 2) as i:
                for b in range(2):
                    step_(2 * i + b, b, i)

        with nc.Block() as block:

            @block.sync
            def _(sp):
                sp.dma_start(ident[:], s.squares[:, 0:P]).then_inc(const_in, 16)
                for j, row in ((B_O, s.x["b_o"]), (G1, mod[0:1, 2 * D:3 * D]), (LN_G, s.x["ln1_g"]), (LN_B, s.x["ln1_b"]),
                               (SC2, mod[0:1, 4 * D:5 * D]), (SH2, mod[0:1, 3 * D:4 * D])):
                    sp.dma_start(rowv[:, j], row.to_broadcast([P, D])).then_inc(const_in, 16)
                sp.dma_start(wr[:], s.x["w_router"][0].rearrange("(k p) e -> p k e", p=P)).then_inc(const_in, 16)
                for n in range(2):
                    if n:
                        sp.wait_ge(w_split, 1)
                    sp.dma_start(w[:], s.x["w_o"][0].rearrange("(k p) n -> p k n", p=P)[:, :, 512 * n:512 * n + 512]).then_inc(w_in, 16)

                def load(n, b, i):
                    sp.wait_ge(m_split, n + 1)
                    sp.dma_start(m[:, b], mF[:, ds(n * P, P)].rearrange("(k p) t -> p k t", p=P)).then_inc(m_in[b], 16)
                    sp.wait_ge(x_free, n + 1)
                    sp.dma_start(x[:, b], s.x["x"][0, ds(n * P, P), :]).then_inc(x_in[b], 16)

                tiles(sp, load)

            @block.tensor
            def _(pe):
                pe.sem_inc(multiplied, 2)
                pe.wait_ge(const_in, 16 * 8)
                pe.wait_ge(w_split, 2)

                def product(n, b):
                    pe.wait_ge(m_split, n + 3)
                    pe.wait_ge(x_free, n + 1)
                    for k in range(KT):
                        for n_pass, (part, weights) in enumerate(((mhi, whi), (mhi, wlo), (mlo, whi))):
                            for c in range(2):
                                mm = nc.tensor.matmul(acc[:, b, 512 * c:512 * c + 512], part[:, b, k, :], weights[:, k, 512 * c:512 * c + 512],
                                                      start=(k == 0 and n_pass == 0), stop=(k == KT - 1 and n_pass == 2))
                    mm.then_inc(multiplied, 1)

                def route(n, b):
                    pe.wait_ge(h2_made, n + 1)
                    pe.wait_ge(cols_made, n)
                    for k in range(KT):
                        mm = nc.tensor.transpose(tp[:, k, :], h2[:, b, k * P:k * P + P], ident[:])
                    mm.then_inc(turned, 1)
                    pe.wait_ge(cols_made, n + 1)
                    pe.wait_ge(aff_made, n)
                    for k in range(KT):
                        mm = nc.tensor.matmul(lg[:, 0:EXPERTS], h2F[:, k, :], wr[:, k, :], start=(k == 0), stop=(k == KT - 1))
                    mm.then_inc(routed, 1)
                    pe.wait_ge(aff_made, n + 1)
                    pe.wait_ge(aff_kept, n)
                    nc.tensor.transpose(at[0:EXPERTS, 0:P], aff[:], ident[:]).then_inc(aff_turned, 1)

                product(0, 0)
                product(1, 1)
                route(0, 0)
                with pe.Fori(1, LCHUNK // 2) as i:
                    product(2 * i, 0)
                    route(2 * i - 1, 1)
                    product(2 * i + 1, 1)
                    route(2 * i, 0)
                route(LCHUNK - 1, 1)

            @block.scalar
            def _(act):
                for n in range(2):
                    act.wait_ge(w_in, 16 * n + 16)
                    nc.scalar.copy(whi[:, :, 512 * n:512 * n + 512], w[:]).then_inc(w_hi, 1)

                def split_hi(n, b, i):
                    act.wait_ge(m_in[b], 16 * i + 16)
                    act.wait_ge(multiplied, n + 1)
                    nc.scalar.copy(mhi[:, b], m[:, b]).then_inc(m_hi, 1)

                def tile(n, b, i):
                    for k in range(2):
                        act.wait_ge(squared, 2 * n + (k + 1))
                        nc.scalar.activation(root[:, 1:2], root[:, 0:1], ACT.Sqrt).then_inc(rooted, 1)
                    act.wait_ge(turned, n + 1)
                    nc.scalar.copy(h2F[:], tp[:]).then_inc(cols_made, 1)
                    act.wait_ge(step, VS * n + 13)
                    nc.scalar.activation(prob[:], lg[:, 0:EXPERTS], ACT.Exp, bias=small[:, 1:2], accum_out=small[:, 2:3]).then_inc(exp_made, 1)
                    act.wait_ge(aff_turned, n + 1)
                    nc.scalar.copy(affF[:, ds(n * P, P)], at[0:EXPERTS, 0:P]).then_inc(aff_kept, 1)

                split_hi(0, 0, 0)
                with act.Fori(0, LCHUNK // 2 - 1) as i:
                    split_hi(2 * i + 1, 1, i)
                    tile(2 * i, 0, i)
                    split_hi(2 * i + 2, 0, i + 1)
                    tile(2 * i + 1, 1, i)
                split_hi(LCHUNK - 1, 1, LCHUNK // 2 - 1)
                tile(LCHUNK - 2, 0, LCHUNK // 2 - 1)
                tile(LCHUNK - 1, 1, LCHUNK // 2 - 1)
                act.wait_ge(aff_kept, LCHUNK)
                act.dma_start(affT, affF[:]).then_inc(aff_out, 16)
                act.wait_ge(aff_out, 16)

            @block.vector
            def _(dve):
                dve.sem_inc(m_split, 2)
                dve.sem_inc(x_free, 2)
                for n in range(2):
                    dve.wait_ge(w_hi, n + 1)
                    V.tensor_tensor(wlo[:, :, 512 * n:512 * n + 512], w[:], whi[:, :, 512 * n:512 * n + 512].bitcast(F32),
                                    ALU.subtract).then_inc(w_split, 1)
                dve.wait_ge(const_in, 16 * 8)
                V.tensor_scalar(rowv[:, SC2], rowv[:, SC2], 1.0, None, ALU.add).then_inc(step, 1)

                def split_lo(n, b):
                    dve.wait_ge(m_hi, n + 1)
                    V.tensor_tensor(mlo[:, b], m[:, b], mhi[:, b].bitcast(F32), ALU.subtract).then_inc(m_split, 1)

                def tile(n, b, i):
                    at = VS * n

                    def then(ins, k):
                        ins.then_inc(step, 1)
                        dve.wait_ge(step, at + (k + 1))

                    def normalised(src, out, k, which):
                        V.bn_stats(stats[:, 0, :], src[:, 0:512]).then_inc(step, 1)
                        then(V.bn_stats(stats[:, 1, :], src[:, 512:1024]), k + 2)
                        dve.sem_inc(carrier, 1)
                        then(V.bn_aggr(mv[:], stats[:]), k + 3)
                        then(V.tensor_scalar(root[:, 1:2], mv[:, 1:2], EPS, None, ALU.add), k + 4)
                        V.reciprocal(root[:, 0:1], root[:, 1:2]).then_inc(squared, 1)
                        dve.wait_ge(rooted, 2 * n + (which + 1))
                        return V.tensor_scalar(out, src, mv[:, 0:1], root[:, 1:2], ALU.subtract, ALU.mult)

                    dve.wait_ge(multiplied, n + 3)
                    dve.wait_ge(x_in[b], 16 * i + 16)
                    for c in range(2):
                        cut = slice(512 * c, 512 * c + 512)
                        ins = V.tensor_tensor(y[:, cut], acc[:, b, cut], rowv[:, B_O, cut], ALU.add)
                    then(ins, 1)
                    then(V.tensor_tensor(y[:], y[:], rowv[:, G1], ALU.mult), 2)
                    V.scalar_tensor_tensor(y[:], x[:, b], ALPHA, y[:], ALU.mult, ALU.add).then_inc(x_free, 1)
                    dve.wait_ge(x_free, n + 3)
                    dve.wait_ge(x1_out[b], 16 * i)
                    normalised(y[:], x1[:, b], 2, 0).then_inc(affine, 1)
                    dve.wait_ge(affine, 4 * n + 2)
                    dve.wait_ge(h2_out[b], 16 * i)
                    normalised(x1[:, b], h2[:, b], 6, 1).then_inc(affine, 1)
                    dve.wait_ge(routed, n + 1)
                    then(V.reduce_max(small[:, 0:1], lg[:, 0:EXPERTS], AX_X), 11)
                    V.tensor_scalar(small[:, 1:2], small[:, 0:1], -1.0, None, ALU.mult).then_inc(step, 1)
                    dve.wait_ge(exp_made, n + 1)
                    then(V.reciprocal(small[:, 3:4], small[:, 2:3]), 13)
                    dve.wait_ge(aff_turned, n)
                    V.tensor_scalar(aff[:], prob[:], small[:, 3:4], None, ALU.mult).then_inc(aff_made, 1)

                split_lo(0, 0)
                with dve.Fori(0, LCHUNK // 2 - 1) as i:
                    split_lo(2 * i + 1, 1)
                    tile(2 * i, 0, i)
                    split_lo(2 * i + 2, 0)
                    tile(2 * i + 1, 1, i)
                split_lo(LCHUNK - 1, 1)
                tile(LCHUNK - 2, 0, LCHUNK // 2 - 1)
                tile(LCHUNK - 1, 1, LCHUNK // 2 - 1)

            @block.gpsimd
            def _(pool):
                G = nc.gpsimd
                pool.wait_ge(step, 1)

                def tile(n, b, i):
                    pool.wait_ge(affine, 4 * n + 1)
                    G.tensor_tensor(x1[:, b], x1[:, b], rowv[:, LN_G], ALU.mult).then_inc(gain, 1)
                    pool.wait_ge(gain, 2 * n + 1)
                    G.tensor_tensor(x1[:, b], x1[:, b], rowv[:, LN_B], ALU.add).then_inc(affine, 1)
                    pool.wait_ge(affine, 4 * n + 2)
                    pool.sem_inc(pool_carrier, 1)
                    pool.dma_start(x1T[ds(n * P, P), :], x1[:, b]).then_inc(x1_out[b], 16)
                    pool.wait_ge(affine, 4 * n + 3)
                    G.tensor_tensor(h2[:, b], h2[:, b], rowv[:, SC2], ALU.mult).then_inc(gain, 1)
                    pool.wait_ge(gain, 2 * n + 2)
                    G.tensor_tensor(h2[:, b], h2[:, b], rowv[:, SH2], ALU.add).then_inc(h2_made, 1)
                    pool.sem_inc(affine, 1)
                    pool.wait_ge(h2_made, n + 1)
                    pool.sem_inc(pool_carrier, 1)
                    pool.dma_start(h2T[ds(n * P, P), :], h2[:, b]).then_inc(h2_out[b], 16)

                tiles(pool, tile)
                for b in range(2):
                    pool.wait_ge(x1_out[b], 16 * LCHUNK // 2)
                    pool.wait_ge(h2_out[b], 16 * LCHUNK // 2)


def expert_stage(s, affT, h2T, moe):
    nc = s.nc
    V = nc.vector
    ROUNDS = CAP // 8
    RAW, SPLIT = 8, 4
    UP_TILES, DOWN_TILES = KT, FF * D // (P * 2048)
    TILES = UP_TILES + DOWN_TILES
    AHEAD = 3
    DKT = FF // P
    PAIRS = EXPERTS // 2 - 1
    with ExitStack() as st:
        ident = own(st, nc, "e_ident", [P, P])
        aff = own(st, nc, "e_aff", [EXPERTS, SEQ])
        best = own(st, nc, "e_best", [EXPERTS, CAP])
        where = own(st, nc, "e_where", [EXPERTS, CAP], U32)
        wheref = own(st, nc, "e_wheref", [EXPERTS, CAP])
        gate = own(st, nc, "e_gate", [P, EXPERTS])
        token = own(st, nc, "e_token", [P, EXPERTS], U32)
        gatec = own(st, nc, "e_gatec", [P, 1])
        gather_rows, scatter_rows = own(st, nc, "e_gather_rows", [P, 2], U32), own(st, nc, "e_scatter_rows", [P, 1], U32)
        zeros = own(st, nc, "e_zeros", [P, D])
        w = own(st, nc, "e_w", [P, RAW, 2048])
        whi, wlo = own(st, nc, "e_whi", [P, SPLIT, 2048], F32R), own(st, nc, "e_wlo", [P, SPLIT, 2048], F32R)
        rows = own(st, nc, "e_rows", [P, 2, D])
        xhi, xlo = own(st, nc, "e_xhi", [P, 2, KT, P], F32R), own(st, nc, "e_xlo", [P, 2, KT, P], F32R)
        ahi, alo = own(st, nc, "e_ahi", [P, DKT, P], F32R), own(st, nc, "e_alo", [P, DKT, P], F32R)
        g, a = own(st, nc, "e_g", [P, FF]), own(st, nc, "e_a", [P, FF])
        y = own(st, nc, "e_y", [P, 2, D])
        gu = bank(st, nc, "e_gu", [P, 2 * FF])
        tp = bank(st, nc, "e_tp", [P, KT, P])
        down = bank(st, nc, "e_down", [P, D])
        const_in, round_step, listed = s.sem("e_const_in"), s.sem("e_round_step"), s.sem("e_listed")
        lists_turned, picked = s.sem("e_lists_turned"), s.sem("e_picked")
        zeros_made, zeros_out = s.sem("e_zeros_made"), s.sem("e_zeros_out")
        w_in = [s.sem(f"e_w_in{j}") for j in range(RAW)]
        w_hi, w_split, w_used = s.sem("e_w_hi"), s.sem("e_w_split"), s.sem("e_w_used")
        gather_listed, scatter_listed, gate_listed = s.sem("e_gather_listed"), s.sem("e_scatter_listed"), s.sem("e_gate_listed")
        rows_in = [s.sem(f"e_rows_in{b}") for b in range(2)]
        y_out, scattered, carrier = s.sem("e_y_out"), s.sem("e_scattered"), s.sem("e_carrier")
        x_turned, x_hi, x_split = s.sem("e_x_turned"), s.sem("e_x_hi"), s.sem("e_x_split")
        silu_made, a_made, a_turned, a_hi, a_split, y_made = (s.sem(f"e_{n}") for n in (
            "silu_made", "a_made", "a_turned", "a_hi", "a_split", "y_made"))
        up_v = s.x["w_gate_up"][0].rearrange("e d f -> (e d) f")
        down_v = s.x["w_down"][0].rearrange("e f d -> (e f) d")

        def cut(start, size):
            return slice(start, start + size) if isinstance(start, int) else ds(start, size)

        def tile_at(at, t):
            i, c = at
            return 2 * TILES * i + (c + t), (c + t) % RAW, 2 * TILES // RAW * i + (c + t) // RAW

        def experts(eng, step):
            with eng.Fori(0, PAIRS) as i:
                step(2 * i + 1, 1, (i, UP_TILES))
                step(2 * i + 2, 0, (i, UP_TILES + TILES))
            step(EXPERTS - 1, 1, (PAIRS, UP_TILES))

        LAST_DOWN = (PAIRS, UP_TILES + TILES)

        with nc.Block() as block:

            @block.sync
            def _(sp):
                sp.dma_start(aff[:], affT).then_inc(const_in, 16)
                sp.dma_start(ident[:], s.squares[:, 0:P]).then_inc(const_in, 16)

                def load_up(e, at):
                    for t in range(UP_TILES):
                        n, slot, _ = tile_at(at, t)
                        sp.wait_ge(w_split, n + 1)
                        sp.dma_start(w[:, slot], up_v[cut(e * D + t * P, P), :]).then_inc(w_in[slot], 16)

                def load_down(e, at):
                    for j in range(DOWN_TILES):
                        n, slot, _ = tile_at(at, j)
                        sp.wait_ge(w_split, n + 1)
                        sp.dma_start(w[:, slot].rearrange("p (k n) -> p k n", k=2),
                                     down_v[cut(e * FF + 2 * j * P, 2 * P), :].rearrange("(k p) n -> p k n", p=P)).then_inc(w_in[slot], 16)

                def step(e, b, at):
                    load_up(e, at)
                    load_down(e - 1, (at[0], at[1] + UP_TILES))

                load_up(0, (0, 0))
                experts(sp, step)
                load_down(EXPERTS - 1, LAST_DOWN)

            @block.scalar
            def _(act):
                def w_tile(at, t):
                    n, slot, turn = tile_at(at, t)
                    act.wait_ge(w_in[slot], 16 * turn + 16)
                    act.wait_ge(w_used, n + 1)
                    nc.scalar.copy(whi[:, slot % SPLIT], w[:, slot]).then_inc(w_hi, 1)

                def x_parts(e, b):
                    act.wait_ge(x_turned, e + 3)
                    nc.scalar.copy(xhi[:, b], tp[:]).then_inc(x_hi, 1)

                def a_parts(e):
                    act.wait_ge(a_turned, e + 1)
                    nc.scalar.copy(ahi[:], tp[:]).then_inc(a_hi, 1)

                def activate(e, at):
                    act.wait_ge(w_used, tile_at(at, UP_TILES)[0] + SPLIT)
                    nc.scalar.activation(g[:], gu[:, 0:FF], ACT.Silu).then_inc(silu_made, 1)

                def step(e, b, at):
                    for t in range(AHEAD, UP_TILES + AHEAD):
                        w_tile(at, t)
                    activate(e, at)
                    last = isinstance(e, int)
                    if not last:
                        x_parts(e + 1, 1 - b)
                    w_tile(at, UP_TILES + AHEAD)
                    for t in range(AHEAD):
                        w_tile(at, TILES + t)
                    a_parts(e)

                w_tile((0, 0), 0)
                w_tile((0, 0), 1)
                x_parts(0, 0)
                for t in range(2, UP_TILES):
                    w_tile((0, 0), t)
                activate(0, (0, 0))
                x_parts(1, 1)
                for t in range(AHEAD):
                    w_tile((0, UP_TILES), t)
                a_parts(0)
                experts(act, step)
                w_tile(LAST_DOWN, AHEAD)

            @block.vector
            def _(dve):
                dve.sem_inc(w_split, RAW)
                dve.sem_inc(y_made, 1)
                V.memset(zeros[:], 0.0).then_inc(zeros_made, 1)

                def w_tile(at, t):
                    n, slot, _ = tile_at(at, t)
                    dve.wait_ge(w_hi, n + 1)
                    V.tensor_tensor(wlo[:, slot % SPLIT], w[:, slot], whi[:, slot % SPLIT].bitcast(F32), ALU.subtract).then_inc(w_split, 1)

                def x_parts(e, b):
                    dve.wait_ge(x_hi, e + 1)
                    V.tensor_tensor(xlo[:, b], tp[:], xhi[:, b].bitcast(F32), ALU.subtract).then_inc(x_split, 1)

                def a_parts(e):
                    dve.wait_ge(a_hi, e + 1)
                    V.tensor_tensor(alo[:], tp[:], ahi[:].bitcast(F32), ALU.subtract).then_inc(a_split, 1)

                def multiply(e):
                    dve.wait_ge(silu_made, e + 1)
                    V.tensor_tensor(a[:], g[:], gu[:, FF:2 * FF], ALU.mult).then_inc(a_made, 1)

                def finish(e, b, need):
                    dve.wait_ge(y_made, e + 1)
                    V.tensor_copy(gatec[:], gate[:, cut(e, 1)]).then_inc(gate_listed, 1)
                    dve.wait_ge(gate_listed, e + 1)
                    dve.wait_ge(w_used, need)
                    dve.wait_ge(scattered, e + 1)
                    V.tensor_scalar(y[:, b], down[:], gatec[:, 0:1], None, ALU.mult).then_inc(y_made, 1)

                dve.wait_ge(const_in, 32)
                for r in range(ROUNDS):
                    found = slice(8 * r, 8 * r + 8)
                    V.max(best[:, found], aff[:]).then_inc(round_step, 1)
                    dve.wait_ge(round_step, 3 * r + 1)
                    V.max_index(where[:, found], best[:, found], aff[:]).then_inc(round_step, 1)
                    dve.wait_ge(round_step, 3 * r + 2)
                    V.match_replace(aff[:], best[:, found], aff[:], -1.0).then_inc(round_step, 1)
                    dve.wait_ge(round_step, 3 * r + 3)
                V.tensor_copy(wheref[:], where[:]).then_inc(listed, 1)
                dve.wait_ge(lists_turned, 1)
                V.tensor_copy(gate[:], tp[:, 0, 0:EXPERTS])
                V.tensor_copy(token[:], tp[:, 0, EXPERTS:2 * EXPERTS]).then_inc(picked, 1)
                w_tile((0, 0), 0)
                w_tile((0, 0), 1)
                x_parts(0, 0)
                for t in range(2, UP_TILES):
                    w_tile((0, 0), t)
                multiply(0)
                x_parts(1, 1)
                for t in range(AHEAD):
                    w_tile((0, UP_TILES), t)
                a_parts(0)
                dve.wait_ge(picked, 1)

                def step(e, b, at):
                    for t in range(AHEAD, UP_TILES + AHEAD):
                        w_tile(at, t)
                    multiply(e)
                    last = isinstance(e, int)
                    if not last:
                        x_parts(e + 1, 1 - b)
                    w_tile(at, UP_TILES + AHEAD)
                    for t in range(AHEAD):
                        w_tile(at, TILES + t)
                    a_parts(e)
                    finish(e - 1, 1 - b, tile_at(at, TILES)[0] + SPLIT)

                experts(dve, step)
                w_tile(LAST_DOWN, AHEAD)
                finish(EXPERTS - 1, 1, EXPERTS * TILES + SPLIT)

            @block.tensor
            def _(pe):
                pe.sem_inc(w_used, SPLIT)
                pe.sem_inc(x_turned, 2)
                pe.wait_ge(const_in, 32)
                pe.wait_ge(listed, 1)
                nc.tensor.transpose(tp[:, 0, 0:EXPERTS], best[:], ident[0:EXPERTS, 0:EXPERTS])
                nc.tensor.transpose(tp[:, 0, EXPERTS:2 * EXPERTS], wheref[:], ident[0:EXPERTS, 0:EXPERTS]).then_inc(lists_turned, 1)

                def turn_x(b, need):
                    pe.wait_ge(rows_in[b], need)
                    for k in range(KT):
                        mm = nc.tensor.transpose(tp[:, k, :], rows[:, b, k * P:k * P + P], ident[:])
                    mm.then_inc(x_turned, 1)

                def turn_a(e):
                    pe.wait_ge(a_made, e + 1)
                    if not (isinstance(e, int) and e == EXPERTS - 1):
                        pe.wait_ge(x_split, e + 2)
                    for k in range(DKT):
                        mm = nc.tensor.transpose(tp[:, k, :], a[:, k * P:k * P + P], ident[:])
                    mm.then_inc(a_turned, 1)

                def gate_up(e, b, at):
                    pe.wait_ge(x_split, e + 1)
                    for k in range(UP_TILES):
                        n, slot, _ = tile_at(at, k)
                        pe.wait_ge(w_split, n + (1 + RAW))
                        for n_pass, (part, weights) in enumerate(((xhi, whi), (xhi, wlo), (xlo, whi))):
                            for c in range(4):
                                mm = nc.tensor.matmul(gu[:, 512 * c:512 * c + 512], part[:, b, k, :],
                                                      weights[:, slot % SPLIT, 512 * c:512 * c + 512],
                                                      start=(k == 0 and n_pass == 0), stop=(k == KT - 1 and n_pass == 2))
                        mm.then_inc(w_used, 1)

                def project_down(at):
                    for j in range(DOWN_TILES):
                        n, slot, _ = tile_at(at, j)
                        pe.wait_ge(w_split, n + (1 + RAW))
                        for half in range(2):
                            k = 2 * j + half
                            for n_pass, (part, weights) in enumerate(((ahi, whi), (ahi, wlo), (alo, whi))):
                                for c in range(2):
                                    col = D * half + 512 * c
                                    mm = nc.tensor.matmul(down[:, 512 * c:512 * c + 512], part[:, k, :],
                                                          weights[:, slot % SPLIT, col:col + 512],
                                                          start=(k == 0 and n_pass == 0), stop=(k == DKT - 1 and n_pass == 2))
                        mm.then_inc(w_used, 1)

                def step(e, b, at):
                    pe.wait_ge(a_made, e)
                    gate_up(e, b, at)
                    pe.wait_ge(a_split, e)
                    if not isinstance(e, int):
                        turn_x(1 - b, 16 * at[0] + 32)
                    pe.wait_ge(y_made, e)
                    project_down((at[0], at[1] + UP_TILES))
                    turn_a(e)

                pe.wait_ge(picked, 1)
                turn_x(0, 16)
                gate_up(0, 0, (0, 0))
                turn_x(1, 16)
                turn_a(0)
                experts(pe, step)
                pe.wait_ge(a_split, EXPERTS)
                pe.wait_ge(y_made, EXPERTS)
                project_down(LAST_DOWN)

            @block.gpsimd
            def _(pool):
                pool.sem_inc(scattered, 2)
                pool.wait_ge(zeros_made, 1)
                for t in range(SEQ // P):
                    pool.dma_start(moe[t * P:t * P + P, :], zeros[:]).then_inc(zeros_out, 16)
                pool.wait_ge(picked, 1)

                def gather(e, b):
                    pool.wait_ge(x_turned, e + 1)
                    nc.gpsimd.tensor_copy(gather_rows[:, b:b + 1], token[:, cut(e, 1)]).then_inc(gather_listed, 1)
                    pool.wait_ge(gather_listed, e + 1)
                    pool.sem_inc(carrier, 1)
                    pool.indirect_dma_start(rows[:, b], None, h2T, bass.IndirectOffsetOnAxis(ap=gather_rows[:, b:b + 1], axis=0)).then_inc(rows_in[b], 16)

                def scatter(e, b):
                    nc.gpsimd.tensor_copy(scatter_rows[:], token[:, cut(e, 1)]).then_inc(scatter_listed, 1)
                    pool.wait_ge(scatter_listed, e + 1)
                    pool.wait_ge(y_made, e + 2)
                    pool.sem_inc(carrier, 1)
                    pool.indirect_dma_start(moe, bass.IndirectOffsetOnAxis(ap=scatter_rows[:, 0:1], axis=0), y[:, b], None,
                                            compute_op=ALU.add).then_inc(y_out, 16)
                    pool.wait_ge(y_out, 16 * e + 16)
                    pool.sem_inc(scattered, 1)

                gather(0, 0)
                gather(1, 1)
                pool.wait_ge(zeros_out, 16 * (SEQ // P))
                with pool.Fori(0, PAIRS) as i:
                    for b in range(2):
                        gather(2 * i + (2 + b), b)
                        scatter(2 * i + b, b)
                for b in range(2):
                    scatter(EXPERTS - 2 + b, b)


def output_stage(s, mod, x1T, moe):
    nc = s.nc
    V = nc.vector
    G2, LN_G, LN_B = range(3)
    with ExitStack() as st:
        rowv = own(st, nc, "o_rows", [P, 3, D])
        x, m, y = own(st, nc, "o_x", [P, 2, D]), own(st, nc, "o_m", [P, 2, D]), own(st, nc, "o_y", [P, 2, D])
        stats, mv, root = own(st, nc, "o_stats", [P, 2, 6]), own(st, nc, "o_mv", [P, 2]), own(st, nc, "o_root", [P, 2])
        const_in, carrier = s.sem("o_const_in"), s.sem("o_carrier")
        tiles_in = [s.sem(f"o_tiles_in{b}") for b in range(2)]
        y_out = [s.sem(f"o_y_out{b}") for b in range(2)]
        free, step, squared, rooted, normed, gained, made = (s.sem(f"o_{n}") for n in ("free", "step", "squared", "rooted", "normed", "gained", "made"))
        VS = 5

        def tiles(eng, step_):
            with eng.Fori(0, LCHUNK // 2) as i:
                for b in range(2):
                    step_(2 * i + b, b, i)

        with nc.Block() as block:

            @block.sync
            def _(sp):
                for j, row in ((G2, mod[0:1, 5 * D:6 * D]), (LN_G, s.x["ln2_g"]), (LN_B, s.x["ln2_b"])):
                    sp.dma_start(rowv[:, j], row.to_broadcast([P, D])).then_inc(const_in, 16)

                def load(n, b, i):
                    sp.wait_ge(free, n + 1)
                    sp.dma_start(m[:, b], moe[ds(n * P, P), :]).then_inc(tiles_in[b], 16)
                    sp.dma_start(x[:, b], x1T[ds(n * P, P), :]).then_inc(tiles_in[b], 16)

                tiles(sp, load)

            @block.vector
            def _(dve):
                dve.sem_inc(free, 2)
                dve.wait_ge(const_in, 48)

                def tile(n, b, i):
                    at = VS * n

                    def then(ins, k):
                        ins.then_inc(step, 1)
                        dve.wait_ge(step, at + k)

                    dve.wait_ge(tiles_in[b], 32 * i + 32)
                    then(V.tensor_tensor(m[:, b], m[:, b], rowv[:, G2], ALU.mult), 1)
                    then(V.scalar_tensor_tensor(x[:, b], x[:, b], ALPHA, m[:, b], ALU.mult, ALU.add), 2)
                    V.bn_stats(stats[:, 0, :], x[:, b, 0:512])
                    then(V.bn_stats(stats[:, 1, :], x[:, b, 512:1024]), 3)
                    dve.sem_inc(carrier, 1)
                    then(V.bn_aggr(mv[:], stats[:]), 4)
                    then(V.tensor_scalar(root[:, 1:2], mv[:, 1:2], EPS, None, ALU.add), 5)
                    V.reciprocal(root[:, 0:1], root[:, 1:2]).then_inc(squared, 1)
                    dve.wait_ge(rooted, n + 1)
                    dve.wait_ge(y_out[b], 16 * i)
                    V.tensor_scalar(y[:, b], x[:, b], mv[:, 0:1], root[:, 1:2], ALU.subtract, ALU.mult).then_inc(normed, 1)
                    dve.wait_ge(normed, n + 1)
                    V.sem_inc(free, 1)
                    V.tensor_tensor(y[:, b], y[:, b], rowv[:, LN_G], ALU.mult).then_inc(gained, 1)

                tiles(dve, tile)

            @block.scalar
            def _(act):
                def tile(n, b, i):
                    act.wait_ge(squared, n + 1)
                    nc.scalar.activation(root[:, 1:2], root[:, 0:1], ACT.Sqrt).then_inc(rooted, 1)

                tiles(act, tile)

            @block.gpsimd
            def _(pool):
                def tile(n, b, i):
                    pool.wait_ge(gained, n + 1)
                    nc.gpsimd.tensor_tensor(y[:, b], y[:, b], rowv[:, LN_B], ALU.add).then_inc(made, 1)
                    pool.wait_ge(made, n + 1)
                    pool.dma_start(s.out[0, ds(n * P, P), :], y[:, b]).then_inc(y_out[b], 16)

                tiles(pool, tile)
                for b in range(2):
                    pool.wait_ge(y_out[b], 16 * LCHUNK // 2)


def program(nc, inputs, out, constants):
    with ExitStack() as ctx:
        s = Stage(nc, inputs, out, ctx)
        s.squares, s.cosine, s.sine, s.masks, s.edges, s.lanes = (constants[n] for n in ("squares", "cosine", "sine", "masks", "edges", "lanes"))
        mod = s.scratch("mod", [2, 6 * D])
        xbcF, xbcT = s.scratch("xbcF", [CONV_CH, TOK]), s.scratch("xbcT", [TOK, CONV_CH])
        qkF, gF = s.scratch("qkF", [(QH + KVH) * HD, KV_TOK]), s.scratch("gF", [2 * D, SEQ])
        zT, vT = s.scratch("zT", [SEQ, D_INNER]), s.scratch("vT", [KV_TOK, KVH * HD])
        dtT = s.scratch("dtT", [TOK, 2 * HEADS])
        tabs, cumrow = s.scratch("tabs", [NCHUNK, P, 5 * 2 * HEADS]), s.scratch("cumrow", [LCHUNK, 2, 2 * HEADS, P])
        before = s.scratch("before", [2, LCHUNK, STATE, D_INNER])
        yT = s.scratch("yT", [SEQ, D_INNER])
        aF = s.scratch("aF", [QH * HD, SEQ])
        mF, x1T, h2T = s.scratch("mF", [D, SEQ]), s.scratch("x1T", [SEQ, D]), s.scratch("h2T", [SEQ, D])
        affT = s.scratch("affT", [EXPERTS, SEQ])
        moe = s.scratch("moe", [SEQ, D])
        adaln_stage(s, mod)
        with ExitStack() as st:
            hi, lo = own(st, nc, "h_hi", [P, KT, TOK], F32R), own(st, nc, "h_lo", [P, KT, TOK], F32R)
            norm_stage(s, mod, hi, lo)
            project_f_stage(s, hi, lo, xbcF, xbcT, qkF, gF)
            project_t_stage(s, hi, lo, zT, vT, dtT)
        decay_stage(s, dtT, tabs, cumrow)
        states_stage(s, xbcT, tabs, before)
        scan_output_stage(s, xbcT, xbcF, zT, tabs, cumrow, before, yT)
        attention_stage(s, qkF, vT, aF)
        s.recycle()
        branch_stage(s, yT, aF, gF, mF)
        residual_stage(s, mod, mF, x1T, h2T, affT)
        expert_stage(s, affT, h2T, moe)
        output_stage(s, mod, x1T, moe)


NAMES = ["x", "c", "ctx", "c_ctx", "w_ada", "b_ada", "w_in", "conv_w", "conv_b", "a_log", "dt_bias", "d_skip",
         "ssd_norm_w", "attn_sink", "w_ssd_br", "w_attn_br", "w_o", "b_o", "ln1_g", "ln1_b",
         "w_router", "w_gate_up", "w_down", "ln2_g", "ln2_b"]


def kernel(**inputs):
    from concourse import bacc
    from concourse.bass_utils import run_bass_kernel_spmd

    nc = bacc.Bacc("TRN2", target_bir_lowering=False, num_devices=1)
    arrays, tensors = {}, {}
    for name in NAMES:
        a = np.ascontiguousarray(inputs[name])
        arrays[f"in_{name}"] = a
        tensors[name] = nc.dram_tensor(f"in_{name}", a.shape, mybir.dt.from_np(a.dtype), kind="ExternalInput").ap()
    nx = CONV_CH // P
    taps = np.concatenate([np.asarray(inputs["conv_w"])[0], np.asarray(inputs["conv_b"])], 0)
    taps = np.ascontiguousarray(taps.reshape(CONV_W + 1, nx, P).transpose(2, 1, 0))
    arrays["in_taps"] = taps
    tensors["taps"] = nc.dram_tensor("in_taps", taps.shape, F32, kind="ExternalInput").ap()
    normw = np.ascontiguousarray(np.asarray(inputs["ssd_norm_w"]).reshape(D_INNER // P, P).T)
    arrays["in_normw"] = normw
    tensors["normw"] = nc.dram_tensor("in_normw", normw.shape, F32, kind="ExternalInput").ap()
    constants = {n: nc.inline_tensor(v, f"const_{n}").ap() for n, v in shape_constants().items()}
    out = nc.dram_tensor("out", (1, SEQ, D), F32, kind="ExternalOutput").ap()
    program(nc, tensors, out, constants)
    r = run_bass_kernel_spmd(nc, [arrays], core_ids=[0])
    return r.results[0]["out"]
```

```python
from contextlib import ExitStack

import numpy as np
import concourse.bass as bass
from concourse import mybir

ALU = mybir.AluOpType
ACT = mybir.ActivationFunctionType
AX_X = mybir.AxisListType.X
F32 = mybir.dt.float32
F32R = mybir.dt.float32r
U32 = mybir.dt.uint32
ds = bass.ds

P = 128
D = 1024
KT = D // P
SEQ = 1024
CTX = 256
TOK = CTX + SEQ
NCHUNK = TOK // P
CCHUNK = CTX // P
LCHUNK = SEQ // P
D_INNER = 2048
GROUPS = 4
STATE = 128
CONV_W = 5
CONV_CH = D_INNER + 2 * GROUPS * STATE
HEADS = 32
HPG = HEADS // GROUPS
PDIM = 64
QH = 16
KVH = 4
HD = 64
GRID_W = 64
WINDOW = 128
FF = 1024
EXPERTS = 16
CAP = 2 * SEQ // EXPERTS
EPS = 1e-5
ALPHA = 2.0 ** 0.25
SCALE = HD ** -0.5
NEG = -1e30

Z0 = 0
XBC0 = Z0 + D_INNER
DT0 = XBC0 + CONV_CH
Q0 = DT0 + 2 * HEADS
K0 = Q0 + QH * HD
V0 = K0 + KVH * HD
G0 = V0 + KVH * HD

BLANK = WINDOW
KV_LAT0 = CTX + BLANK
KV_TOK = KV_LAT0 + SEQ + BLANK


def shape_constants():
    i = np.arange(P)
    upper = (i[:, None] <= i[None, :]).astype(np.float32)
    inv = 10000.0 ** (-np.arange(0, HD // 2, 2, dtype=np.float32) / (HD // 2))
    t = np.arange(SEQ)
    row = (t // GRID_W).astype(np.float32)[:, None] * inv[None, :]
    col = (t % GRID_W).astype(np.float32)[:, None] * inv[None, :]
    ang = np.concatenate([row, row, col, col], -1).astype(np.float32).T
    ang = np.concatenate([ang, ang], 0)
    rotate = np.zeros((P, P), np.float32)
    for m in range(P):
        quarter = (m % HD) // (HD // 4)
        rotate[m + 16 if quarter % 2 == 0 else m - 16, m] = -1.0 if quarter % 2 == 0 else 1.0
    q, k = i[:, None], np.arange(3 * P)[None, :]
    near = np.abs(k - P - q) <= WINDOW
    masks = np.zeros((LCHUNK, P, CTX + 3 * P), np.float32)
    for b in range(LCHUNK):
        pos = b * P - WINDOW + k
        masks[b, :, CTX:] = np.where(near & (pos >= 0) & (pos < SEQ), 0.0, NEG)
    edges = np.stack([masks[:, :, CTX:CTX + P].transpose(0, 2, 1), masks[:, :, CTX + 2 * P:].transpose(0, 2, 1)], 2)
    return {
        "lanes": np.ascontiguousarray(np.tile(-np.eye(4, dtype=np.float32)[:, :, None], (2, 4, P))).reshape(8, 16 * P),
        "edges": np.ascontiguousarray(edges).reshape(LCHUNK, P, 2 * P),
        "squares": np.concatenate([np.eye(P, dtype=np.float32), upper, upper.T, np.ones((P, P), np.float32), rotate,
                                   np.eye(P, dtype=np.float32)[::-1]], 1),
        "cosine": np.cos(ang).astype(np.float32),
        "sine": np.sin(ang).astype(np.float32),
        "masks": masks,
    }


class Stage:

    def __init__(self, nc, inputs, out, ctx):
        self.nc, self.x, self.out, self.ctx = nc, inputs, out, ctx
        self.sems = []
        self.credits, self.credit_lines = 0, self.scratch("credit_lines", [P, P])

    def sem(self, name):
        self.sems.append(self.nc.alloc_semaphore(name=name))
        return self.sems[-1]

    def recycle(self):
        self.nc.clear_and_free_semaphores(self.sems)
        self.nc.all_engine_barrier()
        self.sems = []

    def credit(self, pool, sems):
        for sem in sems:
            line = self.credits
            self.credits += 1
            pool.dma_start(self.credit_lines[line:line + 1, :], self.squares[line:line + 1, 0:P]).then_inc(sem, 16)

    def scratch(self, name, shape):
        return self.nc.dram_tensor(name, shape, F32).ap()


def own(stack, nc, name, shape, dtype=F32):
    return stack.enter_context(nc.sbuf_tensor(name, shape, dtype))


def bank(stack, nc, name, shape, dtype=F32):
    return stack.enter_context(nc.psum_tensor(name, shape, dtype))


def adaln_stage(s, mod):
    nc = s.nc
    NB = 2 * D // 512
    with ExitStack() as st:
        cond = own(st, nc, "cond", [P, 2, KT])
        act_c = own(st, nc, "act_c", [P, 2, KT])
        w = own(st, nc, "w_ada_t", [P, 2, KT, 512])
        bias = own(st, nc, "b_ada_t", [2, 2 * D])
        row = own(st, nc, "mod_row", [2, 2 * D])
        acc = bank(st, nc, "mod_acc", [P, 2, 512])
        cond_in, bias_in, silu_done = s.sem("cond_in"), s.sem("bias_in"), s.sem("cond_silu")
        w_in = [s.sem(f"ada_w_in{b}") for b in range(2)]
        w_free, acc_free = s.sem("ada_w_free"), s.sem("mod_acc_free")
        stored = s.sem("mod_stored")
        wv = s.x["w_ada"][0].rearrange("(p k) n -> p k n", k=KT)
        with nc.Block() as block:

            @block.sync
            def _(sp):
                sp.dma_start(cond[:, 0, :], s.x["c"][0].rearrange("(p k) -> p k", k=KT)).then_inc(cond_in, 16)
                sp.dma_start(cond[:, 1, :], s.x["c_ctx"].rearrange("(p k) -> p k", k=KT)).then_inc(cond_in, 16)
                for r in range(2):
                    sp.dma_start(bias[r:r + 1, :], s.x["b_ada"][:, 0:2 * D]).then_inc(bias_in, 16)
                with sp.Fori(0, NB // 2) as i:
                    for b in range(2):
                        sp.wait_ge(w_free, 2 * i + b + 1)
                        sp.dma_start(w[:, b], wv[:, :, ds(1024 * i + 512 * b, 512)]).then_inc(w_in[b], 16)

            @block.scalar
            def _(act):
                act.wait_ge(cond_in, 32)
                nc.scalar.activation(act_c[:], cond[:], ACT.Silu).then_inc(silu_done, 1)

            @block.tensor
            def _(pe):
                pe.sem_inc(w_free, 2)
                pe.wait_ge(silu_done, 1)
                with pe.Fori(0, NB // 2) as i:
                    for b in range(2):
                        pe.wait_ge(w_in[b], 16 * i + 16)
                        pe.wait_ge(acc_free, 2 * i + b + 1)
                        for k in range(KT):
                            mm = nc.tensor.matmul(acc[0:2, b, :], act_c[:, :, k], w[:, b, k, :],
                                                  start=(k == 0), stop=(k == KT - 1))
                        mm.then_inc(w_free, 1)

            @block.vector
            def _(dve):
                dve.sem_inc(acc_free, 2)
                dve.wait_ge(bias_in, 32)
                with dve.Fori(0, NB // 2) as i:
                    for b in range(2):
                        dve.wait_ge(w_free, 2 * i + b + 3)
                        nc.vector.tensor_tensor(row[:, ds(1024 * i + 512 * b, 512)], acc[0:2, b, :],
                                                bias[:, ds(1024 * i + 512 * b, 512)], ALU.add).then_inc(acc_free, 1)

            @block.gpsimd
            def _(pool):
                pool.wait_ge(acc_free, NB + 2)
                pool.dma_start(mod[:, 0:2 * D], row[:]).then_inc(stored, 16)
                pool.wait_ge(stored, 16)


def norm_stage(s, mod, hi, lo):
    nc = s.nc
    DONE = 2 * D
    with ExitStack() as st:
        ident = own(st, nc, "ident1", [P, P])
        colm = own(st, nc, "mod_cols", [P, 4, KT])
        x = own(st, nc, "x_in", [P, 2, D])
        xn = own(st, nc, "x_norm", [P, 2, D])
        stats = own(st, nc, "ln_stats", [P, 2, 6])
        mv = own(st, nc, "ln_mv", [P, 2])
        rstd = own(st, nc, "ln_rstd", [P, 2])
        carrier = s.sem("ln_carrier")
        h = own(st, nc, "h_full", [P, 2, KT, P])
        tp = bank(st, nc, "ln_tp", [P, 2, KT, P])
        cond, act_c = own(st, nc, "cond2", [P, 2, KT]), own(st, nc, "act_c2", [P, 2, KT])
        w = own(st, nc, "w_ada2", [P, 2, KT, 512])
        bias, ones = own(st, nc, "b_ada2", [1, 2, 512]), own(st, nc, "ones2", [1, 2])
        modrows = own(st, nc, "mod_rows", [4 * KT, P])
        row = own(st, nc, "mod_row2", [2, 2, 512])
        acc = bank(st, nc, "mod_acc2", [P, 2, 512])
        cols_ps = bank(st, nc, "mod_cols_ps", [P, 512])
        cond_in, silu_done, ones_made = s.sem("cond2_in"), s.sem("cond2_silu"), s.sem("ones2_made")
        ada_in = [s.sem(f"ada2_w_in{b}") for b in range(2)]
        ada_used, ada_kept, cols_turned = s.sem("ada2_used"), s.sem("ada2_kept"), s.sem("mod_cols_turned")
        ada_out, ada_read = s.sem("ada2_out"), s.sem("ada2_read")
        wv = s.x["w_ada"][0].rearrange("(p k) n -> p k n", k=KT)
        ident_in, cols_in = s.sem("ident1_in"), s.sem("mod_cols_in")
        x_in = [s.sem(f"x_in{b}") for b in range(2)]
        x_free, turned = s.sem("x_free"), s.sem("x_turned")
        var_ready, root_ready, chain = s.sem("ln_var"), s.sem("ln_root"), s.sem("ln_chain")
        hi_ready = s.sem("h_hi_ready")
        chain2 = s.sem("ln_chain2")
        STEPS, STEPS2 = 5, 3

        def staggered(eng, first, second):
            def pair(n, b, turn, m):
                first(n + 1, 1 - b, turn)
                second(n, b, m)

            first(0, 0, 0)
            pair(0, 0, 0, 0)
            pair(1, 1, 1, 0)
            with eng.Fori(0, LCHUNK // 2 - 1) as i:
                pair(2 * i + 2, 0, i + 1, 2)
                pair(2 * i + 3, 1, i + 2, 2)
            pair(NCHUNK - 2, 0, NCHUNK // 2 - 1, 2)
            second(NCHUNK - 1, 1, 2)

        with nc.Block() as block:

            @block.sync
            def _(sp):
                sp.dma_start(ident[:], s.squares[:, 0:P]).then_inc(ident_in, 16)
                for j, (r, part) in enumerate([(1, 0), (1, 1), (0, 0), (0, 1)]):
                    sp.dma_start(modrows[KT * j:KT * j + KT, :],
                                 mod[r:r + 1, part * D:part * D + D].rearrange("o (k p) -> (o k) p", p=P)).then_inc(cols_in, 16)

                def load(src, t, b, n):
                    sp.wait_ge(x_free, n + 1)
                    sp.dma_start(x[:, b], src).then_inc(x_in[b], 16)

                for t in range(CCHUNK):
                    load(s.x["ctx"][0, t * P:t * P + P, :], t, t % 2, t)
                sp.dma_start(cond[:, 0, :], s.x["c"][0].rearrange("(p k) -> p k", k=KT)).then_inc(cond_in, 16)
                sp.dma_start(cond[:, 1, :], s.x["c_ctx"].rearrange("(p k) -> p k", k=KT)).then_inc(cond_in, 16)
                with sp.Fori(0, LCHUNK // 2) as i:
                    for b in range(2):
                        load(s.x["x"][0, ds((2 * i + b) * P, P), :], None, b, 2 * i + b + CCHUNK)
                        sp.wait_ge(ada_used, 2 * i + b + 1)
                        sp.dma_start(w[:, b], wv[:, :, ds(1024 * i + (DONE + 512 * b), 512)]).then_inc(ada_in[b], 16)
                        sp.dma_start(bias[:, b], s.x["b_ada"][:, ds(1024 * i + (DONE + 512 * b), 512)]).then_inc(ada_in[b], 16)

            @block.vector
            def _(dve):
                dve.sem_inc(x_free, 2)
                dve.memset(ones[:], 1.0).then_inc(ones_made, 1)
                dve.wait_ge(cols_turned, 1)
                turned_cols = cols_ps[:, 0:4 * KT].rearrange("p (j k) -> p j k", k=KT)
                dve.tensor_scalar(colm[:, 1::2, :], turned_cols[:, 1::2, :], 1.0, None, ALU.add).then_inc(chain, 1)
                dve.tensor_copy(colm[:, 0::2, :], turned_cols[:, 0::2, :]).then_inc(chain, 1)

                def normalise(n, b, turn):
                    at = 2 + STEPS * n

                    def then(ins, k):
                        ins.then_inc(chain, 1)
                        dve.wait_ge(chain, at + k)

                    dve.wait_ge(x_in[b], 16 * turn + 16)
                    nc.vector.bn_stats(stats[:, 0, :], x[:, b, 0:512]).then_inc(chain, 1)
                    then(nc.vector.bn_stats(stats[:, 1, :], x[:, b, 512:1024]), 2)
                    dve.sem_inc(carrier, 1)
                    then(nc.vector.bn_aggr(mv[:], stats[:]), 3)
                    then(nc.vector.tensor_scalar(rstd[:, 0:1], mv[:, 1:2], EPS, None, ALU.add), 4)
                    then(nc.vector.reciprocal(rstd[:, 1:2], rstd[:, 0:1]), 5)
                    nc.vector.tensor_scalar(rstd[:, 0:1], rstd[:, 1:2], 1.0, None, ALU.mult).then_inc(var_ready, 1)
                    dve.wait_ge(root_ready, n + 1)
                    if not isinstance(n, int) or n > 1:
                        dve.wait_ge(turned, n - 1)
                    nc.vector.tensor_scalar(xn[:, b], x[:, b], mv[:, 0:1], rstd[:, 1:2],
                                            ALU.subtract, ALU.mult).then_inc(x_free, 1)
                    dve.wait_ge(x_free, n + 3)

                def modulate(n, b, m):
                    at = STEPS2 * n

                    def then(ins, k):
                        ins.then_inc(chain2, 1)
                        dve.wait_ge(chain2, at + k)

                    dve.wait_ge(turned, n + 1)
                    if isinstance(n, int) and n == 0:
                        dve.wait_ge(chain, 2)
                    then(nc.vector.tensor_tensor(h[:, b], tp[:, b], colm[:, m + 1, :].unsqueeze(2).to_broadcast([P, KT, P]),
                                                 ALU.mult), 1)
                    then(nc.vector.tensor_tensor(h[:, b], h[:, b], colm[:, m, :].unsqueeze(2).to_broadcast([P, KT, P]),
                                                 ALU.add), 2)
                    dve.wait_ge(hi_ready, n + 1)
                    cut = slice(n * P, n * P + P) if isinstance(n, int) else ds(n * P, P)
                    then(nc.vector.tensor_tensor(lo[:, :, cut], h[:, b], hi[:, :, cut].bitcast(F32), ALU.subtract), 3)

                staggered(dve, normalise, modulate)

            @block.scalar
            def _(act):
                def take_root(n, b, turn):
                    act.wait_ge(var_ready, n + 1)
                    nc.scalar.activation(rstd[:, 1:2], rstd[:, 0:1], ACT.Sqrt).then_inc(root_ready, 1)

                def round_off(n, b, m):
                    act.wait_ge(chain2, STEPS2 * n + 2)
                    cut = slice(n * P, n * P + P) if isinstance(n, int) else ds(n * P, P)
                    nc.scalar.copy(hi[:, :, cut], h[:, b]).then_inc(hi_ready, 1)
                    if m:
                        act.wait_ge(ada_used, n + 1)
                        act.wait_ge(ada_read, n - 1)
                        nc.scalar.copy(row[:, b, :], acc[0:2, b, :]).then_inc(ada_kept, 1)

                act.wait_ge(cond_in, 32)
                nc.scalar.activation(act_c[:], cond[:], ACT.Silu).then_inc(silu_done, 1)
                staggered(act, take_root, round_off)

            @block.tensor
            def _(pe):
                pe.sem_inc(ada_used, 2)
                pe.wait_ge(ident_in, 16)
                pe.wait_ge(cols_in, 64)
                nc.tensor.transpose(cols_ps[:, 0:4 * KT], modrows[:], ident[0:4 * KT, 0:4 * KT]).then_inc(cols_turned, 1)

                def more_mod(j, b, i):
                    pe.wait_ge(ada_in[b], 32 * i + 32)
                    pe.wait_ge(ada_kept, j + 1)
                    for k in range(KT):
                        nc.tensor.matmul(acc[0:2, b, :], act_c[:, :, k], w[:, b, k, :], start=(k == 0), stop=False)
                    nc.tensor.matmul(acc[0:2, b, :], ones[:], bias[:, b],
                                     start=False, stop=True).then_inc(ada_used, 1)

                def tile(n, b):
                    pe.wait_ge(x_free, n + 3)
                    for k in range(KT):
                        mm = nc.tensor.transpose(tp[:, b, k, :], xn[:, b, k * P:k * P + P], ident[:])
                    mm.then_inc(turned, 1)

                for t in range(CCHUNK):
                    tile(t, t % 2)
                pe.wait_ge(silu_done, 1)
                pe.wait_ge(ones_made, 1)
                with pe.Fori(0, LCHUNK // 2) as i:
                    for b in range(2):
                        tile(2 * i + b + CCHUNK, b)
                        more_mod(2 * i + b, b, i)

            @block.gpsimd
            def _(pool):
                pool.sem_inc(ada_kept, 2)
                pool.sem_inc(ada_read, 2)
                with pool.Fori(0, LCHUNK // 2) as i:
                    for b in range(2):
                        j = 2 * i + b
                        pool.wait_ge(ada_kept, j + 3)
                        pool.dma_start(mod[:, ds(1024 * i + (DONE + 512 * b), 512)], row[:, b, :]).then_inc(ada_out, 16)
                        pool.wait_ge(ada_out, 16 * j + 16)
                        pool.sem_inc(ada_read, 1)


def project_f_stage(s, hi, lo, xbcF, xbcT, qkF, gF):
    nc = s.nc
    NX, NQK, NG = CONV_CH // P, (QH + KVH) * HD // P, 2 * D // P
    NQ = QH * HD // P
    PAD = 2 + CTX + 4 + SEQ + 2
    W_OUT = PAD - 4
    with ExitStack() as st:
        squares = own(st, nc, "squares", [P, 5, P])
        cos, sin = own(st, nc, "cos", [P, SEQ]), own(st, nc, "sin", [P, SEQ])
        taps = own(st, nc, "conv_taps", [P, NX, CONV_W + 1])
        w = own(st, nc, "w_raw", [P, 2, KT, P])
        whi = own(st, nc, "w_hi", [P, 2, KT, P], F32R)
        wlo = own(st, nc, "w_lo", [P, 2, KT, P], F32R)
        padded = own(st, nc, "conv_in", [P, 2, PAD])
        conv = own(st, nc, "conv_acc", [P, 2, W_OUT])
        wide = own(st, nc, "f_out", [P, 2, TOK])
        zeros = own(st, nc, "f_zeros", [P, BLANK])
        turned = own(st, nc, "t_out", [P, 2, TOK])
        tap = own(st, nc, "conv_tap_cols", [P, 2, CONV_W + 1])
        lat = bank(st, nc, "f_lat", [P, 2, SEQ])
        cxt = bank(st, nc, "f_ctx", [P, 2, 2 * CTX])
        tp = bank(st, nc, "f_tp", [P, SEQ])
        ident, rotate = squares[:, 0, :], squares[:, 4, :]

        tables_in = s.sem("f_tables_in")
        w_in = [s.sem(f"f_w_in{b}") for b in range(2)]
        hi_made, w_free = s.sem("f_hi_made"), s.sem("f_w_free")
        used, acc_free = s.sem("f_w_used"), s.sem("f_acc_free")
        conv_step, wide_made = s.sem("f_conv_step"), s.sem("f_wide_made")
        tp_full, tp_free = s.sem("f_tp_full"), s.sem("f_tp_free")
        ctx_turned = s.sem("f_ctx_turned")
        rot_step = s.sem("f_rot_step")
        wide_out = [s.sem(f"f_wide_out{b}") for b in range(2)]
        turned_out = [s.sem(f"f_turned_out{b}") for b in range(2)]
        zeros_made, blanks_out = s.sem("f_zeros_made"), s.sem("f_blanks_out")
        CS = CONV_W + 1
        wv = s.x["w_in"][0].rearrange("(k p) n -> p k n", p=P)
        NF = NX + NQK + NG

        def pairs(eng, kind, step):
            f0, n = {"xbc": (0, NX), "q": (NX, NQ), "k": (NX + NQ, NQK - NQ), "gate": (NX + NQK, NG - 2)}[kind]
            w0 = NQ if kind == "k" else 0
            with eng.Fori(0, n // 2) as i:
                for b in range(2):
                    step(2 * i + (f0 + b), b, kind, i + f0 // 2, 2 * i + (w0 + b))

        with nc.Block() as block:

            @block.sync
            def _(sp):
                sp.dma_start(squares[:], s.squares.rearrange("p (a q) -> p a q", q=P)[:, 0:5, :]).then_inc(tables_in, 16)
                sp.dma_start(cos[:], s.cosine).then_inc(tables_in, 16)
                sp.dma_start(sin[:], s.sine).then_inc(tables_in, 16)
                sp.dma_start(taps[:], s.x["taps"]).then_inc(tables_in, 16)
                for col, f0, n in ((XBC0, 0, NX), (Q0, NX, NQK), (G0, NX + NQK, NG)):
                    with sp.Fori(0, n // 2) as i:
                        for b in range(2):
                            sp.wait_ge(w_free, 2 * i + (f0 + b + 1))
                            sp.dma_start(w[:, b], wv[:, :, ds(2 * P * i + (col + P * b), P)]).then_inc(w_in[b], 16)

            @block.tensor
            def _(pe):
                pe.sem_inc(used, 2)
                pe.wait_ge(tables_in, 64)

                def product(f, b, ctx, after_turn=False):
                    pe.wait_ge(w_free, f + 3)
                    pe.wait_ge(acc_free, f + 1)
                    if after_turn:
                        pe.wait_ge(ctx_turned, f + 1)
                    outs = [(cxt[:, b, 0:CTX], 0, CTX)] if ctx else []
                    outs += [(lat[:, b, 0:512], CTX, 512), (lat[:, b, 512:1024], CTX + 512, 512)]
                    for k in range(KT):
                        for n_pass, (weights, part) in enumerate(((whi, hi), (whi, lo), (wlo, hi))):
                            for o, a, n in outs:
                                mm = nc.tensor.matmul(o, weights[:, b, k, :], part[:, k, a:a + n],
                                                      start=(k == 0 and n_pass == 0),
                                                      stop=(k == KT - 1 and n_pass == 2))
                    mm.then_inc(used, 1)

                def turn(f, b):
                    pe.wait_ge(wide_made, f + 3)
                    pe.wait_ge(tp_free, f + 1)
                    for c in range(NCHUNK):
                        at = cxt[:, b, CTX + c * P:CTX + c * P + P] if c < CCHUNK else tp[:, (c - CCHUNK) * P:(c - CCHUNK) * P + P]
                        mm = nc.tensor.transpose(at, wide[:, b, c * P:c * P + P], ident)
                    mm.then_inc(tp_full, 1)

                def rotated(f, b):
                    pe.wait_ge(acc_free, f + 3)
                    pe.wait_ge(tp_free, f + 1)
                    for n in range(2):
                        mm = nc.tensor.matmul(tp[:, n * 512:n * 512 + 512], rotate,
                                              wide[:, b, CTX + n * 512:CTX + n * 512 + 512], start=True, stop=True)
                    mm.then_inc(tp_full, 1)

                product(0, 0, True, True)
                product(1, 1, True, True)
                turn(0, 0)
                with pe.Fori(1, NX // 2) as i:
                    product(2 * i, 0, True, True)
                    turn(2 * i - 1, 1)
                    product(2 * i + 1, 1, True, True)
                    turn(2 * i, 0)
                product(NX, 0, False)
                turn(NX - 1, 1)
                product(NX + 1, 1, False)
                rotated(NX, 0)
                with pe.Fori(1, NQ // 2) as i:
                    product(2 * i + NX, 0, False)
                    rotated(2 * i + (NX - 1), 1)
                    product(2 * i + (NX + 1), 1, False)
                    rotated(2 * i + NX, 0)
                for f in range(NX + NQ, NX + NQK, 2):
                    product(f, 0, True)
                    rotated(f - 1, 1)
                    product(f + 1, 1, True)
                    rotated(f, 0)
                product(NX + NQK, 0, False)
                rotated(NX + NQK - 1, 1)
                product(NX + NQK + 1, 1, False)
                with pe.Fori(1, NG // 2) as i:
                    for b in range(2):
                        product(2 * i + (NX + NQK + b), b, False)

            @block.scalar
            def _(act):
                act.sem_inc(acc_free, 2)
                act.sem_inc(wide_made, 2)
                act.sem_inc(tp_free, 1)
                act.sem_inc(ctx_turned, 2)

                def split_hi(f, b, turn):
                    act.wait_ge(w_in[b], 16 * turn + 16)
                    act.wait_ge(used, f + 1)
                    nc.scalar.copy(whi[:, b], w[:, b]).then_inc(hi_made, 1)

                def turned_copy(f, b, turn):
                    act.wait_ge(tp_full, f + 1)
                    act.wait_ge(turned_out[b], 16 * turn + 16)
                    nc.scalar.copy(turned[:, b, 0:CTX], cxt[:, b, CTX:2 * CTX]).then_inc(ctx_turned, 1)
                    nc.scalar.copy(turned[:, b, CTX:TOK], tp[:]).then_inc(tp_free, 1)

                def evacuate(f, b, kind, turn, within):
                    act.wait_ge(used, f + 3)
                    if kind == "xbc":
                        act.wait_ge(conv_step, CS * f + CS)
                        nc.scalar.copy(padded[:, b, 2:2 + CTX], cxt[:, b, 0:CTX])
                        nc.scalar.copy(padded[:, b, 6 + CTX:6 + CTX + SEQ], lat[:, b, :]).then_inc(acc_free, 1)
                        if not (isinstance(f, int) and f == 0):
                            turned_copy(f - 1, 1 - b, turn - (1 - b))
                            act.wait_ge(wide_out[b], 16 * turn)
                        act.wait_ge(conv_step, CS * f + 3 * CS)
                        nc.scalar.activation(wide[:, b, 0:CTX], conv[:, b, 0:CTX], ACT.Silu, bias=tap[:, b, CONV_W:CS])
                        nc.scalar.activation(wide[:, b, CTX:TOK], conv[:, b, 4 + CTX:W_OUT], ACT.Silu,
                                             bias=tap[:, b, CONV_W:CS]).then_inc(wide_made, 1)
                    elif kind in ("q", "k"):
                        act.wait_ge(wide_out[b], 16 * turn)
                        if kind == "k":
                            nc.scalar.copy(wide[:, b, 0:CTX], cxt[:, b, 0:CTX])
                        nc.scalar.copy(wide[:, b, CTX:TOK], lat[:, b, :]).then_inc(acc_free, 1)
                    else:
                        act.wait_ge(wide_out[b], 16 * turn + 16 * (NQK - NQ) // 2)
                        nc.scalar.activation(wide[:, b, CTX:TOK], lat[:, b, :], ACT.Sigmoid).then_inc(acc_free, 1)

                def step(f, b, kind, turn, within):
                    split_hi(f + 1, 1 - b, turn + b)
                    evacuate(f, b, kind, turn, within)

                split_hi(0, 0, 0)
                step(0, 0, "xbc", 0, 0)
                step(1, 1, "xbc", 0, 1)
                with act.Fori(1, NX // 2) as i:
                    step(2 * i, 0, "xbc", i, 2 * i)
                    step(2 * i + 1, 1, "xbc", i, 2 * i + 1)
                split_hi(NX + 1, 1, NX // 2)
                turned_copy(NX - 1, 1, NX // 2 - 1)
                evacuate(NX, 0, "q", NX // 2, 0)
                step(NX + 1, 1, "q", NX // 2, 1)
                with act.Fori(1, NQ // 2) as i:
                    for b in range(2):
                        step(2 * i + (NX + b), b, "q", i + NX // 2, 2 * i + b)
                pairs(act, "k", step)
                pairs(act, "gate", step)
                step(NF - 2, 0, "gate", NF // 2 - 1, NG - 2)
                evacuate(NF - 1, 1, "gate", NF // 2 - 1, NG - 1)

            @block.vector
            def _(dve):
                dve.sem_inc(w_free, 2)
                dve.wait_ge(tables_in, 64)
                dve.memset(padded[:], 0.0).then_inc(conv_step, 2 * CS)

                def split_lo(f, b):
                    dve.wait_ge(hi_made, f + 1)
                    nc.vector.tensor_tensor(wlo[:, b], w[:, b], whi[:, b].bitcast(F32), ALU.subtract).then_inc(w_free, 1)

                def convolve(f, b, kind, turn, within):
                    split_lo(f + 1, 1 - b)
                    dve.wait_ge(wide_made, f + 1)
                    cut = slice(f, f + 1) if isinstance(f, int) else ds(f, 1)
                    nc.vector.tensor_copy(tap[:, b, :], taps[:, cut, :].rearrange("p o c -> p (o c)")).then_inc(conv_step, 1)
                    dve.wait_ge(acc_free, f + 3)
                    dve.wait_ge(conv_step, CS * f + 2 * CS + 1)
                    nc.vector.tensor_scalar(conv[:, b], padded[:, b, 0:W_OUT], tap[:, b, 0:1], None,
                                            ALU.mult).then_inc(conv_step, 1)
                    for c in range(1, CONV_W):
                        dve.wait_ge(conv_step, CS * f + 2 * CS + 1 + c)
                        nc.vector.scalar_tensor_tensor(conv[:, b], padded[:, b, c:c + W_OUT], tap[:, b, c:c + 1],
                                                       conv[:, b], ALU.mult, ALU.add).then_inc(conv_step, 1)

                def rotate_in(f, b, within):
                    dve.wait_ge(tp_full, f + 1)
                    nc.vector.tensor_tensor(conv[:, b, 0:SEQ], tp[:, 0:SEQ], sin[:], ALU.mult).then_inc(tp_free, 1)
                    nc.vector.tensor_tensor(wide[:, b, CTX:TOK], wide[:, b, CTX:TOK], cos[:], ALU.mult).then_inc(rot_step, 1)
                    dve.wait_ge(tp_free, f + 2)
                    dve.wait_ge(rot_step, 2 * within + 1)
                    nc.vector.tensor_tensor(wide[:, b, CTX:TOK], wide[:, b, CTX:TOK], conv[:, b, 0:SEQ],
                                            ALU.add).then_inc(rot_step, 1)

                split_lo(0, 0)
                pairs(dve, "xbc", convolve)
                dve.wait_ge(wide_made, NX + 2)
                split_lo(NX + 1, 1)
                split_lo(NX + 2, 0)
                rotate_in(NX, 0, 0)
                with dve.Fori(1, NQK // 2) as i:
                    split_lo(2 * i + (NX + 1), 1)
                    rotate_in(2 * i + (NX - 1), 1, 2 * i - 1)
                    split_lo(2 * i + (NX + 2), 0)
                    rotate_in(2 * i + NX, 0, 2 * i)
                split_lo(NX + NQK + 1, 1)
                rotate_in(NX + NQK - 1, 1, NQK - 1)
                with dve.Fori(1, NG // 2) as i:
                    split_lo(2 * i + (NX + NQK), 0)
                    split_lo(2 * i + (NX + NQK + 1), 1)

            @block.gpsimd
            def _(pool):
                s.credit(pool, turned_out)
                pool.memset(zeros[:], 0.0).then_inc(zeros_made, 1)
                pool.wait_ge(zeros_made, 1)
                for a in (CTX, KV_LAT0 + SEQ):
                    pool.dma_start(qkF[:, a:a + BLANK].rearrange("(f p) t -> p f t", p=P),
                                   zeros[:].unsqueeze(1).to_broadcast([P, NQK, BLANK])).then_inc(blanks_out, 16)

                def store(f, b, kind, turn, within):
                    row = within * P
                    rows = slice(row, row + P) if isinstance(row, int) else ds(row, P)
                    if kind == "xbc":
                        pool.wait_ge(wide_made, f + 3)
                        pool.dma_start(xbcF[rows, :], wide[:, b]).then_inc(wide_out[b], 16)
                        pool.wait_ge(tp_free, f + 2)
                        pool.dma_start(xbcT[:, rows].rearrange("(c p) n -> p c n", p=P),
                                       turned[:, b].rearrange("p (c n) -> p c n", n=P)).then_inc(turned_out[b], 16)
                    elif kind == "q":
                        pool.wait_ge(rot_step, 2 * within + 2)
                        pool.dma_start(qkF[rows, KV_LAT0:KV_LAT0 + SEQ], wide[:, b, CTX:TOK]).then_inc(wide_out[b], 16)
                    elif kind == "k":
                        pool.wait_ge(rot_step, 2 * within + 2)
                        pool.dma_start(qkF[rows, 0:CTX], wide[:, b, 0:CTX]).then_inc(wide_out[b], 16)
                        pool.dma_start(qkF[rows, KV_LAT0:KV_LAT0 + SEQ], wide[:, b, CTX:TOK]).then_inc(wide_out[b], 16)
                    else:
                        pool.wait_ge(acc_free, f + 3)
                        pool.dma_start(gF[rows, :], wide[:, b, CTX:TOK]).then_inc(wide_out[b], 16)

                for kind in ("xbc", "q", "k", "gate"):
                    pairs(pool, kind, store)
                for b in range(2):
                    store(NF - 2 + b, b, "gate", NF // 2 - 1, NG - 2 + b)
                pool.wait_ge(blanks_out, 32)
                for b in range(2):
                    pool.wait_ge(wide_out[b], 16 * (NF + NQK - NQ) // 2)
                    pool.wait_ge(turned_out[b], 16 * NX // 2 + 16)


def project_t_stage(s, hi, lo, zT, vT, dtT):
    nc = s.nc
    NZ, VW, DW = D_INNER // 512, KVH * HD, 2 * HEADS
    STAGED = 4
    with ExitStack() as st:
        w = own(st, nc, "wt_raw", [P, 2, KT, 512])
        whi = own(st, nc, "wt_hi", [P, 2, KT, 512], F32R)
        wlo = own(st, nc, "wt_lo", [P, 2, KT, 512], F32R)
        rows = own(st, nc, "t_rows", [P, STAGED, 512])
        zeros = own(st, nc, "t_zeros", [P, VW])
        acc = bank(st, nc, "t_acc", [P, 8, 512])
        w_in = [s.sem(f"t_w_in{b}") for b in range(2)]
        hi_made, w_free = s.sem("t_hi_made"), s.sem("t_w_free")
        acc_full, acc_free = s.sem("t_acc_full"), s.sem("t_acc_free")
        rows_out = [s.sem(f"t_rows_out{j}") for j in range(STAGED)]
        zeros_made, zeros_out = s.sem("t_zeros_made"), s.sem("t_zeros_out")
        wv = s.x["w_in"][0].rearrange("(k p) n -> p k n", p=P)

        with nc.Block() as block:

            @block.sync
            def _(sp):
                with sp.Fori(0, NZ // 2) as i:
                    for b in range(2):
                        sp.wait_ge(w_free, 2 * i + (b + 1))
                        sp.dma_start(w[:, b], wv[:, :, ds(1024 * i + (Z0 + 512 * b), 512)]).then_inc(w_in[b], 16)
                sp.wait_ge(w_free, NZ + 1)
                sp.dma_start(w[:, 0, :, 0:VW], wv[:, :, V0:V0 + VW]).then_inc(w_in[0], 16)
                sp.dma_start(w[:, 0, :, VW:VW + DW], wv[:, :, DT0:DT0 + DW]).then_inc(w_in[0], 16)

            @block.tensor
            def _(pe):
                def product(u, b, tiles, t0, width):
                    pe.wait_ge(w_free, u + 3)
                    for t in range(tiles):
                        a = (t0 + t) * P
                        pe.wait_ge(acc_free, u * LCHUNK + (t + 1))
                        for k in range(KT):
                            for n_pass, (part, weights) in enumerate(((hi, whi), (hi, wlo), (lo, whi))):
                                mm = nc.tensor.matmul(acc[:, t % 8, 0:width], part[:, k, a:a + P],
                                                      weights[:, b, k, 0:width],
                                                      start=(k == 0 and n_pass == 0), stop=(k == KT - 1 and n_pass == 2))
                        mm.then_inc(acc_full, 1)

                with pe.Fori(0, NZ // 2) as i:
                    for b in range(2):
                        product(2 * i + b, b, LCHUNK, CCHUNK, 512)
                product(NZ, 0, NCHUNK, 0, VW + DW)

            @block.scalar
            def _(act):
                act.sem_inc(acc_free, 8)

                def split_hi(u, b, need, width):
                    act.wait_ge(w_in[b], need)
                    if not isinstance(u, int) or u > 1:
                        act.wait_ge(acc_full, LCHUNK * u - LCHUNK)
                    nc.scalar.copy(whi[:, b, :, 0:width], w[:, b, :, 0:width]).then_inc(hi_made, 1)

                def tile(n, j, turn, func, width, t):
                    act.wait_ge(acc_full, n + 1)
                    act.wait_ge(rows_out[j], 16 * turn)
                    nc.scalar.activation(rows[:, j, 0:width], acc[:, t % 8, 0:width], func).then_inc(acc_free, 1)

                def silu_tiles(u):
                    for t in range(LCHUNK):
                        tile(u * LCHUNK + t, t % STAGED, 2 * u + t // STAGED, ACT.Silu, 512, t)

                split_hi(0, 0, 16, 512)
                split_hi(1, 1, 16, 512)
                silu_tiles(0)
                with act.Fori(1, NZ // 2) as i:
                    split_hi(2 * i, 0, 16 * i + 16, 512)
                    silu_tiles(2 * i - 1)
                    split_hi(2 * i + 1, 1, 16 * i + 16, 512)
                    silu_tiles(2 * i)
                split_hi(NZ, 0, 16 * (NZ // 2) + 32, VW + DW)
                silu_tiles(NZ - 1)
                for t in range(NCHUNK):
                    turns = 2 * NZ + t // STAGED
                    extra = t // STAGED
                    tile(NZ * LCHUNK + t, t % STAGED, turns + extra, ACT.Copy, VW + DW, t)

            @block.vector
            def _(dve):
                dve.sem_inc(w_free, 2)

                def split_lo(u, b, width):
                    dve.wait_ge(hi_made, u + 1)
                    nc.vector.tensor_tensor(wlo[:, b, :, 0:width], w[:, b, :, 0:width],
                                            whi[:, b, :, 0:width].bitcast(F32), ALU.subtract).then_inc(w_free, 1)

                with dve.Fori(0, NZ // 2) as i:
                    for b in range(2):
                        split_lo(2 * i + b, b, 512)
                split_lo(NZ, 0, VW + DW)

            @block.gpsimd
            def _(pool):
                pool.memset(zeros[:], 0.0).then_inc(zeros_made, 1)
                pool.wait_ge(zeros_made, 1)
                for a in (CTX, KV_LAT0 + SEQ):
                    pool.dma_start(vT[a:a + BLANK, :], zeros[:]).then_inc(zeros_out, 16)

                def store(u, col):
                    for t in range(LCHUNK):
                        pool.wait_ge(acc_free, u * LCHUNK + (8 + t + 1))
                        pool.dma_start(zT[t * P:t * P + P, ds(col, 512)], rows[:, t % STAGED, :]).then_inc(rows_out[t % STAGED], 16)

                with pool.Fori(0, NZ) as i:
                    store(i, 512 * i)
                for t in range(NCHUNK):
                    j = t % STAGED
                    pool.wait_ge(acc_free, NZ * LCHUNK + 8 + t + 1)
                    a = t * P if t < CCHUNK else KV_LAT0 + (t - CCHUNK) * P
                    pool.dma_start(vT[a:a + P, :], rows[:, j, 0:VW]).then_inc(rows_out[j], 16)
                    pool.dma_start(dtT[t * P:t * P + P, :], rows[:, j, VW:VW + DW]).then_inc(rows_out[j], 16)
                pool.wait_ge(zeros_out, 32)
                for j in range(STAGED):
                    last = sum(2 for t in range(NCHUNK) if t % STAGED == j)
                    pool.wait_ge(rows_out[j], 16 * (2 * NZ + last))


def decay_stage(s, dtT, tabs, cumrow):
    nc = s.nc
    W = 2 * HEADS
    CUM, ECUM, DT, WX, DEC = range(5)
    SERIES = [1.0 / (2 * n + 1) for n in range(8, 0, -1)]
    with ExitStack() as st:
        sq = own(st, nc, "d_squares", [P, 4, P])
        raw = own(st, nc, "d_raw", [P, NCHUNK, W])
        bias, alog = own(st, nc, "d_bias", [P, W]), own(st, nc, "d_alog", [P, W])
        mag, e, r, q, t = (own(st, nc, f"d_{n}", [P, NCHUNK, W]) for n in ("mag", "e", "r", "q", "t"))
        a = own(st, nc, "d_a", [P, W])
        da, end = own(st, nc, "d_da", [P, NCHUNK, W]), own(st, nc, "d_end", [P, NCHUNK, W])
        tab = own(st, nc, "d_tab", [P, NCHUNK, 5, W])
        rows_hi, rows_lo = own(st, nc, "d_rows_hi", [W, LCHUNK, P], F32R), own(st, nc, "d_rows_lo", [W, LCHUNK, P], F32R)
        cum_ps = bank(st, nc, "d_cum_ps", [P, 2, 512])
        end_ps = bank(st, nc, "d_end_ps", [P, 2, 512])
        row_ps = bank(st, nc, "d_row_ps", [P, LCHUNK, P])
        loaded, step, act_done = s.sem("d_loaded"), s.sem("d_step"), s.sem("d_act_done")
        sums_done, rows_done, copied, stored = s.sem("d_sums_done"), s.sem("d_rows_done"), s.sem("d_copied"), s.sem("d_stored")

        def wide(ap):
            return ap.unsqueeze(1).to_broadcast([P, NCHUNK, W])

        with nc.Block() as block:

            @block.sync
            def _(sp):
                sp.dma_start(raw[:], dtT.rearrange("(c p) n -> p c n", p=P)).then_inc(loaded, 16)
                sp.dma_start(bias[:], s.x["dt_bias"].rearrange("a d h -> a (d h)").to_broadcast([P, W])).then_inc(loaded, 16)
                sp.dma_start(alog[:], s.x["a_log"].rearrange("a d h -> a (d h)").to_broadcast([P, W])).then_inc(loaded, 16)
                sp.dma_start(sq[:], s.squares.rearrange("p (a q) -> p a q", q=P)[:, 0:4, :]).then_inc(loaded, 16)
                sp.wait_ge(copied, 2)
                sp.dma_start(tabs.rearrange("c p n -> p c n"), tab[:].rearrange("p c k n -> p c (k n)")).then_inc(stored, 16)
                sp.wait_ge(copied, 4)
                for part, rows in enumerate((rows_hi, rows_lo)):
                    sp.dma_start(cumrow[:, part].rearrange("c n i -> n c i"), rows[:].bitcast(F32)).then_inc(stored, 16)
                sp.wait_ge(stored, 48)

            @block.vector
            def _(dve):
                done = 0

                def then(ins):
                    nonlocal done
                    done += 1
                    ins.then_inc(step, 1)
                    dve.wait_ge(step, done)

                V = nc.vector
                dve.wait_ge(loaded, 64)
                then(V.tensor_tensor(raw[:], raw[:], wide(bias[:]), ALU.add))
                then(V.tensor_scalar(mag[:], raw[:], -1.0, None, ALU.mult))
                then(V.tensor_tensor(mag[:], mag[:], raw[:], ALU.max))
                dve.wait_ge(act_done, 1)
                then(V.tensor_scalar(t[:], e[:], 2.0, None, ALU.add))
                then(V.reciprocal(q[:], t[:]))
                then(V.tensor_tensor(r[:], e[:], q[:], ALU.mult))
                then(V.tensor_tensor(q[:], r[:], r[:], ALU.mult))
                then(V.tensor_scalar(t[:], q[:], SERIES[0], None, ALU.mult))
                for c in SERIES[1:]:
                    then(V.scalar_tensor_tensor(t[:], t[:], c, q[:], ALU.add, ALU.mult))
                then(V.scalar_tensor_tensor(t[:], t[:], 1.0, r[:], ALU.add, ALU.mult))
                then(V.tensor_scalar(raw[:], raw[:], 0.0, None, ALU.max))
                then(V.scalar_tensor_tensor(tab[:, :, DT, :], t[:], 2.0, raw[:], ALU.mult, ALU.add))
                dve.wait_ge(act_done, 2)
                then(V.tensor_scalar(a[:], a[:], -1.0, None, ALU.mult))
                V.tensor_tensor(da[:], tab[:, :, DT, :], wide(a[:]), ALU.mult).then_inc(copied, 1)
                dve.wait_ge(sums_done, 1)
                for d in range(2):
                    h = slice(HEADS * d, HEADS * d + HEADS)
                    then(V.tensor_copy(tab[:, :, CUM, h], cum_ps[:, d, 0:NCHUNK * HEADS].rearrange("p (c h) -> p c h", h=HEADS)))
                    then(V.tensor_copy(end[:, :, h], end_ps[:, d, 0:NCHUNK * HEADS].rearrange("p (c h) -> p c h", h=HEADS)))
                then(V.tensor_tensor(r[:], end[:], tab[:, :, CUM, :], ALU.subtract))
                V.nop().then_inc(rows_done, 1)
                dve.wait_ge(act_done, 5)
                V.tensor_tensor(tab[:, :, WX, :], q[:], tab[:, :, DT, :], ALU.mult).then_inc(copied, 1)
                dve.wait_ge(rows_done, 2)
                V.tensor_copy(rows_hi[:], row_ps[0:W]).then_inc(copied, 1)
                dve.wait_ge(copied, 3)
                V.tensor_tensor(rows_lo[:], row_ps[0:W], rows_hi[:].bitcast(F32), ALU.subtract).then_inc(copied, 1)

            @block.scalar
            def _(act):
                act.wait_ge(step, 3)
                nc.scalar.activation(e[:], mag[:], ACT.Exp, scale=-1.0).then_inc(act_done, 1)
                nc.scalar.activation(a[:], alog[:], ACT.Exp).then_inc(act_done, 1)
                act.wait_ge(rows_done, 1)
                nc.scalar.activation(q[:], r[:], ACT.Exp).then_inc(act_done, 1)
                nc.scalar.activation(tab[:, :, ECUM, :], tab[:, :, CUM, :], ACT.Exp).then_inc(act_done, 1)
                nc.scalar.activation(tab[:, :, DEC, :], end[:], ACT.Exp).then_inc(act_done, 1)

            @block.tensor
            def _(pe):
                pe.wait_ge(copied, 1)
                for d, triangle in ((0, 1), (1, 2)):
                    rhs = da[:, :, HEADS * d:HEADS * d + HEADS]
                    out = [o[:, d, 0:NCHUNK * HEADS].rearrange("p (c h) -> p c h", h=HEADS) for o in (cum_ps, end_ps)]
                    nc.tensor.matmul(out[0], sq[:, triangle, :], rhs, start=True, stop=True)
                    mm = nc.tensor.matmul(out[1], sq[:, 3, :], rhs, start=True, stop=True)
                mm.then_inc(sums_done, 1)
                pe.wait_ge(rows_done, 1)
                for c in range(LCHUNK):
                    mm = nc.tensor.transpose(row_ps[0:W, c, :], tab[:, CCHUNK + c, CUM, :], sq[:, 0, :])
                mm.then_inc(rows_done, 1)


def states_stage(s, xbcT, tabs, before):
    nc = s.nc
    WX, DEC = range(2)
    XB = D_INNER + GROUPS * STATE
    PAIRS = [(n, CCHUNK - 1 - n if n < CCHUNK else NCHUNK + CCHUNK - 1 - n) for n in range(NCHUNK)]
    with ExitStack() as st:
        xb = own(st, nc, "s_xb", [P, NCHUNK, XB])
        weights = own(st, nc, "s_weights", [P, NCHUNK, 2, 2 * HEADS])
        xw = own(st, nc, "s_xw", [P, 2, 2, D_INNER])
        state = own(st, nc, "s_state", [P, 2, 2, D_INNER])
        add = bank(st, nc, "s_add", [P, 2, D_INNER])
        loaded = [s.sem(f"s_loaded{c}") for c in range(NCHUNK)]
        kept = [[s.sem(f"s_kept{d}{b}") for b in range(2)] for d in range(2)]
        xw_made, added, decayed, made = s.sem("s_xw_made"), s.sem("s_added"), s.sem("s_decayed"), s.sem("s_state_made")

        def heads(ap):
            return ap.rearrange("p (h q) -> p h q", q=PDIM)

        def column(c, kind, d):
            return weights[:, c, kind, HEADS * d:HEADS * d + HEADS].unsqueeze(2).to_broadcast([P, HEADS, PDIM])

        with nc.Block() as block:

            @block.sync
            def _(sp):
                first_use = []
                for pair in PAIRS:
                    first_use += [c for c in pair if c not in first_use]
                for c in first_use:
                    sp.dma_start(xb[:, c], xbcT[c * P:c * P + P, 0:XB]).then_inc(loaded[c], 16)
                    sp.dma_start(weights[:, c], tabs[c, :, 3 * 2 * HEADS:].rearrange("p (k n) -> p k n", k=2)).then_inc(loaded[c], 16)

            @block.gpsimd
            def _(pool):
                for n, chunks in enumerate(PAIRS):
                    for d, c in enumerate(chunks):
                        pool.wait_ge(loaded[c], 32)
                        if n >= 2:
                            pool.wait_ge(added, 2 * (n - 2) + d + 1)
                        nc.gpsimd.tensor_tensor(heads(xw[:, d, n % 2]), heads(xb[:, c, 0:D_INNER]), column(c, WX, d), ALU.mult).then_inc(xw_made, 1)

            @block.tensor
            def _(pe):
                for n, chunks in enumerate(PAIRS):
                    for d, c in enumerate(chunks):
                        pe.wait_ge(loaded[c], 32)
                        pe.wait_ge(xw_made, 2 * n + d + 1)
                        if n >= 1:
                            pe.wait_ge(made, 2 * n + d + 1)
                        for g in range(GROUPS):
                            mm = nc.tensor.matmul(add[:, d, 512 * g:512 * g + 512], xb[:, c, D_INNER + STATE * g:D_INNER + STATE * g + STATE],
                                                  xw[:, d, n % 2, 512 * g:512 * g + 512], start=True, stop=True)
                        mm.then_inc(added, 1)

            @block.vector
            def _(dve):
                dve.memset(state[:, :, 0, :], 0.0).then_inc(made, 2)
                for n, chunks in enumerate(PAIRS):
                    b = n % 2
                    for d, c in enumerate(chunks):
                        dve.wait_ge(made, 2 * n + d + 1)
                        dve.wait_ge(loaded[c], 32)
                        if n > CCHUNK:
                            dve.wait_ge(kept[d][1 - b], 16 * ((n - 1) // 2))
                        nc.vector.tensor_tensor(heads(state[:, d, 1 - b]), heads(state[:, d, b]), column(c, DEC, d), ALU.mult).then_inc(decayed, 1)
                        dve.wait_ge(decayed, 2 * n + d + 1)
                        dve.wait_ge(added, 2 * n + d + 1)
                        nc.vector.tensor_tensor(state[:, d, 1 - b], state[:, d, 1 - b], add[:, d], ALU.add).then_inc(made, 1)

            @block.scalar
            def _(act):
                for n in range(CCHUNK, NCHUNK):
                    for d, c in enumerate(PAIRS[n]):
                        act.wait_ge(made, 2 * n + d + 1)
                        act.dma_start(before[d, c - CCHUNK], state[:, d, n % 2]).then_inc(kept[d][n % 2], 16)
                for d in range(2):
                    for b in range(2):
                        act.wait_ge(kept[d][b], 16 * LCHUNK // 2)


def scan_output_stage(s, xbcT, xbcF, zT, tabs, cumrow, before, yT):
    nc = s.nc
    V = nc.vector
    LANES = 4
    NARG = 2 + 2 * LANES
    ONES, HI, LO = slice(0, 2), slice(2, 2 + LANES), slice(2 + LANES, NARG)
    BANKS = 2 * HPG // LANES
    G = GROUPS
    with ExitStack() as st:
        sq = own(st, nc, "y_squares", [P, 3, P])
        ident = own(st, nc, "y_ident", [P, P], F32R)
        neg, negs = own(st, nc, "y_neg", [P, 2, P]), own(st, nc, "y_negs", [P, 2, LANES, P], F32R)
        dskip = own(st, nc, "y_dskip", [P, HEADS])
        x, z = own(st, nc, "y_x", [P, 2, D_INNER]), own(st, nc, "y_z", [P, 2, D_INNER])
        bc = own(st, nc, "y_bc", [P, 2, 2, GROUPS, P])
        before_t = own(st, nc, "y_before", [P, 2, 2, D_INNER])
        tab = own(st, nc, "y_tab", [P, 2, 5, 2, HEADS])
        own_cum = own(st, nc, "y_own_cum", [NARG, 2, 2, HEADS // LANES, P], F32R)
        all_cum = own(st, nc, "y_all_cum", [NARG, 2, 2, HPG, P], F32R)
        decay = own(st, nc, "y_decay", [P, 2, 2, HPG, P])
        xs = own(st, nc, "y_xs", [P, 2, 3, 512])
        part, pre = own(st, nc, "y_part", [P, 2, 512]), own(st, nc, "y_pre", [P, 2, 512])
        y = own(st, nc, "y_y", [P, D_INNER])
        g_ps = bank(st, nc, "y_g_ps", [P, 2, GROUPS, P])
        arg_ps = bank(st, nc, "y_arg_ps", [P, 2, LANES, P])
        off_ps, diag_ps = bank(st, nc, "y_off_ps", [P, 2, 512]), bank(st, nc, "y_diag_ps", [P, 2, 512])
        const_in, ready = s.sem("y_const_in"), s.sem("y_ready")
        tiles_in, cum_in = [s.sem(f"y_tiles_in{b}") for b in range(2)], [s.sem(f"y_cum_in{b}") for b in range(2)]
        args_made, exps_made, g_made, l_made = (s.sem(f"y_{n}") for n in ("args_made", "exps_made", "g_made", "l_made"))
        xs_made, off_made, off_read, diag_made, diag_read = (s.sem(f"y_{n}") for n in ("xs_made", "off_made", "off_read", "diag_made", "diag_read"))
        part_step, y_step, y_made, y_out, carrier, pool_carrier = (s.sem(f"y_{n}") for n in ("part_step", "y_step", "y_made", "y_out", "carrier", "pool_carrier"))
        TI = 9 * 16
        bf = xbcF.rearrange("(a g n) t -> n a g t", g=GROUPS, n=P)

        def cut(start, size):
            return slice(start, start + size) if isinstance(start, int) else ds(start, size)

        def chunks(eng, step):
            with eng.Fori(0, LCHUNK // 2 - 1) as i:
                for b in range(2):
                    step(2 * i + b, b, i, True)
            for b in range(2):
                step(LCHUNK - 2 + b, b, LCHUNK // 2 - 1, b == 0)

        def heads(ap):
            return ap.rearrange("p (h q) -> p h q", q=PDIM)

        def with_next(ahead, now):
            def step(n, b, i, more):
                for g in range(G):
                    if g < G - 1:
                        ahead(n, b, i, g + 1)
                    elif more:
                        ahead(n + 1, 1 - b, i + b, 0)
                    now(n, b, i, g)
            return step

        with nc.Block() as block:

            @block.sync
            def _(sp):
                def load_cum(n, g):
                    sp.wait_ge(args_made, BANKS * G * n + (BANKS * (g - 1) + BANKS + 1))
                    sp.sem_inc(carrier, 1)
                    src = cumrow.rearrange("c e (d h) i -> c e d h i", d=2)[cut(n, 1), :, :, HPG * g:HPG * g + HPG, :]
                    for d in range(2):
                        sp.dma_start(all_cum[ONES, g % 2, d].bitcast(F32), src[0:1, :, d].rearrange("c e h i -> (c e) h i")).then_inc(cum_in[g % 2], 16)

                def load_tiles(n, b):
                    if not isinstance(n, int) or n > 0:
                        sp.wait_ge(y_made, G * n)
                    sp.sem_inc(carrier, 1)
                    for a in range(2):
                        sp.dma_start(bc[:, b, a], bf[:, D_INNER // 512 + a, :, cut(n * P + CTX, P)]).then_inc(tiles_in[b], 16)
                    sp.dma_start(tab[:, b], tabs.rearrange("c p n -> (c p) n")[cut(n * P + CTX, P), :].rearrange("p (k d h) -> p k d h", k=5, d=2)).then_inc(tiles_in[b], 16)
                    for part_, lanes in enumerate((HI, LO)):
                        src = cumrow[cut(n, 1), part_].rearrange("c (q r) i -> (c r) q i", r=LANES)
                        sp.dma_start(own_cum[lanes, b].rearrange("r d q i -> r (d q) i").bitcast(F32), src).then_inc(tiles_in[b], 16)
                    sp.dma_start(x[:, b], xbcT[cut(n * P + CTX, P), 0:D_INNER]).then_inc(tiles_in[b], 16)
                    for d in range(2):
                        sp.dma_start(before_t[:, b, d], before[d].rearrange("c n q -> (c n) q")[cut(n * P, P), :]).then_inc(tiles_in[b], 16)
                    sp.dma_start(z[:, b], zT[cut(n * P, P), :]).then_inc(tiles_in[b], 16)

                def step(n, b, i, more):
                    for g in range(G):
                        load_cum(n, g)
                    if more:
                        load_tiles(n + 1, 1 - b)

                sp.dma_start(sq[:], s.squares.rearrange("p (a q) -> p a q", q=P)[:, 0:3, :]).then_inc(const_in, 16)
                sp.dma_start(dskip[:], s.x["d_skip"].to_broadcast([P, HEADS])).then_inc(const_in, 16)
                sp.dma_start(all_cum[2:NARG].rearrange("r b d h i -> r b (d h i)")[:, 0].bitcast(F32), s.lanes).then_inc(const_in, 16)
                sp.dma_start(all_cum[2:NARG].rearrange("r b d h i -> r b (d h i)")[:, 1].bitcast(F32), s.lanes).then_inc(const_in, 16)
                load_tiles(0, 0)
                chunks(sp, step)

            @block.tensor
            def _(pe):
                pe.sem_inc(args_made, BANKS + 1)

                def exponents(n, b, i, g):
                    if g == 0:
                        pe.wait_ge(tiles_in[b], TI * i + TI)
                        for k in range(G):
                            mm = nc.tensor.matmul(g_ps[:, b, k, :], bc[:, b, 0, k, :], bc[:, b, 1, k, :], start=True, stop=True)
                        mm.then_inc(g_made, 1)
                    pe.wait_ge(cum_in[g % 2], 64 * n + (32 * (g // 2) + 32))
                    for k in range(BANKS):
                        d, half = k // 2, k % 2
                        pe.wait_ge(exps_made, BANKS * G * n + (BANKS * g + k + 1))
                        nc.tensor.matmul(arg_ps[:, k % 2], ident[:], negs[:, d], start=True, stop=False)
                        nc.tensor.matmul(arg_ps[:, k % 2], own_cum[:, b, d, 2 * g + half, :],
                                         all_cum[:, g % 2, d, LANES * half:LANES * half + LANES, :], start=False, stop=True).then_inc(args_made, 1)

                def sums(n, b, i, g):
                    pe.wait_ge(off_read, G * n + (g + 1))
                    for d in range(2):
                        mm = nc.tensor.matmul(off_ps[:, d], bc[:, b, 1, g, :], before_t[:, b, d, 512 * g:512 * g + 512], start=True, stop=True)
                    mm.then_inc(off_made, 1)
                    pe.wait_ge(xs_made, 3 * G * n + (3 * g + 3))
                    pe.wait_ge(diag_read, G * n + (g + 1))
                    pe.wait_ge(l_made, 2 * G * n + (2 * g + 2))
                    for h in range(HPG):
                        cols = slice(PDIM * h, PDIM * h + PDIM)
                        nc.tensor.matmul(diag_ps[:, g % 2, cols], decay[:, g % 2, 0, h, :], xs[:, g % 2, 0, cols], start=True, stop=False)
                        mm = nc.tensor.matmul(diag_ps[:, g % 2, cols], decay[:, g % 2, 1, h, :], xs[:, g % 2, 1, cols], start=False, stop=True)
                    mm.then_inc(diag_made, 1)

                pe.wait_ge(const_in, 64)
                pe.wait_ge(ready, 3)
                exponents(0, 0, 0, 0)
                chunks(pe, with_next(exponents, sums))

            @block.scalar
            def _(act):
                act.sem_inc(exps_made, 2)

                def step(n, b, i, more):
                    for g in range(G):
                        act.wait_ge(diag_made, G * n + (g + 1))
                        for k in range(BANKS):
                            d, half = k // 2, k % 2
                            act.wait_ge(args_made, BANKS * G * n + (BANKS * g + k + BANKS + 2))
                            nc.scalar.activation(decay[:, g % 2, d, LANES * half:LANES * half + LANES], arg_ps[:, k % 2], ACT.Exp).then_inc(exps_made, 1)

                chunks(act, step)

            @block.vector
            def _(dve):
                dve.sem_inc(off_read, 1)
                dve.sem_inc(diag_read, 2)
                dve.sem_inc(diag_made, 2)
                V.memset(own_cum[ONES].bitcast(F32), 1.0).then_inc(ready, 1)
                dve.wait_ge(const_in, 64)
                V.tensor_copy(ident[:], sq[:, 0, :])
                V.tensor_scalar(neg[:], sq[:, 1:3, :], -NEG, NEG, ALU.mult, ALU.add).then_inc(ready, 1)
                dve.wait_ge(ready, 2)
                V.tensor_copy(negs[:], neg[:].unsqueeze(2).to_broadcast([P, 2, LANES, P])).then_inc(ready, 1)

                def step(n, b, i, more):
                    dve.wait_ge(tiles_in[b], TI * i + TI)
                    dve.wait_ge(g_made, n + 1)
                    for g in range(G):
                        at = 3 * G * n + 3 * g
                        for d in range(2):
                            dve.wait_ge(exps_made, BANKS * G * n + (BANKS * g + 2 * d + 4))
                            V.tensor_tensor(decay[:, g % 2, d], decay[:, g % 2, d], g_ps[:, b, g, :].unsqueeze(1).to_broadcast([P, HPG, P]),
                                            ALU.mult).then_inc(l_made, 1)
                        dve.wait_ge(off_made, G * n + (g + 1))
                        dve.wait_ge(part_step, at + 1)
                        for d in range(2):
                            ins = V.tensor_tensor(heads(part[:, d]), heads(off_ps[:, d]),
                                                  tab[:, b, 1, d, HPG * g:HPG * g + HPG].unsqueeze(2).to_broadcast([P, HPG, PDIM]), ALU.mult)
                            ins.then_inc(part_step, 1)
                        dve.wait_ge(part_step, at + 3)
                        V.tensor_tensor(part[:, 0], part[:, 0], part[:, 1], ALU.add).then_inc(off_read, 1)
                        dve.wait_ge(off_read, G * n + (g + 2))
                        dve.wait_ge(diag_made, G * n + (g + 3))
                        dve.wait_ge(y_made, G * n + (g + 3))
                        V.tensor_tensor(pre[:, g % 2], part[:, 0], diag_ps[:, g % 2], ALU.add).then_inc(diag_read, 1)
                        dve.wait_ge(diag_read, G * n + (g + 3))
                        dve.sem_inc(part_step, 1)

                dve.sem_inc(part_step, 1)
                chunks(dve, step)

            @block.gpsimd
            def _(pool):
                pool.sem_inc(y_made, G)
                pool.wait_ge(const_in, 64)

                def scale(n, b, i, g):
                    if g == 0:
                        pool.wait_ge(tiles_in[b], TI * i + TI)
                    pool.wait_ge(diag_made, G * n + (g + 1))
                    pool.wait_ge(y_made, G * n + (g + 3))
                    hs = slice(HPG * g, HPG * g + HPG)
                    for j in range(3):
                        col = tab[:, b, 2, j, hs] if j < 2 else dskip[:, hs]
                        nc.gpsimd.tensor_tensor(heads(xs[:, g % 2, j]), heads(x[:, b, 512 * g:512 * g + 512]),
                                                col.unsqueeze(2).to_broadcast([P, HPG, PDIM]), ALU.mult).then_inc(xs_made, 1)

                def finish(n, b, i, g):
                    cols = slice(512 * g, 512 * g + 512)
                    pool.wait_ge(diag_read, G * n + (g + 3))
                    pool.wait_ge(xs_made, 3 * G * n + (3 * g + 3))
                    nc.gpsimd.tensor_tensor(xs[:, g % 2, 2], pre[:, g % 2], xs[:, g % 2, 2], ALU.add).then_inc(y_step, 1)
                    pool.wait_ge(y_step, G * n + (g + 1))
                    nc.gpsimd.tensor_tensor(y[:, cols], xs[:, g % 2, 2], z[:, b, cols], ALU.mult).then_inc(y_made, 1)
                    if g == G - 1:
                        pool.wait_ge(y_made, G * n + 2 * G)
                        pool.sem_inc(pool_carrier, 1)
                        pool.dma_start(yT[cut(n * P, P), :], y[:]).then_inc(y_out, 16)
                        pool.wait_ge(y_out, 16 * n + 16)

                scale(0, 0, 0, 0)
                chunks(pool, with_next(scale, finish))


def attention_stage(s, qkF, vT, aF):
    nc = s.nc
    V = nc.vector
    KEYS = CTX + 3 * P
    NKT = KEYS // P
    PER_KV = QH // KVH
    TOP_HI, TOP_LO = HD, HD + 32
    K2 = TOP_LO + 1
    ORDER = (0, 2, 1, 4, 3)
    EDGES = (2, 4)
    HEAD_CUTS = ((0, 4), (4, 10), (10, 16))
    with ExitStack() as st:
        ident = own(st, nc, "a_ident", [P, P])
        sink, negsink = own(st, nc, "a_sink", [P, QH]), own(st, nc, "a_negsink", [P, QH])
        q_raw, k_raw = own(st, nc, "a_q_raw", [P, QH, P]), own(st, nc, "a_k_raw", [P, KVH, 3 * P])
        kc_raw = own(st, nc, "a_kc_raw", [P, KVH, CTX])
        q1, q2 = own(st, nc, "a_q1", [P, 2, QH, P], F32R), own(st, nc, "a_q2", [P, 2, QH, P], F32R)
        k1, k2 = own(st, nc, "a_k1", [P, 2, KVH, KEYS], F32R), own(st, nc, "a_k2", [P, 2, KVH, KEYS], F32R)
        vctx, vwin = own(st, nc, "a_vctx", [P, CCHUNK, KVH, 2 * HD]), own(st, nc, "a_vwin", [P, 2, 3, KVH, 2 * HD])
        mask, edge = own(st, nc, "a_mask", [P, 2, KEYS]), own(st, nc, "a_edge", [P, 2, 2, P])
        masked = own(st, nc, "a_masked", [P, 2, KEYS])
        top, negtop = own(st, nc, "a_top", [P, QH]), own(st, nc, "a_negtop", [P, QH])
        sink_col, sunk = own(st, nc, "a_sink_col", [QH, 1]), own(st, nc, "a_sunk", [QH, P])
        sunk_spread = own(st, nc, "a_sunk_spread", [P, 2, QH])
        thi, tlo = own(st, nc, "a_thi", [QH, P], F32R), own(st, nc, "a_tlo", [QH, P], F32R)
        prob = own(st, nc, "a_prob", [P, 2, NKT, PER_KV, P])
        cols, inverse = own(st, nc, "a_cols", [P, 2, QH, P]), own(st, nc, "a_inverse", [HD, QH, P])
        sums, inv_sums = own(st, nc, "a_sums", [P, QH]), own(st, nc, "a_inv_sums", [P, QH])
        a_ps = bank(st, nc, "a_a_ps", [P, 2, 1024])
        b_ps = bank(st, nc, "a_b_ps", [P, 2, PER_KV, P])
        c_ps = bank(st, nc, "a_c_ps", [P, PER_KV, P])
        tp = bank(st, nc, "a_tp", [P, 512])
        const_in, raw_in, top_in = s.sem("a_const_in"), s.sem("a_raw_in"), s.sem("a_top_in")
        block_in = [s.sem(f"a_block_in{b}") for b in range(2)]
        fixed, k_hi, q_hi, k_lo, q_lo, q2_made = (s.sem(f"a_{n}") for n in ("fixed", "k_hi", "q_hi", "k_lo", "q_lo", "q2_made"))
        scored, maxed, negated, sunk_made = (s.sem(f"a_{n}") for n in ("scored", "maxed", "negated", "sunk_made"))
        top_turned, top_hi, top_lo = s.sem("a_top_turned"), s.sem("a_top_hi"), s.sem("a_top_lo")
        b_made, b_masked, exps_made = s.sem("a_b_made"), s.sem("a_b_masked"), s.sem("a_exps_made")
        summed, cols_made, carrier = s.sem("a_summed"), s.sem("a_cols_made"), s.sem("a_carrier")
        with_sink = s.sem("a_with_sink")
        sums_in, inverted, inv_out, inv_in = s.sem("a_sums_in"), s.sem("a_inverted"), s.sem("a_inv_out"), s.sem("a_inv_in")
        divided, cols_out, stored = s.sem("a_divided"), s.sem("a_cols_out"), s.sem("a_stored")
        inv_rows = s.scratch("inv_rows", [P, QH])
        kc_in, blanked, pool_carrier, sp_carrier = s.sem("a_kc_in"), s.sem("a_blanked"), s.sem("a_pool_carrier"), s.sem("a_sp_carrier")
        RAW_LOADS, BLOCK_LOADS = 4, 5
        G = KVH

        def cut(start, size):
            return slice(start, start + size) if isinstance(start, int) else ds(start, size)

        def blocks(eng, step):
            with eng.Fori(0, LCHUNK // 2 - 1) as i:
                for b in range(2):
                    step(2 * i + b, b, i, True, True)
            step(LCHUNK - 2, 0, LCHUNK // 2 - 1, False, True)
            step(LCHUNK - 1, 1, LCHUNK // 2 - 1, False, False)

        with nc.Block() as block:

            @block.sync
            def _(sp):
                kF = qkF[QH * HD:, :].rearrange("(g d) t -> d g t", d=HD)
                qF = qkF[0:QH * HD, :].rearrange("(h d) t -> d h t", d=HD)

                def load_raw(m):
                    for half in range(2):
                        part = slice(HD * half, HD * half + HD)
                        sp.dma_start(k_raw[part], kF[:, :, cut(m * P + CTX, 3 * P)]).then_inc(raw_in, 16)
                        sp.dma_start(q_raw[part], qF[:, :, cut(m * P + KV_LAT0, P)]).then_inc(raw_in, 16)

                def load_block(m, b):
                    for c in range(3):
                        sp.dma_start(vwin[:, b, c, :, 0:HD],
                                     vT[cut(m * P + (CTX + c * P), P), :].rearrange("p (g d) -> p g d", d=HD)).then_inc(block_in[b], 16)
                    sp.dma_start(mask[:, b], s.masks.rearrange("c p n -> (c p) n")[cut(m * P, P), :]).then_inc(block_in[b], 16)
                    sp.dma_start(edge[:, b], s.edges.rearrange("c p (e q) -> (c p) e q", e=2)[cut(m * P, P)]).then_inc(block_in[b], 16)

                def load_top(m, b):
                    sp.wait_ge(top_hi, m + 1)
                    sp.sem_inc(sp_carrier, 1)
                    sp.wait_ge(top_lo, m + 1)
                    sp.sem_inc(sp_carrier, 1)
                    sp.dma_start(q2[TOP_HI:TOP_HI + 1, b].bitcast(F32), thi[:].bitcast(F32)).then_inc(top_in, 16)
                    sp.dma_start(q2[TOP_LO:TOP_LO + 1, b].bitcast(F32), tlo[:].bitcast(F32)).then_inc(top_in, 16)
                    sp.wait_ge(sunk_made, m + 1)
                    sp.sem_inc(sp_carrier, 1)
                    sp.dma_start(sunk_spread[:, b], sunk[:]).then_inc(top_in, 16)

                def step(n, b, i, split, ahead):
                    if split:
                        sp.wait_ge(k_lo, n + 3)
                        sp.sem_inc(sp_carrier, 1)
                        sp.wait_ge(q_lo, n + 2)
                        sp.sem_inc(sp_carrier, 1)
                        sp.wait_ge(q2_made, n + 2)
                        sp.sem_inc(sp_carrier, 1)
                        load_raw(n + 2)
                    if ahead:
                        load_top(n + 1, 1 - b)
                    if split:
                        sp.wait_ge(summed, G * n + (G + 2))
                        sp.sem_inc(sp_carrier, 1)
                        load_block(n + 2, b)

                for half in range(2):
                    sp.dma_start(kc_raw[HD * half:HD * half + HD], kF[:, :, 0:CTX]).then_inc(kc_in, 16)
                load_raw(0)
                sp.dma_start(ident[:], s.squares[:, 0:P]).then_inc(const_in, 16)
                sp.dma_start(sink[:], s.x["attn_sink"].to_broadcast([P, QH])).then_inc(const_in, 16)
                sp.dma_start(sink_col[:], s.x["attn_sink"].rearrange("o h -> h o")).then_inc(const_in, 16)
                sp.wait_ge(fixed, 1)
                for c in range(CCHUNK):
                    sp.dma_start(vctx[:, c, :, 0:HD], vT[c * P:c * P + P, :].rearrange("p (g d) -> p g d", d=HD)).then_inc(const_in, 16)
                load_block(0, 0)
                load_block(1, 1)
                sp.wait_ge(k_lo, 2)
                sp.wait_ge(q_lo, 1)
                sp.wait_ge(q2_made, 1)
                load_raw(1)
                load_top(0, 0)
                blocks(sp, step)

            CONSTS = 16 * (3 + CCHUNK)

            @block.tensor
            def _(pe):
                pe.sem_inc(summed, 2)

                def a(m, b, heads):
                    for h in heads:
                        pe.wait_ge(maxed, QH * m + (h + 1))
                        g = h // PER_KV
                        for lo, hi in ((0, 512), (512, KEYS)):
                            nc.tensor.matmul(a_ps[:, h % 2, lo:hi], q1[:, b, h], k1[:, b, g, lo:hi], start=True, stop=False)
                            mm = nc.tensor.matmul(a_ps[:, h % 2, lo:hi], q2[0:HD, b, h], k2[0:HD, b, g, lo:hi], start=False, stop=True)
                        mm.then_inc(scored, 1)

                def turn_top(m):
                    pe.wait_ge(negated, m + 2)
                    nc.tensor.transpose(tp[0:QH, 0:P], negtop[:], ident[:]).then_inc(top_turned, 1)

                def b_scores(n, b, g):
                    for k, t in enumerate(ORDER):
                        pe.wait_ge(exps_made, NKT * G * n + (NKT * g + k + 1))
                        out = b_ps[:, (g + k) % 2]
                        nc.tensor.matmul(out, k1[:, b, g, t * P:t * P + P], q1[:, b, PER_KV * g:PER_KV * g + PER_KV], start=True, stop=False)
                        nc.tensor.matmul(out, k2[0:K2, b, g, t * P:t * P + P], q2[0:K2, b, PER_KV * g:PER_KV * g + PER_KV],
                                         start=False, stop=True).then_inc(b_made, 1)

                def c(n, b, g):
                    pe.wait_ge(exps_made, NKT * G * n + (NKT * g + NKT + 2))
                    pe.wait_ge(cols_made, G * n + (g + 1))
                    for t in range(NKT):
                        values = vctx[:, t, g] if t < CCHUNK else vwin[:, b, t - CCHUNK, g]
                        mm = nc.tensor.matmul(c_ps[:], values, prob[:, g % 2, t], start=(t == 0), stop=(t == NKT - 1))
                    mm.then_inc(summed, 1)

                def step(n, b, i, split, ahead):
                    c(n, b, 0)
                    if ahead:
                        pe.wait_ge(block_in[1 - b], 16 * BLOCK_LOADS * i + 16 * BLOCK_LOADS * (1 + b))
                        pe.wait_ge(k_lo, n + 3)
                        pe.wait_ge(q_lo, n + 2)
                        pe.wait_ge(q2_made, n + 2)
                        a(n + 1, 1 - b, range(*HEAD_CUTS[0]))
                    for g in range(1, G):
                        b_scores(n, b, g)
                        if ahead and g < 3:
                            a(n + 1, 1 - b, range(*HEAD_CUTS[g]))
                        elif ahead:
                            turn_top(n + 1)
                        c(n, b, g)
                    if ahead:
                        pe.wait_ge(top_in, 48 * n + 96)
                        b_scores(n + 1, 1 - b, 0)

                pe.wait_ge(const_in, CONSTS)
                for b in range(2):
                    pe.wait_ge(block_in[b], 16 * BLOCK_LOADS)
                pe.wait_ge(k_lo, 2)
                pe.wait_ge(q_lo, 1)
                pe.wait_ge(q2_made, 1)
                a(0, 0, range(QH))
                turn_top(0)
                pe.wait_ge(top_in, 48)
                b_scores(0, 0, 0)
                blocks(pe, step)

            @block.scalar
            def _(act):
                act.sem_inc(exps_made, 2)
                act.sem_inc(cols_made, 1)

                def split_hi(m, b):
                    act.wait_ge(raw_in, 16 * RAW_LOADS * m + 16 * RAW_LOADS)
                    nc.scalar.copy(k1[:, b, :, CTX:KEYS], k_raw[:]).then_inc(k_hi, 1)
                    nc.scalar.copy(q1[:, b], q_raw[:]).then_inc(q_hi, 1)
                    nc.scalar.copy(q2[0:HD, b], q_raw[0:HD]).then_inc(q2_made, 1)

                def top_parts(m, b):
                    act.wait_ge(top_turned, m + 1)
                    if not isinstance(m, int) or m > 0:
                        act.wait_ge(top_in, 48 * m)
                    nc.scalar.activation(sunk[:], tp[0:QH, 0:P], ACT.Exp, scale=SCALE, bias=sink_col[:]).then_inc(sunk_made, 1)
                    nc.scalar.copy(thi[:], tp[0:QH, 0:P]).then_inc(top_hi, 1)

                def exponentials(n, b, g):
                    act.wait_ge(summed, G * n + (g + 1))
                    for k, t in enumerate(ORDER):
                        act.wait_ge(b_made, NKT * G * n + (NKT * g + k + 1))
                        if t in EDGES:
                            act.wait_ge(b_masked, 2 * G * n + (2 * g + EDGES.index(t) + 1))
                        nc.scalar.activation(prob[:, g % 2, t], b_ps[:, (g + k) % 2], ACT.Exp, scale=SCALE).then_inc(exps_made, 1)

                def keep(n, b, g):
                    act.wait_ge(summed, G * n + (g + 3))
                    if g == 0:
                        act.wait_ge(stored, n + 1)
                    nc.scalar.copy(cols[:, b, PER_KV * g:PER_KV * g + PER_KV], c_ps[:]).then_inc(cols_made, 1)

                def step(n, b, i, split, ahead):
                    keep(n, b, 0)
                    for g in range(1, G):
                        exponentials(n, b, g)
                        if ahead and g == 3:
                            top_parts(n + 1, 1 - b)
                        if split and g == 3:
                            split_hi(n + 2, b)
                        keep(n, b, g)
                    if ahead:
                        exponentials(n + 1, 1 - b, 0)

                act.wait_ge(kc_in, 32)
                for b in range(2):
                    nc.scalar.copy(k1[:, b, :, 0:CTX], kc_raw[:])
                split_hi(0, 0)
                split_hi(1, 1)
                top_parts(0, 0)
                exponentials(0, 0, 0)
                blocks(act, step)

            @block.vector
            def _(dve):
                dve.sem_inc(maxed, 2)
                V.memset(vctx[:], 1.0)
                V.memset(vwin[:], 1.0).then_inc(fixed, 1)

                def split_lo(m, b):
                    dve.wait_ge(q_hi, m + 1)
                    half = slice(HD, P)
                    V.tensor_tensor(q1[half, b], q_raw[half], q1[half, b].bitcast(F32), ALU.subtract).then_inc(q_lo, 1)

                def maxima(m, b, heads):
                    for h in heads:
                        dve.wait_ge(scored, QH * m + (h + 1))
                        dve.wait_ge(maxed, QH * m + (h + 1))
                        dve.sem_inc(carrier, 1)
                        V.tensor_tensor_reduce(masked[:, h % 2], a_ps[:, h % 2, 0:KEYS], mask[:, b], 1.0, NEG,
                                               ALU.add, ALU.max, top[:, h:h + 1]).then_inc(maxed, 1)

                def negate(m):
                    dve.wait_ge(maxed, QH * m + (QH + 2))
                    V.scalar_tensor_tensor(negtop[:], top[:], -1.0, negsink[:], ALU.mult, ALU.min).then_inc(negated, 1)

                def top_parts(m):
                    dve.wait_ge(top_hi, m + 1)
                    V.tensor_tensor(tlo[:], tp[0:QH, 0:P], thi[:].bitcast(F32), ALU.subtract).then_inc(top_lo, 1)

                def mask_edges(n, b, g):
                    for e, t in enumerate(EDGES):
                        k = ORDER.index(t)
                        dve.wait_ge(b_made, NKT * G * n + (NKT * g + k + 1))
                        out = b_ps[:, (g + k) % 2]
                        V.tensor_tensor(out, out, edge[:, b, e].unsqueeze(1).to_broadcast([P, PER_KV, P]), ALU.add).then_inc(b_masked, 1)

                def invert(n, b):
                    dve.wait_ge(sums_in, 16 * n + 16)
                    dve.sem_inc(carrier, 1)
                    V.tensor_tensor(sums[:], sums[:], sunk_spread[:, b], ALU.add).then_inc(with_sink, 1)
                    dve.wait_ge(with_sink, n + 1)
                    V.reciprocal(inv_sums[:], sums[:]).then_inc(inverted, 1)

                def step(n, b, i, split, ahead):
                    if ahead:
                        dve.wait_ge(block_in[1 - b], 16 * BLOCK_LOADS * i + 16 * BLOCK_LOADS * (1 + b))
                        maxima(n + 1, 1 - b, range(*HEAD_CUTS[0]))
                    for g in range(1, G):
                        mask_edges(n, b, g)
                        if ahead and g < 3:
                            maxima(n + 1, 1 - b, range(*HEAD_CUTS[g]))
                        if ahead and g == 2:
                            negate(n + 1)
                        if ahead and g == 3:
                            top_parts(n + 1)
                    if ahead:
                        mask_edges(n + 1, 1 - b, 0)
                    if split:
                        split_lo(n + 2, b)
                    invert(n, b)

                dve.wait_ge(const_in, CONSTS)
                V.tensor_scalar(negsink[:], sink[:], -1.0 / SCALE, None, ALU.mult).then_inc(negated, 1)
                dve.wait_ge(k_hi, 1)
                for b in range(2):
                    V.tensor_tensor(k2[0:HD, b, :, 0:CTX], kc_raw[0:HD], k1[0:HD, b, :, 0:CTX].bitcast(F32), ALU.subtract)
                split_lo(0, 0)
                dve.wait_ge(negated, 1)
                for b in range(2):
                    dve.wait_ge(block_in[b], 16 * BLOCK_LOADS)
                maxima(0, 0, range(QH))
                negate(0)
                split_lo(1, 1)
                top_parts(0)
                mask_edges(0, 0, 0)
                blocks(dve, step)

            @block.gpsimd
            def _(pool):
                for b in range(2):
                    nc.gpsimd.memset(q2[HD:P, b].bitcast(F32), 0.0)
                    nc.gpsimd.memset(k2[HD:P, b].bitcast(F32), 1.0).then_inc(blanked, 1)
                pool.wait_ge(blanked, 2)

                def split_lo(m, b):
                    pool.wait_ge(k_hi, m + 1)
                    nc.gpsimd.tensor_tensor(k2[0:HD, b, :, CTX:KEYS], k_raw[0:HD], k1[0:HD, b, :, CTX:KEYS].bitcast(F32), ALU.subtract).then_inc(k_lo, 1)

                def step(n, b, i, split, ahead):
                    if split:
                        split_lo(n + 2, b)
                    divide(n, b)

                def divide(n, b):
                    pool.wait_ge(cols_made, G * n + (G + 1))
                    pool.sem_inc(pool_carrier, 1)
                    pool.dma_start(sums[:], cols[HD:HD + 1, b]).then_inc(sums_in, 16)
                    pool.wait_ge(inverted, n + 1)
                    pool.sem_inc(pool_carrier, 1)
                    pool.dma_start(inv_rows, inv_sums[:]).then_inc(inv_out, 16)
                    pool.wait_ge(inv_out, 16 * n + 16)
                    pool.sem_inc(pool_carrier, 1)
                    pool.dma_start(inverse[:], inv_rows.rearrange("p h -> (p h)").rearrange("(o h q) -> o h q", o=1, q=P).to_broadcast([HD, QH, P])).then_inc(inv_in, 16)
                    pool.wait_ge(inv_in, 16 * n + 16)
                    pool.sem_inc(pool_carrier, 1)
                    nc.gpsimd.tensor_tensor(cols[0:HD, b], cols[0:HD, b], inverse[:], ALU.mult).then_inc(divided, 1)
                    pool.wait_ge(divided, n + 1)
                    pool.sem_inc(pool_carrier, 1)
                    pool.dma_start(aF[:, cut(n * P, P)].rearrange("(h d) t -> d h t", d=HD), cols[0:HD, b]).then_inc(cols_out, 16)
                    pool.wait_ge(cols_out, 16 * n + 16)
                    pool.sem_inc(stored, 1)

                pool.sem_inc(stored, 2)
                pool.sem_inc(k_lo, 1)
                for m in range(2):
                    split_lo(m, m)
                blocks(pool, step)


def branch_stage(s, yT, aF, gF, mF):
    nc = s.nc
    V = nc.vector
    HALF = SEQ // 2
    TILES = HALF // P
    KY, KA = D_INNER // P, QH * HD // P
    KW = KY + KA
    with ExitStack() as st:
        ident = own(st, nc, "b_ident", [P, P])
        normw = own(st, nc, "b_normw", [P, KY])
        y = own(st, nc, "b_y", [P, 2, D_INNER])
        dump = own(st, nc, "b_dump", [P, D_INNER], mybir.dt.bfloat16)
        full = own(st, nc, "b_full", [P, KY, P])
        a = own(st, nc, "b_a", [P, 2, KA, P])
        ssq, mean, root = (own(st, nc, f"b_{n}", [P, 2]) for n in ("ssq", "mean", "root"))
        hi, lo = own(st, nc, "b_hi", [P, KW, HALF], F32R), own(st, nc, "b_lo", [P, KW, HALF], F32R)
        w = own(st, nc, "b_w", [P, KW, P])
        whi, wlo = own(st, nc, "b_whi", [P, 2, KW, P], F32R), own(st, nc, "b_wlo", [P, 2, KW, P], F32R)
        gates = own(st, nc, "b_gates", [P, 2, 2, HALF])
        m = own(st, nc, "b_m", [P, 2, HALF])
        part = own(st, nc, "b_part", [P, HALF])
        tp = bank(st, nc, "b_tp", [P, KY, P])
        acc = bank(st, nc, "b_acc", [P, 2, 2, 512])
        carrier = s.sem("b_carrier")
        const_in, w_in = s.sem("b_const_in"), s.sem("b_w_in")
        a_in = [s.sem(f"b_a_in{j}") for j in range(2)]
        y_in = [s.sem(f"b_y_in{j}") for j in range(2)]
        gates_in = [s.sem(f"b_gates_in{j}") for j in range(2)]
        m_out = [s.sem(f"b_m_out{j}") for j in range(2)]
        y_free, squared, rooted, step, scaled, turned, full_made = (s.sem(f"b_{n}") for n in (
            "y_free", "squared", "rooted", "step", "scaled", "turned", "full_made"))
        y_split, a_hi, a_split = s.sem("b_y_hi"), s.sem("b_a_hi"), s.sem("b_a_split")
        y_lo, w_hi, w_split, used, m_made, m_step = (s.sem(f"b_{n}") for n in ("y_lo", "w_hi", "w_split", "used", "m_made", "m_step"))
        FT = D // P

        def cut(start, size):
            return slice(start, start + size) if isinstance(start, int) else ds(start, size)

        ssd_v = s.x["w_ssd_br"][0].rearrange("(k p) n -> p k n", p=P)
        attn_v = s.x["w_attn_br"][0].rearrange("(k p) n -> p k n", p=P)

        with nc.Block() as block:

            @block.sync
            def _(sp):
                sp.dma_start(ident[:], s.squares[:, 0:P]).then_inc(const_in, 16)
                sp.dma_start(normw[:], s.x["normw"]).then_inc(const_in, 16)

                def load_weights(f, b, half, col):
                    sp.wait_ge(w_split, f + 1)
                    sp.sem_inc(carrier, 1)
                    sp.dma_start(w[:, 0:KY], ssd_v[:, :, cut(col, P)]).then_inc(w_in, 16)
                    sp.dma_start(w[:, KY:KW], attn_v[:, :, cut(col, P)]).then_inc(w_in, 16)
                    sp.wait_ge(m_made, f + 1)
                    sp.sem_inc(carrier, 1)
                    for j in range(2):
                        sp.dma_start(gates[:, b, j], gF[cut(col + j * D, P), half * HALF:half * HALF + HALF]).then_inc(gates_in[b], 16)

                for half in range(2):
                    if half:
                        load_weights(FT, 0, 1, 0)
                    for n in range(half * TILES, half * TILES + TILES):
                        sp.wait_ge(y_free, n + 1)
                        sp.dma_start(y[:, n % 2], yT[n * P:n * P + P, :]).then_inc(y_in[n % 2], 16)
                        sp.wait_ge(a_split, n + 1)
                        sp.dma_start(a[:, n % 2], aF[:, n * P:n * P + P].rearrange("(k p) t -> p k t", p=P)).then_inc(a_in[n % 2], 16)
                        if n == 1:
                            load_weights(0, 0, 0, 0)
                    with sp.Fori(0, FT // 2 - 1) as i:
                        for b in range(2):
                            load_weights(2 * i + (half * FT + b + 1), 1 - b, half, 2 * P * i + P * (b + 1))
                    load_weights(half * FT + FT - 1, 1, half, D - P)

            @block.scalar
            def _(act):
                def norm(n):
                    act.wait_ge(y_in[n % 2], 16 * (n // 2) + 16)
                    if n >= 1:
                        act.wait_ge(squared, n)
                    if n >= 2:
                        act.wait_ge(scaled, n - 1)
                    nc.scalar.activation(dump[:], y[:, n % 2], ACT.Square, accum_out=ssq[:, n % 2:n % 2 + 1]).then_inc(squared, 1)
                    act.wait_ge(step, 2 * n + 2)
                    nc.scalar.activation(root[:, n % 2:n % 2 + 1], mean[:, n % 2:n % 2 + 1], ACT.Sqrt).then_inc(rooted, 1)

                def split_hi(f, b):
                    act.wait_ge(w_in, 32 * f + 32)
                    act.wait_ge(used, f + 1)
                    nc.scalar.copy(whi[:, b], w[:]).then_inc(w_hi, 1)

                for half in range(2):
                    t0 = half * TILES
                    norm(t0)
                    norm(t0 + 1)
                    for n in range(t0, t0 + TILES):
                        cols = slice((n - t0) * P, (n - t0) * P + P)
                        act.wait_ge(a_in[n % 2], 16 * (n // 2) + 16)
                        nc.scalar.copy(hi[:, KY:KW, cols], a[:, n % 2]).then_inc(a_hi, 1)
                        act.wait_ge(full_made, n + 1)
                        nc.scalar.copy(hi[:, 0:KY, cols], full[:]).then_inc(y_split, 1)
                        if n + 2 < t0 + TILES:
                            norm(n + 2)
                        if n == t0 + 1:
                            split_hi(half * FT, 0)
                    with act.Fori(0, FT // 2 - 1) as i:
                        for b in range(2):
                            split_hi(2 * i + (half * FT + b + 1), 1 - b)
                    split_hi(half * FT + FT - 1, 1)

            @block.vector
            def _(dve):
                dve.sem_inc(y_free, 2)
                dve.sem_inc(a_split, 2)
                dve.sem_inc(w_split, 1)
                dve.sem_inc(m_made, 2)
                dve.wait_ge(const_in, 32)

                def split_lo(f, b):
                    dve.wait_ge(w_hi, f + 1)
                    V.tensor_tensor(wlo[:, b], w[:], whi[:, b].bitcast(F32), ALU.subtract).then_inc(w_split, 1)

                def inverse_mean(n):
                    col = slice(n % 2, n % 2 + 1)
                    dve.wait_ge(squared, n + 1)
                    V.tensor_scalar(mean[:, col], ssq[:, col], 1.0 / D_INNER, EPS, ALU.mult, ALU.add).then_inc(step, 1)
                    dve.wait_ge(step, 2 * n + 1)
                    V.reciprocal(mean[:, col], mean[:, col]).then_inc(step, 1)

                def scale(n):
                    col = slice(n % 2, n % 2 + 1)
                    dve.wait_ge(rooted, n + 1)
                    V.tensor_scalar(y[:, n % 2], y[:, n % 2], root[:, col], None, ALU.mult).then_inc(scaled, 1)

                for half in range(2):
                    if half:
                        dve.wait_ge(used, FT + 2)
                    t0 = half * TILES
                    inverse_mean(t0)
                    scale(t0)
                    inverse_mean(t0 + 1)
                    for n in range(t0, t0 + TILES):
                        cols = slice((n - t0) * P, (n - t0) * P + P)
                        dve.wait_ge(turned, n + 1)
                        V.sem_inc(y_free, 1)
                        V.tensor_tensor(full[:], tp[:], normw[:].unsqueeze(2).to_broadcast([P, KY, P]), ALU.mult).then_inc(full_made, 1)
                        if n + 1 < t0 + TILES:
                            scale(n + 1)
                        dve.wait_ge(a_hi, n + 1)
                        V.tensor_tensor(lo[:, KY:KW, cols], a[:, n % 2], hi[:, KY:KW, cols].bitcast(F32), ALU.subtract).then_inc(a_split, 1)
                        dve.wait_ge(y_split, n + 1)
                        V.tensor_tensor(lo[:, 0:KY, cols], full[:], hi[:, 0:KY, cols].bitcast(F32), ALU.subtract).then_inc(y_lo, 1)
                        dve.wait_ge(y_lo, n + 1)
                        if n + 2 < t0 + TILES:
                            inverse_mean(n + 2)
                        if n == t0 + 1:
                            split_lo(half * FT, 0)

                    def merge(f, b, turn):
                        dve.wait_ge(used, f + 3)
                        dve.wait_ge(gates_in[b], 32 * turn + 32)
                        dve.wait_ge(m_out[b], 16 * turn + 16)
                        dve.wait_ge(m_made, f + 2)
                        V.tensor_tensor(m[:, b], acc[:, b, 0], gates[:, b, 0], ALU.mult).then_inc(m_step, 1)
                        V.tensor_tensor(part[:], acc[:, b, 1], gates[:, b, 1], ALU.mult).then_inc(m_step, 1)
                        dve.wait_ge(m_step, 2 * f + 2)
                        V.tensor_tensor(m[:, b], m[:, b], part[:], ALU.add).then_inc(m_made, 1)

                    f0, t0 = half * FT, half * FT // 2
                    with dve.Fori(0, FT // 2 - 1) as i:
                        split_lo(2 * i + (f0 + 1), 1)
                        merge(2 * i + f0, 0, i + t0)
                        split_lo(2 * i + (f0 + 2), 0)
                        merge(2 * i + (f0 + 1), 1, i + t0)
                    split_lo(f0 + FT - 1, 1)
                    merge(f0 + FT - 2, 0, t0 + FT // 2 - 1)
                    merge(f0 + FT - 1, 1, t0 + FT // 2 - 1)

            @block.tensor
            def _(pe):
                pe.sem_inc(used, 2)
                pe.wait_ge(const_in, 32)
                for half in range(2):
                    for n in range(half * TILES, half * TILES + TILES):
                        pe.wait_ge(scaled, n + 1)
                        if n:
                            pe.wait_ge(full_made, n)
                        for k in range(KY):
                            mm = nc.tensor.transpose(tp[:, k, :], y[:, n % 2, k * P:k * P + P], ident[:])
                        mm.then_inc(turned, 1)
                    pe.wait_ge(y_lo, TILES * (half + 1))
                    pe.wait_ge(a_split, TILES * (half + 1) + 2)
                    with pe.Fori(0, FT // 2) as i:
                        for b in range(2):
                            f = 2 * i + (half * FT + b)
                            pe.wait_ge(w_split, f + 2)
                            pe.wait_ge(m_made, f + 1)
                            for j, ks in ((0, range(KY)), (1, range(KY, KW))):
                                for k in ks:
                                    for n_pass, (weights, xpart) in enumerate(((whi, hi), (whi, lo), (wlo, hi))):
                                        mm = nc.tensor.matmul(acc[:, b, j], weights[:, b, k, :], xpart[:, k, :],
                                                              start=(k == ks[0] and n_pass == 0), stop=(k == ks[-1] and n_pass == 2))
                            mm.then_inc(used, 1)

            @block.gpsimd
            def _(pool):
                s.credit(pool, m_out)
                for half in range(2):
                    with pool.Fori(0, FT // 2) as i:
                        for b in range(2):
                            pool.wait_ge(m_made, 2 * i + (half * FT + b + 3))
                            pool.dma_start(mF[ds(2 * P * i + P * b, P), half * HALF:half * HALF + HALF], m[:, b]).then_inc(m_out[b], 16)
                for b in range(2):
                    pool.wait_ge(m_out[b], 16 * FT + 16)


def residual_stage(s, mod, mF, x1T, h2T, affT):
    nc = s.nc
    V = nc.vector
    B_O, G1, LN_G, LN_B, SC2, SH2 = range(6)
    with ExitStack() as st:
        ident = own(st, nc, "r_ident", [P, P])
        rowv = own(st, nc, "r_rows", [P, 6, D])
        wr = own(st, nc, "r_router", [P, KT, EXPERTS])
        WP = D // 4
        w = own(st, nc, "r_w", [P, 2, KT, WP])
        whi, wlo = own(st, nc, "r_whi", [P, KT, D], F32R), own(st, nc, "r_wlo", [P, KT, D], F32R)
        m = own(st, nc, "r_m", [P, 2, KT, P])
        mhi, mlo = own(st, nc, "r_mhi", [P, 2, KT, P], F32R), own(st, nc, "r_mlo", [P, 2, KT, P], F32R)
        x = own(st, nc, "r_x", [P, 2, D])
        y, x1 = own(st, nc, "r_y", [P, D]), own(st, nc, "r_x1", [P, 2, D])
        h2 = own(st, nc, "r_h2", [P, 2, D])
        h2F = own(st, nc, "r_h2F", [P, KT, P])
        stats, mv, root = own(st, nc, "r_stats", [P, 2, 6]), own(st, nc, "r_mv", [P, 2]), own(st, nc, "r_root", [P, 2])
        carrier, pool_carrier = s.sem("r_carrier"), s.sem("r_pool_carrier")
        small = own(st, nc, "r_small", [P, 4])
        prob = own(st, nc, "r_prob", [P, EXPERTS])
        aff = own(st, nc, "r_aff", [P, LCHUNK, EXPERTS])
        affF = own(st, nc, "r_affF", [EXPERTS, SEQ])
        acc = bank(st, nc, "r_acc", [P, 2, D])
        tp = bank(st, nc, "r_tp", [P, KT, P])
        lg = bank(st, nc, "r_logits", [P, 512])
        const_in, w_hi, w_split = s.sem("r_const_in"), s.sem("r_w_hi"), s.sem("r_w_split")
        w_in = [s.sem(f"r_w_in{b}") for b in range(2)]
        m_in = [s.sem(f"r_m_in{b}") for b in range(2)]
        x_in = [s.sem(f"r_x_in{b}") for b in range(2)]
        x1_out = [s.sem(f"r_x1_out{b}") for b in range(2)]
        h2_out = [s.sem(f"r_h2_out{b}") for b in range(2)]
        m_hi, m_split, multiplied, x_free, step = (s.sem(f"r_{n}") for n in ("m_hi", "m_split", "multiplied", "x_free", "step"))
        squared, rooted, affine, gain, h2_made = (s.sem(f"r_{n}") for n in ("squared", "rooted", "affine", "gain", "h2_made"))
        turned, cols_made, routed, exp_made, aff_made, aff_turned, aff_kept, aff_out = (s.sem(f"r_{n}") for n in (
            "turned", "cols_made", "routed", "exp_made", "aff_made", "aff_turned", "aff_kept", "aff_out"))
        route_step, rows_in = s.sem("r_route_step"), s.sem("r_rows_in")
        VS = 10

        def staggered(eng, split, first_part, router_part, second_part, before_last=None, before_route=None):
            def step(n, b, i, last=False):
                if not last:
                    split(n + 1, 1 - b, i + b)
                first_part(n, b, i)
                router_part(n - 1, 1 - b)
                second_part(n, b, i)

            split(0, 0, 0)
            split(1, 1, 0)
            first_part(0, 0, 0)
            second_part(0, 0, 0)
            with eng.Fori(0, LCHUNK // 2 - 1) as j:
                step(2 * j + 1, 1, j)
                step(2 * j + 2, 0, j + 1)
            if before_last:
                before_last()
            step(LCHUNK - 1, 1, LCHUNK // 2 - 1, last=True)
            if before_route:
                before_route()
            router_part(LCHUNK - 1, 1)

        def cut_of(start, size):
            return slice(start, start + size) if isinstance(start, int) else ds(start, size)


        def tiles(eng, step_):
            with eng.Fori(0, LCHUNK // 2) as i:
                for b in range(2):
                    step_(2 * i + b, b, i)

        with nc.Block() as block:

            @block.sync
            def _(sp):
                def load_w(n):
                    sp.dma_start(w[:, n % 2], s.x["w_o"][0].rearrange("(k p) n -> p k n", p=P)[:, :, WP * n:WP * n + WP]).then_inc(w_in[n % 2], 16)

                for n in range(4):
                    if n >= 2:
                        sp.wait_ge(w_split, n - 1)
                    load_w(n)
                sp.dma_start(ident[:], s.squares[:, 0:P]).then_inc(const_in, 16)
                sp.dma_start(wr[:], s.x["w_router"][0].rearrange("(k p) e -> p k e", p=P)).then_inc(const_in, 16)

                def load(n, b, i):
                    sp.wait_ge(m_split, n + 1)
                    sp.dma_start(m[:, b], mF[:, ds(n * P, P)].rearrange("(k p) t -> p k t", p=P)).then_inc(m_in[b], 16)
                    sp.wait_ge(x_free, n + 1)
                    sp.dma_start(x[:, b], s.x["x"][0, ds(n * P, P), :]).then_inc(x_in[b], 16)

                tiles(sp, load)

            @block.tensor
            def _(pe):
                pe.sem_inc(multiplied, 2)
                pe.wait_ge(w_split, 4)

                def product(n, b):
                    pe.wait_ge(m_split, n + 3)
                    pe.wait_ge(x_free, n + 1)
                    for k in range(KT):
                        for n_pass, (part, weights) in enumerate(((mhi, whi), (mhi, wlo), (mlo, whi))):
                            for c in range(2):
                                mm = nc.tensor.matmul(acc[:, b, 512 * c:512 * c + 512], part[:, b, k, :], weights[:, k, 512 * c:512 * c + 512],
                                                      start=(k == 0 and n_pass == 0), stop=(k == KT - 1 and n_pass == 2))
                    mm.then_inc(multiplied, 1)

                def route(n, b):
                    pe.wait_ge(h2_made, n + 1)
                    pe.wait_ge(cols_made, n + 1)
                    for k in range(KT):
                        mm = nc.tensor.transpose(tp[:, k, :], h2[:, b, k * P:k * P + P], ident[:])
                    mm.then_inc(turned, 1)
                    pe.wait_ge(cols_made, n + 2)
                    pe.wait_ge(exp_made, n + 1)
                    for k in range(KT):
                        mm = nc.tensor.matmul(lg[:, 0:EXPERTS], h2F[:, k, :], wr[:, k, :], start=(k == 0), stop=(k == KT - 1))
                    mm.then_inc(routed, 1)

                product(0, 0)
                product(1, 1)
                pe.wait_ge(const_in, 32)
                route(0, 0)
                with pe.Fori(1, LCHUNK // 2) as i:
                    product(2 * i, 0)
                    route(2 * i - 1, 1)
                    product(2 * i + 1, 1)
                    route(2 * i, 0)
                route(LCHUNK - 1, 1)
                pe.wait_ge(aff_made, LCHUNK)
                for n in range(LCHUNK):
                    mm = nc.tensor.transpose(tp[0:EXPERTS, n, :], aff[:, n, :], ident[:])
                mm.then_inc(aff_turned, 1)

            @block.scalar
            def _(act):
                act.sem_inc(cols_made, 1)
                act.sem_inc(exp_made, 1)
                for n in range(4):
                    act.wait_ge(w_in[n % 2], 16 * (n // 2) + 16)
                    nc.scalar.copy(whi[:, :, WP * n:WP * n + WP], w[:, n % 2]).then_inc(w_hi, 1)
                for j, row in ((B_O, s.x["b_o"]), (G1, mod[0:1, 2 * D:3 * D]), (LN_G, s.x["ln1_g"]), (LN_B, s.x["ln1_b"]),
                               (SC2, mod[0:1, 4 * D:5 * D]), (SH2, mod[0:1, 3 * D:4 * D])):
                    act.dma_start(rowv[:, j], row.to_broadcast([P, D])).then_inc(rows_in, 16)

                def split_hi(n, b, i):
                    act.wait_ge(m_in[b], 16 * i + 16)
                    act.wait_ge(multiplied, n + 1)
                    nc.scalar.copy(mhi[:, b], m[:, b]).then_inc(m_hi, 1)

                def take_root(which):
                    def part(n, b, i):
                        act.wait_ge(squared, 2 * n + (which + 1))
                        nc.scalar.activation(root[:, 1:2], root[:, 0:1], ACT.Sqrt).then_inc(rooted, 1)
                    return part

                def route(n, b):
                    act.wait_ge(route_step, 3 * n + 2)
                    nc.scalar.activation(prob[:], lg[:, 0:EXPERTS], ACT.Exp, bias=small[:, 1:2], accum_out=small[:, 2:3]).then_inc(exp_made, 1)

                def keep_turned(n):
                    act.wait_ge(turned, n + 1)
                    nc.scalar.copy(h2F[:], tp[:]).then_inc(cols_made, 1)

                def split_and_keep(n, b, i):
                    split_hi(n, b, i)
                    if not isinstance(n, int) or n > 1:
                        keep_turned(n - 2)

                staggered(act, split_and_keep, take_root(0), route, take_root(1),
                          before_last=lambda: keep_turned(LCHUNK - 2), before_route=lambda: keep_turned(LCHUNK - 1))
                act.wait_ge(aff_turned, 1)
                nc.scalar.copy(affF[:], tp[0:EXPERTS].rearrange("e n t -> e (n t)")).then_inc(aff_kept, 1)
                act.wait_ge(aff_kept, 1)
                act.dma_start(affT, affF[:]).then_inc(aff_out, 16)
                act.wait_ge(aff_out, 16)

            @block.vector
            def _(dve):
                dve.sem_inc(m_split, 2)
                dve.sem_inc(x_free, 2)
                for n in range(4):
                    dve.wait_ge(w_hi, n + 1)
                    V.tensor_tensor(wlo[:, :, WP * n:WP * n + WP], w[:, n % 2], whi[:, :, WP * n:WP * n + WP].bitcast(F32),
                                    ALU.subtract).then_inc(w_split, 1)

                def split_lo(n, b, i):
                    dve.wait_ge(m_hi, n + 1)
                    V.tensor_tensor(mlo[:, b], m[:, b], mhi[:, b].bitcast(F32), ALU.subtract).then_inc(m_split, 1)

                def then(ins, value):
                    ins.then_inc(step, 1)
                    dve.wait_ge(step, value + 1)

                def normalised(n, src, out, k, which):
                    at = VS * n + k
                    V.bn_stats(stats[:, 0, :], src[:, 0:512]).then_inc(step, 1)
                    then(V.bn_stats(stats[:, 1, :], src[:, 512:1024]), at + 2)
                    dve.sem_inc(carrier, 1)
                    then(V.bn_aggr(mv[:], stats[:]), at + 3)
                    then(V.tensor_scalar(root[:, 1:2], mv[:, 1:2], EPS, None, ALU.add), at + 4)
                    V.reciprocal(root[:, 0:1], root[:, 1:2]).then_inc(squared, 1)
                    dve.wait_ge(rooted, 2 * n + (which + 1))
                    return V.tensor_scalar(out, src, mv[:, 0:1], root[:, 1:2], ALU.subtract, ALU.mult)

                def x1_part(n, b, i):
                    if isinstance(n, int) and n == 0:
                        dve.wait_ge(rows_in, 16 * 6)
                        V.tensor_scalar(rowv[:, SC2], rowv[:, SC2], 1.0, None, ALU.add).then_inc(step, 1)
                    dve.wait_ge(multiplied, n + 3)
                    dve.wait_ge(x_in[b], 16 * i + 16)
                    for c in range(2):
                        cut = slice(512 * c, 512 * c + 512)
                        ins = V.tensor_tensor(y[:, cut], acc[:, b, cut], rowv[:, B_O, cut], ALU.add)
                    then(ins, VS * n + 1)
                    then(V.tensor_tensor(y[:], y[:], rowv[:, G1], ALU.mult), VS * n + 2)
                    V.scalar_tensor_tensor(y[:], x[:, b], ALPHA, y[:], ALU.mult, ALU.add).then_inc(x_free, 1)
                    dve.wait_ge(x_free, n + 3)
                    dve.wait_ge(x1_out[b], 16 * i + 16)
                    normalised(n, y[:], x1[:, b], 2, 0).then_inc(affine, 1)

                def h2_part(n, b, i):
                    dve.wait_ge(affine, 4 * n + 2)
                    dve.wait_ge(h2_out[b], 16 * i + 16)
                    normalised(n, x1[:, b], h2[:, b], 6, 1).then_inc(affine, 1)

                def route(n, b):
                    dve.wait_ge(routed, n + 1)
                    V.reduce_max(small[:, 0:1], lg[:, 0:EXPERTS], AX_X).then_inc(route_step, 1)
                    dve.wait_ge(route_step, 3 * n + 1)
                    V.tensor_scalar(small[:, 1:2], small[:, 0:1], -1.0, None, ALU.mult).then_inc(route_step, 1)
                    dve.wait_ge(exp_made, n + 2)
                    V.reciprocal(small[:, 3:4], small[:, 2:3]).then_inc(route_step, 1)
                    dve.wait_ge(route_step, 3 * n + 3)
                    V.tensor_scalar(aff[:, cut_of(n, 1), :].rearrange("p o e -> p (o e)"), prob[:], small[:, 3:4], None, ALU.mult).then_inc(aff_made, 1)

                staggered(dve, split_lo, x1_part, route, h2_part)

            @block.gpsimd
            def _(pool):
                G = nc.gpsimd
                s.credit(pool, x1_out + h2_out)
                pool.wait_ge(step, 1)

                def tile(n, b, i):
                    pool.wait_ge(affine, 4 * n + 1)
                    G.tensor_tensor(x1[:, b], x1[:, b], rowv[:, LN_G], ALU.mult).then_inc(gain, 1)
                    pool.wait_ge(gain, 2 * n + 1)
                    G.tensor_tensor(x1[:, b], x1[:, b], rowv[:, LN_B], ALU.add).then_inc(affine, 1)
                    pool.wait_ge(affine, 4 * n + 2)
                    pool.sem_inc(pool_carrier, 1)
                    pool.dma_start(x1T[ds(n * P, P), :], x1[:, b]).then_inc(x1_out[b], 16)
                    pool.wait_ge(affine, 4 * n + 3)
                    G.tensor_tensor(h2[:, b], h2[:, b], rowv[:, SC2], ALU.mult).then_inc(gain, 1)
                    pool.wait_ge(gain, 2 * n + 2)
                    G.tensor_tensor(h2[:, b], h2[:, b], rowv[:, SH2], ALU.add).then_inc(h2_made, 1)
                    pool.sem_inc(affine, 1)
                    pool.wait_ge(h2_made, n + 1)
                    pool.sem_inc(pool_carrier, 1)
                    pool.dma_start(h2T[ds(n * P, P), :], h2[:, b]).then_inc(h2_out[b], 16)

                tiles(pool, tile)
                for b in range(2):
                    pool.wait_ge(x1_out[b], 16 * LCHUNK // 2 + 16)
                    pool.wait_ge(h2_out[b], 16 * LCHUNK // 2 + 16)


def expert_stage(s, affT, h2T, moe):
    nc = s.nc
    V = nc.vector
    ROUNDS = CAP // 8
    RAW, SPLIT = 8, 4
    UP_TILES, DOWN_TILES = KT, FF * D // (P * 2048)
    TILES = UP_TILES + DOWN_TILES
    AHEAD = 3
    DKT = FF // P
    HALF = SEQ // 2
    PAIRS = EXPERTS // 2 - 1
    with ExitStack() as st:
        ident, reverse = own(st, nc, "e_ident", [P, P]), own(st, nc, "e_reverse", [P, P])
        aff = own(st, nc, "e_aff", [2 * EXPERTS, HALF])
        best = own(st, nc, "e_best", [2 * EXPERTS, CAP])
        where = own(st, nc, "e_where", [2 * EXPERTS, CAP], U32)
        wheref = own(st, nc, "e_wheref", [2 * EXPERTS, CAP])
        lists = own(st, nc, "e_lists", [P, 2, 2, EXPERTS])
        first, far, gap, token_f = (own(st, nc, f"e_{n}", [P, EXPERTS]) for n in ("first", "far", "gap", "token_f"))
        gate = own(st, nc, "e_gate", [P, EXPERTS])
        token = own(st, nc, "e_token", [P, EXPERTS], U32)
        gatec = own(st, nc, "e_gatec", [P, 1])
        gather_rows, scatter_rows = own(st, nc, "e_gather_rows", [P, 2], U32), own(st, nc, "e_scatter_rows", [P, 1], U32)
        zeros = own(st, nc, "e_zeros", [P, D])
        w = own(st, nc, "e_w", [P, RAW, 2048])
        whi, wlo = own(st, nc, "e_whi", [P, SPLIT, 2048], F32R), own(st, nc, "e_wlo", [P, SPLIT, 2048], F32R)
        rows = own(st, nc, "e_rows", [P, 2, D])
        xhi, xlo = own(st, nc, "e_xhi", [P, 2, KT, P], F32R), own(st, nc, "e_xlo", [P, 2, KT, P], F32R)
        ahi, alo = own(st, nc, "e_ahi", [P, DKT, P], F32R), own(st, nc, "e_alo", [P, DKT, P], F32R)
        g, a = own(st, nc, "e_g", [P, FF]), own(st, nc, "e_a", [P, FF])
        y = own(st, nc, "e_y", [P, 2, D])
        gu = bank(st, nc, "e_gu", [P, 2 * FF])
        tp = bank(st, nc, "e_tp", [P, KT, P])
        down = bank(st, nc, "e_down", [P, D])
        const_in, round_step, listed = s.sem("e_const_in"), s.sem("e_round_step"), s.sem("e_listed")
        lists_turned, lists_kept, lists_reversed, merge_step, picked = (s.sem(f"e_{n}") for n in (
            "lists_turned", "lists_kept", "lists_reversed", "merge_step", "picked"))
        zeros_made, zeros_out = s.sem("e_zeros_made"), s.sem("e_zeros_out")
        w_in = [s.sem(f"e_w_in{j}") for j in range(RAW)]
        w_hi, w_split, w_used = s.sem("e_w_hi"), s.sem("e_w_split"), s.sem("e_w_used")
        gather_listed, scatter_listed, gate_listed = s.sem("e_gather_listed"), s.sem("e_scatter_listed"), s.sem("e_gate_listed")
        rows_in = [s.sem(f"e_rows_in{b}") for b in range(2)]
        y_out, scattered, carrier = s.sem("e_y_out"), s.sem("e_scattered"), s.sem("e_carrier")
        x_turned, x_hi, x_split = s.sem("e_x_turned"), s.sem("e_x_hi"), s.sem("e_x_split")
        silu_made, a_made, a_turned, a_hi, a_split, y_made = (s.sem(f"e_{n}") for n in (
            "silu_made", "a_made", "a_turned", "a_hi", "a_split", "y_made"))
        up_v = s.x["w_gate_up"][0].rearrange("e d f -> (e d) f")
        down_v = s.x["w_down"][0].rearrange("e f d -> (e f) d")

        def cut(start, size):
            return slice(start, start + size) if isinstance(start, int) else ds(start, size)

        def tile_at(at, t):
            i, c = at
            return 2 * TILES * i + (c + t), (c + t) % RAW, 2 * TILES // RAW * i + (c + t) // RAW

        def experts(eng, step):
            with eng.Fori(0, PAIRS) as i:
                step(2 * i + 1, 1, (i, UP_TILES))
                step(2 * i + 2, 0, (i, UP_TILES + TILES))
            step(EXPERTS - 1, 1, (PAIRS, UP_TILES))

        LAST_DOWN = (PAIRS, UP_TILES + TILES)

        with nc.Block() as block:

            @block.sync
            def _(sp):
                for half in range(2):
                    sp.dma_start(aff[EXPERTS * half:EXPERTS * half + EXPERTS, :], affT[:, HALF * half:HALF * half + HALF]).then_inc(const_in, 16)
                sp.dma_start(ident[:], s.squares[:, 0:P]).then_inc(const_in, 16)
                sp.dma_start(reverse[:], s.squares[:, 5 * P:6 * P]).then_inc(const_in, 16)

                def load_up(e, at):
                    for t in range(UP_TILES):
                        n, slot, _ = tile_at(at, t)
                        sp.wait_ge(w_split, n + 1)
                        sp.dma_start(w[:, slot], up_v[cut(e * D + t * P, P), :]).then_inc(w_in[slot], 16)

                def load_down(e, at):
                    for j in range(DOWN_TILES):
                        n, slot, _ = tile_at(at, j)
                        sp.wait_ge(w_split, n + 1)
                        sp.dma_start(w[:, slot].rearrange("p (k n) -> p k n", k=2),
                                     down_v[cut(e * FF + 2 * j * P, 2 * P), :].rearrange("(k p) n -> p k n", p=P)).then_inc(w_in[slot], 16)

                def step(e, b, at):
                    load_up(e, at)
                    load_down(e - 1, (at[0], at[1] + UP_TILES))

                load_up(0, (0, 0))
                experts(sp, step)
                load_down(EXPERTS - 1, LAST_DOWN)

            @block.scalar
            def _(act):
                def w_tile(at, t):
                    n, slot, turn = tile_at(at, t)
                    act.wait_ge(w_in[slot], 16 * turn + 16)
                    act.wait_ge(w_used, n + 1)
                    nc.scalar.copy(whi[:, slot % SPLIT], w[:, slot]).then_inc(w_hi, 1)

                def x_parts(e, b):
                    act.wait_ge(x_turned, e + 3)
                    nc.scalar.copy(xhi[:, b], tp[:]).then_inc(x_hi, 1)

                def a_parts(e):
                    act.wait_ge(a_turned, e + 1)
                    nc.scalar.copy(ahi[:], tp[:]).then_inc(a_hi, 1)

                def activate(e, at):
                    act.wait_ge(w_used, tile_at(at, UP_TILES)[0] + SPLIT)
                    nc.scalar.activation(g[:], gu[:, 0:FF], ACT.Silu).then_inc(silu_made, 1)

                def step(e, b, at):
                    for t in range(AHEAD, UP_TILES + AHEAD):
                        w_tile(at, t)
                    activate(e, at)
                    last = isinstance(e, int)
                    if not last:
                        x_parts(e + 1, 1 - b)
                    w_tile(at, UP_TILES + AHEAD)
                    for t in range(AHEAD):
                        w_tile(at, TILES + t)
                    a_parts(e)

                for t in range(SPLIT):
                    w_tile((0, 0), t)
                x_parts(0, 0)
                for t in range(SPLIT, UP_TILES):
                    w_tile((0, 0), t)
                activate(0, (0, 0))
                x_parts(1, 1)
                for t in range(AHEAD):
                    w_tile((0, UP_TILES), t)
                a_parts(0)
                experts(act, step)
                w_tile(LAST_DOWN, AHEAD)

            @block.vector
            def _(dve):
                dve.sem_inc(w_split, RAW)
                dve.sem_inc(y_made, 1)
                V.memset(zeros[:], 0.0).then_inc(zeros_made, 1)

                def w_tile(at, t):
                    n, slot, _ = tile_at(at, t)
                    dve.wait_ge(w_hi, n + 1)
                    V.tensor_tensor(wlo[:, slot % SPLIT], w[:, slot], whi[:, slot % SPLIT].bitcast(F32), ALU.subtract).then_inc(w_split, 1)

                def x_parts(e, b):
                    dve.wait_ge(x_hi, e + 1)
                    V.tensor_tensor(xlo[:, b], tp[:], xhi[:, b].bitcast(F32), ALU.subtract).then_inc(x_split, 1)

                def a_parts(e):
                    dve.wait_ge(a_hi, e + 1)
                    V.tensor_tensor(alo[:], tp[:], ahi[:].bitcast(F32), ALU.subtract).then_inc(a_split, 1)

                def multiply(e):
                    dve.wait_ge(silu_made, e + 1)
                    V.tensor_tensor(a[:], g[:], gu[:, FF:2 * FF], ALU.mult).then_inc(a_made, 1)

                def finish(e, b, need):
                    dve.wait_ge(y_made, e + 1)
                    V.tensor_copy(gatec[:], gate[:, cut(e, 1)]).then_inc(gate_listed, 1)
                    dve.wait_ge(gate_listed, e + 1)
                    dve.wait_ge(w_used, need)
                    dve.wait_ge(scattered, e + 1)
                    V.tensor_scalar(y[:, b], down[:], gatec[:, 0:1], None, ALU.mult).then_inc(y_made, 1)

                dve.wait_ge(const_in, 64)
                for r in range(ROUNDS):
                    found = slice(8 * r, 8 * r + 8)
                    V.max(best[:, found], aff[:]).then_inc(round_step, 1)
                    dve.wait_ge(round_step, 3 * r + 1)
                    V.max_index(where[:, found], best[:, found], aff[:]).then_inc(round_step, 1)
                    dve.wait_ge(round_step, 3 * r + 2)
                    V.match_replace(aff[:], best[:, found], aff[:], -1.0).then_inc(round_step, 1)
                    dve.wait_ge(round_step, 3 * r + 3)
                V.tensor_copy(wheref[:], where[:]).then_inc(listed, 1)
                dve.wait_ge(lists_turned, 1)
                V.tensor_copy(lists[:], tp[:, 0, 0:4 * EXPERTS].rearrange("p (v h e) -> p v h e", v=2, h=2)).then_inc(lists_kept, 1)
                dve.wait_ge(lists_reversed, 1)
                dve.wait_ge(lists_kept, 1)
                other, other_number = tp[:, 1, 0:EXPERTS], tp[:, 1, EXPERTS:2 * EXPERTS]
                V.tensor_tensor(gate[:], lists[:, 0, 0], other, ALU.max).then_inc(merge_step, 1)
                V.tensor_tensor(first[:], lists[:, 0, 0], other, ALU.is_ge).then_inc(merge_step, 1)
                V.tensor_scalar(far[:], other_number, float(HALF), None, ALU.add).then_inc(merge_step, 1)
                dve.wait_ge(merge_step, 3)
                V.tensor_tensor(gap[:], lists[:, 1, 0], far[:], ALU.subtract).then_inc(merge_step, 1)
                dve.wait_ge(merge_step, 4)
                V.tensor_tensor(token_f[:], gap[:], first[:], ALU.mult).then_inc(merge_step, 1)
                dve.wait_ge(merge_step, 5)
                V.tensor_tensor(gap[:], token_f[:], far[:], ALU.add).then_inc(merge_step, 1)
                dve.wait_ge(merge_step, 6)
                V.tensor_copy(token[:], gap[:]).then_inc(picked, 1)
                x_parts(0, 0)
                dve.wait_ge(w_split, RAW + SPLIT)
                for t in range(SPLIT, UP_TILES):
                    w_tile((0, 0), t)
                multiply(0)
                x_parts(1, 1)
                for t in range(AHEAD):
                    w_tile((0, UP_TILES), t)
                a_parts(0)
                dve.wait_ge(picked, 1)

                def step(e, b, at):
                    for t in range(AHEAD, UP_TILES + AHEAD):
                        w_tile(at, t)
                    multiply(e)
                    last = isinstance(e, int)
                    if not last:
                        x_parts(e + 1, 1 - b)
                    w_tile(at, UP_TILES + AHEAD)
                    for t in range(AHEAD):
                        w_tile(at, TILES + t)
                    a_parts(e)
                    finish(e - 1, 1 - b, tile_at(at, TILES)[0] + SPLIT)

                experts(dve, step)
                w_tile(LAST_DOWN, AHEAD)
                finish(EXPERTS - 1, 1, EXPERTS * TILES + SPLIT)

            @block.tensor
            def _(pe):
                pe.sem_inc(w_used, SPLIT)
                pe.sem_inc(x_turned, 2)
                pe.wait_ge(const_in, 64)
                pe.wait_ge(listed, 1)
                R = 2 * EXPERTS
                nc.tensor.transpose(tp[:, 0, 0:R], best[:], ident[0:R, 0:R])
                nc.tensor.transpose(tp[:, 0, R:2 * R], wheref[:], ident[0:R, 0:R]).then_inc(lists_turned, 1)
                pe.wait_ge(lists_kept, 1)
                nc.tensor.matmul(tp[:, 1, 0:R], reverse[:], lists[:, :, 1, :], start=True, stop=True).then_inc(lists_reversed, 1)

                def turn_x(b, need):
                    pe.wait_ge(rows_in[b], need)
                    for k in range(KT):
                        mm = nc.tensor.transpose(tp[:, k, :], rows[:, b, k * P:k * P + P], ident[:])
                    mm.then_inc(x_turned, 1)

                def turn_a(e):
                    pe.wait_ge(a_made, e + 1)
                    if not (isinstance(e, int) and e == EXPERTS - 1):
                        pe.wait_ge(x_split, e + 2)
                    for k in range(DKT):
                        mm = nc.tensor.transpose(tp[:, k, :], a[:, k * P:k * P + P], ident[:])
                    mm.then_inc(a_turned, 1)

                def gate_up(e, b, at):
                    pe.wait_ge(x_split, e + 1)
                    for k in range(UP_TILES):
                        n, slot, _ = tile_at(at, k)
                        pe.wait_ge(w_split, n + (1 + RAW))
                        for n_pass, (part, weights) in enumerate(((xhi, whi), (xhi, wlo), (xlo, whi))):
                            for c in range(4):
                                mm = nc.tensor.matmul(gu[:, 512 * c:512 * c + 512], part[:, b, k, :],
                                                      weights[:, slot % SPLIT, 512 * c:512 * c + 512],
                                                      start=(k == 0 and n_pass == 0), stop=(k == KT - 1 and n_pass == 2))
                        mm.then_inc(w_used, 1)

                def project_down(at):
                    for j in range(DOWN_TILES):
                        n, slot, _ = tile_at(at, j)
                        pe.wait_ge(w_split, n + (1 + RAW))
                        for half in range(2):
                            k = 2 * j + half
                            for n_pass, (part, weights) in enumerate(((ahi, whi), (ahi, wlo), (alo, whi))):
                                for c in range(2):
                                    col = D * half + 512 * c
                                    mm = nc.tensor.matmul(down[:, 512 * c:512 * c + 512], part[:, k, :],
                                                          weights[:, slot % SPLIT, col:col + 512],
                                                          start=(k == 0 and n_pass == 0), stop=(k == DKT - 1 and n_pass == 2))
                        mm.then_inc(w_used, 1)

                def step(e, b, at):
                    pe.wait_ge(a_made, e)
                    gate_up(e, b, at)
                    pe.wait_ge(a_split, e)
                    if not isinstance(e, int):
                        turn_x(1 - b, 16 * at[0] + 32)
                    pe.wait_ge(y_made, e)
                    project_down((at[0], at[1] + UP_TILES))
                    turn_a(e)

                pe.wait_ge(picked, 1)
                turn_x(0, 16)
                gate_up(0, 0, (0, 0))
                turn_x(1, 16)
                turn_a(0)
                experts(pe, step)
                pe.wait_ge(a_split, EXPERTS)
                pe.wait_ge(y_made, EXPERTS)
                project_down(LAST_DOWN)

            @block.gpsimd
            def _(pool):
                pool.sem_inc(scattered, 2)
                pool.wait_ge(zeros_made, 1)
                for t in range(SEQ // P):
                    pool.dma_start(moe[t * P:t * P + P, :], zeros[:]).then_inc(zeros_out, 16)
                for t in range(SPLIT):
                    pool.wait_ge(w_hi, t + 1)
                    nc.gpsimd.tensor_tensor(wlo[:, t], w[:, t], whi[:, t].bitcast(F32), ALU.subtract).then_inc(w_split, 1)
                pool.wait_ge(picked, 1)

                def gather(e, b):
                    pool.wait_ge(x_turned, e + 1)
                    nc.gpsimd.tensor_copy(gather_rows[:, b:b + 1], token[:, cut(e, 1)]).then_inc(gather_listed, 1)
                    pool.wait_ge(gather_listed, e + 1)
                    pool.sem_inc(carrier, 1)
                    pool.indirect_dma_start(rows[:, b], None, h2T, bass.IndirectOffsetOnAxis(ap=gather_rows[:, b:b + 1], axis=0)).then_inc(rows_in[b], 16)

                def scatter(e, b):
                    nc.gpsimd.tensor_copy(scatter_rows[:], token[:, cut(e, 1)]).then_inc(scatter_listed, 1)
                    pool.wait_ge(scatter_listed, e + 1)
                    pool.wait_ge(y_made, e + 2)
                    pool.sem_inc(carrier, 1)
                    pool.indirect_dma_start(moe, bass.IndirectOffsetOnAxis(ap=scatter_rows[:, 0:1], axis=0), y[:, b], None,
                                            compute_op=ALU.add).then_inc(y_out, 16)
                    pool.wait_ge(y_out, 16 * e + 16)
                    pool.sem_inc(scattered, 1)

                gather(0, 0)
                gather(1, 1)
                pool.wait_ge(zeros_out, 16 * (SEQ // P))
                with pool.Fori(0, PAIRS) as i:
                    for b in range(2):
                        gather(2 * i + (2 + b), b)
                        scatter(2 * i + b, b)
                for b in range(2):
                    scatter(EXPERTS - 2 + b, b)


def output_stage(s, mod, x1T, moe):
    nc = s.nc
    V = nc.vector
    G2, LN_G, LN_B = range(3)
    with ExitStack() as st:
        rowv = own(st, nc, "o_rows", [P, 3, D])
        x, m, y = own(st, nc, "o_x", [P, 2, D]), own(st, nc, "o_m", [P, 2, D]), own(st, nc, "o_y", [P, 2, D])
        stats, mv, root = own(st, nc, "o_stats", [P, 2, 6]), own(st, nc, "o_mv", [P, 2]), own(st, nc, "o_root", [P, 2])
        const_in, carrier = s.sem("o_const_in"), s.sem("o_carrier")
        tiles_in = [s.sem(f"o_tiles_in{b}") for b in range(2)]
        y_out = [s.sem(f"o_y_out{b}") for b in range(2)]
        free, step, squared, rooted, normed, gained, made = (s.sem(f"o_{n}") for n in ("free", "step", "squared", "rooted", "normed", "gained", "made"))
        VS = 5

        def tiles(eng, step_):
            with eng.Fori(0, LCHUNK // 2) as i:
                for b in range(2):
                    step_(2 * i + b, b, i)

        with nc.Block() as block:

            @block.sync
            def _(sp):
                for j, row in ((G2, mod[0:1, 5 * D:6 * D]), (LN_G, s.x["ln2_g"]), (LN_B, s.x["ln2_b"])):
                    sp.dma_start(rowv[:, j], row.to_broadcast([P, D])).then_inc(const_in, 16)

                def load(n, b, i):
                    sp.wait_ge(free, n + 1)
                    sp.dma_start(m[:, b], moe[ds(n * P, P), :]).then_inc(tiles_in[b], 16)
                    sp.dma_start(x[:, b], x1T[ds(n * P, P), :]).then_inc(tiles_in[b], 16)

                tiles(sp, load)

            @block.vector
            def _(dve):
                dve.sem_inc(free, 2)
                dve.wait_ge(const_in, 48)

                def tile(n, b, i):
                    at = VS * n

                    def then(ins, k):
                        ins.then_inc(step, 1)
                        dve.wait_ge(step, at + k)

                    dve.wait_ge(tiles_in[b], 32 * i + 32)
                    then(V.tensor_tensor(m[:, b], m[:, b], rowv[:, G2], ALU.mult), 1)
                    then(V.scalar_tensor_tensor(x[:, b], x[:, b], ALPHA, m[:, b], ALU.mult, ALU.add), 2)
                    V.bn_stats(stats[:, 0, :], x[:, b, 0:512])
                    then(V.bn_stats(stats[:, 1, :], x[:, b, 512:1024]), 3)
                    dve.sem_inc(carrier, 1)
                    then(V.bn_aggr(mv[:], stats[:]), 4)
                    then(V.tensor_scalar(root[:, 1:2], mv[:, 1:2], EPS, None, ALU.add), 5)
                    V.reciprocal(root[:, 0:1], root[:, 1:2]).then_inc(squared, 1)
                    dve.wait_ge(rooted, n + 1)
                    dve.wait_ge(y_out[b], 16 * i + 16)
                    V.tensor_scalar(y[:, b], x[:, b], mv[:, 0:1], root[:, 1:2], ALU.subtract, ALU.mult).then_inc(normed, 1)
                    dve.wait_ge(normed, n + 1)
                    V.sem_inc(free, 1)

                tiles(dve, tile)

            @block.scalar
            def _(act):
                def tile(n, b, i):
                    act.wait_ge(squared, n + 1)
                    nc.scalar.activation(root[:, 1:2], root[:, 0:1], ACT.Sqrt).then_inc(rooted, 1)

                tiles(act, tile)

            @block.gpsimd
            def _(pool):
                s.credit(pool, y_out)
                pool.wait_ge(const_in, 48)

                def tile(n, b, i):
                    pool.wait_ge(normed, n + 1)
                    nc.gpsimd.tensor_tensor(y[:, b], y[:, b], rowv[:, LN_G], ALU.mult).then_inc(gained, 1)
                    pool.wait_ge(gained, n + 1)
                    nc.gpsimd.tensor_tensor(y[:, b], y[:, b], rowv[:, LN_B], ALU.add).then_inc(made, 1)
                    pool.wait_ge(made, n + 1)
                    pool.dma_start(s.out[0, ds(n * P, P), :], y[:, b]).then_inc(y_out[b], 16)

                tiles(pool, tile)
                for b in range(2):
                    pool.wait_ge(y_out[b], 16 * LCHUNK // 2 + 16)


def program(nc, inputs, out, constants):
    with ExitStack() as ctx:
        s = Stage(nc, inputs, out, ctx)
        s.squares, s.cosine, s.sine, s.masks, s.edges, s.lanes = (constants[n] for n in ("squares", "cosine", "sine", "masks", "edges", "lanes"))
        mod = s.scratch("mod", [2, 6 * D])
        xbcF, xbcT = s.scratch("xbcF", [CONV_CH, TOK]), s.scratch("xbcT", [TOK, CONV_CH])
        qkF, gF = s.scratch("qkF", [(QH + KVH) * HD, KV_TOK]), s.scratch("gF", [2 * D, SEQ])
        zT, vT = s.scratch("zT", [SEQ, D_INNER]), s.scratch("vT", [KV_TOK, KVH * HD])
        dtT = s.scratch("dtT", [TOK, 2 * HEADS])
        tabs, cumrow = s.scratch("tabs", [NCHUNK, P, 5 * 2 * HEADS]), s.scratch("cumrow", [LCHUNK, 2, 2 * HEADS, P])
        before = s.scratch("before", [2, LCHUNK, STATE, D_INNER])
        yT = s.scratch("yT", [SEQ, D_INNER])
        aF = s.scratch("aF", [QH * HD, SEQ])
        mF, x1T, h2T = s.scratch("mF", [D, SEQ]), s.scratch("x1T", [SEQ, D]), s.scratch("h2T", [SEQ, D])
        affT = s.scratch("affT", [EXPERTS, SEQ])
        moe = s.scratch("moe", [SEQ, D])
        adaln_stage(s, mod)
        with ExitStack() as st:
            hi, lo = own(st, nc, "h_hi", [P, KT, TOK], F32R), own(st, nc, "h_lo", [P, KT, TOK], F32R)
            norm_stage(s, mod, hi, lo)
            project_f_stage(s, hi, lo, xbcF, xbcT, qkF, gF)
            project_t_stage(s, hi, lo, zT, vT, dtT)
        decay_stage(s, dtT, tabs, cumrow)
        states_stage(s, xbcT, tabs, before)
        scan_output_stage(s, xbcT, xbcF, zT, tabs, cumrow, before, yT)
        attention_stage(s, qkF, vT, aF)
        s.recycle()
        branch_stage(s, yT, aF, gF, mF)
        residual_stage(s, mod, mF, x1T, h2T, affT)
        expert_stage(s, affT, h2T, moe)
        output_stage(s, mod, x1T, moe)


NAMES = ["x", "c", "ctx", "c_ctx", "w_ada", "b_ada", "w_in", "conv_w", "conv_b", "a_log", "dt_bias", "d_skip",
         "ssd_norm_w", "attn_sink", "w_ssd_br", "w_attn_br", "w_o", "b_o", "ln1_g", "ln1_b",
         "w_router", "w_gate_up", "w_down", "ln2_g", "ln2_b"]


def kernel(**inputs):
    from concourse import bacc
    from concourse.bass_utils import run_bass_kernel_spmd

    nc = bacc.Bacc("TRN2", target_bir_lowering=False, num_devices=1)
    arrays, tensors = {}, {}
    for name in NAMES:
        a = np.ascontiguousarray(inputs[name])
        arrays[f"in_{name}"] = a
        tensors[name] = nc.dram_tensor(f"in_{name}", a.shape, mybir.dt.from_np(a.dtype), kind="ExternalInput").ap()
    nx = CONV_CH // P
    taps = np.concatenate([np.asarray(inputs["conv_w"])[0], np.asarray(inputs["conv_b"])], 0)
    taps = np.ascontiguousarray(taps.reshape(CONV_W + 1, nx, P).transpose(2, 1, 0))
    arrays["in_taps"] = taps
    tensors["taps"] = nc.dram_tensor("in_taps", taps.shape, F32, kind="ExternalInput").ap()
    normw = np.ascontiguousarray(np.asarray(inputs["ssd_norm_w"]).reshape(D_INNER // P, P).T)
    arrays["in_normw"] = normw
    tensors["normw"] = nc.dram_tensor("in_normw", normw.shape, F32, kind="ExternalInput").ap()
    constants = {n: nc.inline_tensor(v, f"const_{n}").ap() for n, v in shape_constants().items()}
    out = nc.dram_tensor("out", (1, SEQ, D), F32, kind="ExternalOutput").ap()
    program(nc, tensors, out, constants)
    r = run_bass_kernel_spmd(nc, [arrays], core_ids=[0])
    return r.results[0]["out"]
```
